# Optimizing a Trainium2 kernel written in Bass

```python
import jax
import jax.numpy as jnp
from jax import lax
import numpy as np

D_MODEL = 1024
BATCH = 1
SEQ = 512
DEPTH = 2
DEC_BATCH = 8
DEC_SEQ = 4
PAST_LEN = 256
PAGE_SIZE = 128

N_MIXERS = 2
N_CONV_LAYERS = (DEPTH + N_MIXERS - 1) // N_MIXERS
N_NSA_LAYERS = DEPTH // N_MIXERS
CONV_WIDTH = 31
N_HEADS = 16
HEAD_DIM = D_MODEL // N_HEADS
KV_GROUPS = 4
GROUP_SIZE = N_HEADS // KV_GROUPS
N_BRANCH = 3
CMP_BLOCK = 32
CMP_STRIDE = 16
CMP_HIDDEN = 2 * HEAD_DIM
SEL_BLOCK = 64
N_SELECT = 16
WINDOW = 512
Q_BLOCK = 64
D_FF = 4 * D_MODEL
PLE_DIM = 256
ROPE_THETA = 10000.0
EPS = 1e-6
Q_COLS = N_HEADS * HEAD_DIM
KV_COLS = 2 * N_BRANCH * KV_GROUPS * HEAD_DIM
GATE_COLS = N_BRANCH * N_HEADS
NSA_IN_COLS = Q_COLS + KV_COLS + GATE_COLS

kernel_name = 'hybrid_conformer_nsa_decode_step'

def rmsnorm(x, g):
    xf = x.astype(jnp.float32)
    y = xf * lax.rsqrt(jnp.mean(xf * xf, axis=-1, keepdims=True) + EPS)
    return (y * g.astype(jnp.float32)).astype(x.dtype)

def rope(x, pos):
    half = x.shape[-1] // 2
    inv = ROPE_THETA ** (-jnp.arange(half, dtype=jnp.float32) / half)
    ang = pos[:, None] * inv[None, :]
    c = jnp.cos(ang)[:, None, :]
    s = jnp.sin(ang)[:, None, :]
    xf = x.astype(jnp.float32)
    x1, x2 = xf[..., :half], xf[..., half:]
    return jnp.concatenate([x1 * c - x2 * s, x2 * c + x1 * s], axis=-1).astype(x.dtype)

def masked_softmax(s, mask):
    s = jnp.where(mask, s.astype(jnp.float32), -jnp.inf)
    m = jnp.max(s, axis=-1, keepdims=True)
    m = jnp.where(jnp.isfinite(m), m, 0.0)
    e = jnp.exp(s - m)
    d = jnp.sum(e, axis=-1, keepdims=True)
    return e / jnp.where(d > 0, d, 1.0)

def conv_module(u, state, w_in, b_in, w_dw, b_dw, ln_g, ln_b, w_out, b_out):
    a = u @ w_in + b_in
    glu = a[..., :D_MODEL] * jax.nn.sigmoid(a[..., D_MODEL:])
    xin = jnp.concatenate([state.astype(glu.dtype), glu], axis=1)
    y = lax.conv_general_dilated(xin, w_dw[:, None, :], window_strides=(1,), padding='VALID',
                                 dimension_numbers=('NWC', 'WIO', 'NWC'),
                                 feature_group_count=D_MODEL) + b_dw
    yf = y.astype(jnp.float32)
    mu = jnp.mean(yf, axis=-1, keepdims=True)
    var = jnp.mean(jnp.square(yf - mu), axis=-1, keepdims=True)
    yn = (yf - mu) * lax.rsqrt(var + EPS) * ln_g.astype(jnp.float32) + ln_b.astype(jnp.float32)
    z = jax.nn.silu(yn).astype(u.dtype) @ w_out + b_out
    return z, xin[:, -(CONV_WIDTH - 1):]

def compress(x, pe, w1, w2):
    b, l, g, dh = x.shape
    n_chunk = -(-l // CMP_STRIDE)
    xp = jnp.pad(x, ((0, 0), (0, n_chunk * CMP_STRIDE - l), (0, 0), (0, 0)))
    ch = xp.reshape(b, n_chunk, CMP_STRIDE, g, dh)
    r = CMP_BLOCK // CMP_STRIDE
    n_cmp = n_chunk - r + 1
    blocks = jnp.concatenate([ch[:, o:o + n_cmp] for o in range(r)], axis=2)
    blocks = blocks + pe[:, None, :]
    flat = blocks.transpose(0, 1, 3, 2, 4).reshape(b, n_cmp, g, CMP_BLOCK * dh)
    return jax.nn.gelu(flat @ w1) @ w2

def cover_matrix(n_cmp, n_sel):
    cs = np.arange(n_cmp) * CMP_STRIDE
    ss = np.arange(n_sel) * SEL_BLOCK
    m = (cs[:, None] < ss[None, :] + SEL_BLOCK) & (cs[:, None] + CMP_BLOCK > ss[None, :])
    return jnp.asarray(m, dtype=jnp.float32)

def nsa_mixer(u, q_offset, pk_c, pv_c, pk_s, pv_s, kw_buf, vw_buf,
              w_in, b_gate, pe_k, pe_v, wk1, wk2, wv1, wv2, w_o):
    b, s, _ = u.shape
    proj = u @ w_in
    q = proj[..., :Q_COLS].reshape(b, s, N_HEADS, HEAD_DIM)
    kv = proj[..., Q_COLS:Q_COLS + KV_COLS].reshape(b, s, 2 * N_BRANCH, KV_GROUPS, HEAD_DIM)
    gates = jax.nn.sigmoid(proj[..., Q_COLS + KV_COLS:] + b_gate).reshape(b, s, KV_GROUPS, GROUP_SIZE, N_BRANCH)
    qpos = q_offset + jnp.arange(s, dtype=jnp.int32)
    fpos = qpos.astype(jnp.float32)
    q_c = q.reshape(b, s, KV_GROUPS, GROUP_SIZE, HEAD_DIM)
    q_r = rope(q, fpos).reshape(b, s, KV_GROUPS, GROUP_SIZE, HEAD_DIM)
    k_c, v_c = kv[:, :, 0], kv[:, :, 1]
    k_s, v_s = rope(kv[:, :, 2], fpos), kv[:, :, 3]
    k_w, v_w = rope(kv[:, :, 4], fpos), kv[:, :, 5]

    ck = compress(jnp.concatenate([pk_c, k_c], axis=1), pe_k, wk1, wk2)
    cv = compress(jnp.concatenate([pv_c, v_c], axis=1), pe_v, wv1, wv2)
    n_cmp = ck.shape[1]
    c_end = jnp.arange(n_cmp, dtype=jnp.int32) * CMP_STRIDE + (CMP_BLOCK - 1)

    ks_all = jnp.concatenate([pk_s, k_s], axis=1)
    vs_all = jnp.concatenate([pv_s, v_s], axis=1)
    l_k = ks_all.shape[1]
    n_sel = -(-l_k // SEL_BLOCK)
    pad = n_sel * SEL_BLOCK - l_k

    def to_sel_blocks(a):
        a = jnp.pad(a, ((0, 0), (0, pad), (0, 0), (0, 0)))
        return a.reshape(b, n_sel, SEL_BLOCK, KV_GROUPS, HEAD_DIM).transpose(0, 3, 1, 2, 4)

    ks_blk = to_sel_blocks(ks_all)
    vs_blk = to_sel_blocks(vs_all)
    cover = cover_matrix(n_cmp, n_sel)
    n_top = min(N_SELECT, n_sel)
    bidx = jnp.arange(b)[:, None, None, None]
    gidx = jnp.arange(KV_GROUPS)[None, :, None, None]
    blk = jnp.arange(n_sel, dtype=jnp.int32)

    wb = kw_buf.shape[1]
    wpad = jnp.zeros((b, WINDOW - wb, KV_GROUPS, HEAD_DIM), k_w.dtype)
    kwa = jnp.concatenate([wpad, kw_buf, k_w], axis=1)
    vwa = jnp.concatenate([wpad, vw_buf, v_w], axis=1)

    qb = Q_BLOCK if s % Q_BLOCK == 0 else s
    n_blk = s // qb
    scale = HEAD_DIM ** -0.5

    def body(xs):
        q_b, qr_b, g_b, n = xs
        start = n * qb
        qp = q_offset + start + jnp.arange(qb, dtype=jnp.int32)
        s_c = jnp.einsum('bqgrd,bngd->bqgrn', q_b, ck) * scale
        p_c = masked_softmax(s_c, (c_end[None, :] <= qp[:, None])[None, :, None, None, :])
        o_c = jnp.einsum('bqgrn,bngd->bqgrd', p_c, cv)
        imp = jnp.einsum('bqgrn,ns->bqgs', p_c, cover)
        cur = qp // SEL_BLOCK
        forced = (blk[None, :] == 0) | (blk[None, :] == cur[:, None]) | (blk[None, :] == cur[:, None] - 1)
        future = blk[None, :] > cur[:, None]
        score = jnp.where(future[None, :, None, :], -jnp.inf,
                          jnp.where(forced[None, :, None, :], jnp.inf, imp))
        _, top = lax.top_k(score, n_top)
        top = top.transpose(0, 2, 1, 3)
        kb = ks_blk[bidx, gidx, top]
        vb = vs_blk[bidx, gidx, top]
        kpos = top[..., None] * SEL_BLOCK + jnp.arange(SEL_BLOCK, dtype=jnp.int32)
        m_s = (kpos <= qp[None, None, :, None, None]).transpose(0, 2, 1, 3, 4)
        m_s = m_s.reshape(b, qb, KV_GROUPS, 1, n_top * SEL_BLOCK)
        s_s = jnp.einsum('bqgrd,bgqksd->bqgrks', qr_b, kb).reshape(b, qb, KV_GROUPS, GROUP_SIZE, n_top * SEL_BLOCK) * scale
        p_s = masked_softmax(s_s, m_s).reshape(b, qb, KV_GROUPS, GROUP_SIZE, n_top, SEL_BLOCK)
        o_s = jnp.einsum('bqgrks,bgqksd->bqgrd', p_s, vb)
        kw_b = lax.dynamic_slice_in_dim(kwa, start, WINDOW + qb, axis=1)
        vw_b = lax.dynamic_slice_in_dim(vwa, start, WINDOW + qb, axis=1)
        wpos = q_offset - WINDOW + start + jnp.arange(WINDOW + qb, dtype=jnp.int32)
        m_w = (wpos[None, :] >= 0) & (wpos[None, :] <= qp[:, None]) & (wpos[None, :] > qp[:, None] - WINDOW)
        s_w = jnp.einsum('bqgrd,bkgd->bqgrk', qr_b, kw_b) * scale
        p_w = masked_softmax(s_w, m_w[None, :, None, None, :])
        o_w = jnp.einsum('bqgrk,bkgd->bqgrd', p_w, vw_b)
        return g_b[..., 0:1] * o_c + g_b[..., 1:2] * o_s + g_b[..., 2:3] * o_w

    def to_blocks(a):
        return jnp.moveaxis(a.reshape((b, n_blk, qb) + a.shape[2:]), 1, 0)

    o = lax.map(body, (to_blocks(q_c), to_blocks(q_r), to_blocks(gates), jnp.arange(n_blk, dtype=jnp.int32)))
    o = jnp.moveaxis(o, 0, 1).reshape(b, s, Q_COLS).astype(u.dtype)
    keep = min(WINDOW, l_k)
    return o @ w_o, (k_c, v_c, k_s, v_s, kwa[:, -keep:], vwa[:, -keep:])

def gather_pages(pool, page_table):
    g = pool[page_table]
    return g.reshape(page_table.shape[0], page_table.shape[1] * pool.shape[1], pool.shape[2], pool.shape[3])

def channel_and_ple(h, p_i, g_pre, g_post, w_ff_in, w_ff_out, w_pg, w_pp):
    u = rmsnorm(h, g_pre)
    f = jnp.square(jax.nn.relu(u @ w_ff_in)) @ w_ff_out
    h = h + rmsnorm(f, g_post)
    return h + jax.nn.sigmoid(h @ w_pg) * (p_i @ w_pp)

def setup_inputs(seed: int = 0) -> dict:
    key = jax.random.key(seed)
    keys = iter(jax.random.split(key, 64))

    def nrm(shape, scale=1.0):
        return jax.random.normal(next(keys), shape, jnp.float32) * scale

    def gain(shape):
        return 1.0 + nrm(shape, 0.02)

    n_pages = PAST_LEN // PAGE_SIZE
    n_used = DEC_BATCH * n_pages
    n_pool = n_used + max(1, n_used // 4)
    wb = min(WINDOW, PAST_LEN)
    pool = (N_NSA_LAYERS, n_pool, PAGE_SIZE, KV_GROUPS, HEAD_DIM)
    win = (N_NSA_LAYERS, DEC_BATCH, wb, KV_GROUPS, HEAD_DIM)
    page_table = jax.random.permutation(next(keys), n_pool)[:n_used].reshape(DEC_BATCH, n_pages).astype(jnp.int32)
    return {
        'x_prompt': nrm((BATCH, SEQ, D_MODEL)),
        'x_sample': nrm((DEC_BATCH, DEC_SEQ, D_MODEL)),
        'state_conv': nrm((N_CONV_LAYERS, DEC_BATCH, CONV_WIDTH - 1, D_MODEL), 0.5),
        'cache_k_cmp': nrm(pool),
        'cache_v_cmp': nrm(pool),
        'cache_k_sel': nrm(pool),
        'cache_v_sel': nrm(pool),
        'state_k_win': nrm(win),
        'state_v_win': nrm(win),
        'page_table': page_table,
        'p_prompt': nrm((DEPTH, BATCH, SEQ, PLE_DIM)),
        'p_sample': nrm((DEPTH, DEC_BATCH, DEC_SEQ, PLE_DIM)),
        'norm_mix_pre': gain((DEPTH, D_MODEL)),
        'norm_mix_post': gain((DEPTH, D_MODEL)),
        'norm_ffn_pre': gain((DEPTH, D_MODEL)),
        'norm_ffn_post': gain((DEPTH, D_MODEL)),
        'conv_w_in': nrm((N_CONV_LAYERS, D_MODEL, 2 * D_MODEL), D_MODEL ** -0.5),
        'conv_b_in': nrm((N_CONV_LAYERS, 2 * D_MODEL), 0.02),
        'conv_w_dw': nrm((N_CONV_LAYERS, CONV_WIDTH, D_MODEL), CONV_WIDTH ** -0.5),
        'conv_b_dw': nrm((N_CONV_LAYERS, D_MODEL), 0.02),
        'conv_ln_g': gain((N_CONV_LAYERS, D_MODEL)),
        'conv_ln_b': nrm((N_CONV_LAYERS, D_MODEL), 0.02),
        'conv_w_out': nrm((N_CONV_LAYERS, D_MODEL, D_MODEL), D_MODEL ** -0.5),
        'conv_b_out': nrm((N_CONV_LAYERS, D_MODEL), 0.02),
        'nsa_w_in': nrm((N_NSA_LAYERS, D_MODEL, NSA_IN_COLS), D_MODEL ** -0.5),
        'nsa_b_gate': nrm((N_NSA_LAYERS, GATE_COLS), 0.02),
        'nsa_pe_k': nrm((N_NSA_LAYERS, CMP_BLOCK, HEAD_DIM), 0.5),
        'nsa_pe_v': nrm((N_NSA_LAYERS, CMP_BLOCK, HEAD_DIM), 0.5),
        'nsa_wk_c1': nrm((N_NSA_LAYERS, CMP_BLOCK * HEAD_DIM, CMP_HIDDEN), (CMP_BLOCK * HEAD_DIM) ** -0.5),
        'nsa_wk_c2': nrm((N_NSA_LAYERS, CMP_HIDDEN, HEAD_DIM), CMP_HIDDEN ** -0.5),
        'nsa_wv_c1': nrm((N_NSA_LAYERS, CMP_BLOCK * HEAD_DIM, CMP_HIDDEN), (CMP_BLOCK * HEAD_DIM) ** -0.5),
        'nsa_wv_c2': nrm((N_NSA_LAYERS, CMP_HIDDEN, HEAD_DIM), CMP_HIDDEN ** -0.5),
        'nsa_w_o': nrm((N_NSA_LAYERS, Q_COLS, D_MODEL), Q_COLS ** -0.5),
        'ffn_w_in': nrm((DEPTH, D_MODEL, D_FF), D_MODEL ** -0.5),
        'ffn_w_out': nrm((DEPTH, D_FF, D_MODEL), D_FF ** -0.5),
        'ple_w_gate': nrm((DEPTH, D_MODEL, D_MODEL), D_MODEL ** -0.5),
        'ple_w_proj': nrm((DEPTH, PLE_DIM, D_MODEL), PLE_DIM ** -0.5),
    }

def reference(x_prompt, x_sample, state_conv, cache_k_cmp, cache_v_cmp, cache_k_sel, cache_v_sel,
              state_k_win, state_v_win, page_table, p_prompt, p_sample,
              norm_mix_pre, norm_mix_post, norm_ffn_pre, norm_ffn_post,
              conv_w_in, conv_b_in, conv_w_dw, conv_b_dw, conv_ln_g, conv_ln_b, conv_w_out, conv_b_out,
              nsa_w_in, nsa_b_gate, nsa_pe_k, nsa_pe_v, nsa_wk_c1, nsa_wk_c2, nsa_wv_c1, nsa_wv_c2, nsa_w_o,
              ffn_w_in, ffn_w_out, ple_w_gate, ple_w_proj):
    past_len = page_table.shape[1] * cache_k_cmp.shape[2]
    n_p = x_prompt.shape[0]
    hp, hs = x_prompt, x_sample
    conv_p, conv_s, nsa_p, nsa_s = [], [], [], []
    for i in range(DEPTH):
        j = i // N_MIXERS
        up = rmsnorm(hp, norm_mix_pre[i])
        us = rmsnorm(hs, norm_mix_pre[i])
        if i % N_MIXERS == 0:
            cw = (conv_w_in[j], conv_b_in[j], conv_w_dw[j], conv_b_dw[j],
                  conv_ln_g[j], conv_ln_b[j], conv_w_out[j], conv_b_out[j])
            mp, st_p = conv_module(up, jnp.zeros((n_p, CONV_WIDTH - 1, D_MODEL), up.dtype), *cw)
            ms, st_s = conv_module(us, state_conv[j], *cw)
            conv_p.append(st_p)
            conv_s.append(st_s)
        else:
            nw = (nsa_w_in[j], nsa_b_gate[j], nsa_pe_k[j], nsa_pe_v[j],
                  nsa_wk_c1[j], nsa_wk_c2[j], nsa_wv_c1[j], nsa_wv_c2[j], nsa_w_o[j])
            empty = jnp.zeros((n_p, 0, KV_GROUPS, HEAD_DIM), up.dtype)
            mp, st_p = nsa_mixer(up, 0, empty, empty, empty, empty, empty, empty, *nw)
            pkc = gather_pages(cache_k_cmp[j], page_table)
            pvc = gather_pages(cache_v_cmp[j], page_table)
            pks = gather_pages(cache_k_sel[j], page_table)
            pvs = gather_pages(cache_v_sel[j], page_table)
            ms, st_s = nsa_mixer(us, past_len, pkc, pvc, pks, pvs, state_k_win[j], state_v_win[j], *nw)
            nsa_p.append(st_p)
            nsa_s.append(st_s)
        fw = (norm_ffn_pre[i], norm_ffn_post[i], ffn_w_in[i], ffn_w_out[i], ple_w_gate[i], ple_w_proj[i])
        hp = channel_and_ple(hp + rmsnorm(mp, norm_mix_post[i]), p_prompt[i], *fw)
        hs = channel_and_ple(hs + rmsnorm(ms, norm_mix_post[i]), p_sample[i], *fw)

    conv_state_p = jnp.stack(conv_p)
    conv_state_s = jnp.stack(conv_s)
    k_cmp_p = jnp.stack([st[0] for st in nsa_p])
    v_cmp_p = jnp.stack([st[1] for st in nsa_p])
    k_sel_p = jnp.stack([st[2] for st in nsa_p])
    v_sel_p = jnp.stack([st[3] for st in nsa_p])
    k_win_p = jnp.stack([st[4] for st in nsa_p])
    v_win_p = jnp.stack([st[5] for st in nsa_p])
    k_cmp_s = jnp.stack([st[0] for st in nsa_s])
    v_cmp_s = jnp.stack([st[1] for st in nsa_s])
    k_sel_s = jnp.stack([st[2] for st in nsa_s])
    v_sel_s = jnp.stack([st[3] for st in nsa_s])
    k_win_s = jnp.stack([st[4] for st in nsa_s])
    v_win_s = jnp.stack([st[5] for st in nsa_s])
    return (hp, hs, conv_state_p, k_cmp_p, v_cmp_p, k_sel_p, v_sel_p, k_win_p, v_win_p,
            conv_state_s, k_cmp_s, v_cmp_s, k_sel_s, v_sel_s, k_win_s, v_win_s)


_drawn_inputs = setup_inputs


def setup_inputs(seed=0):
    import zlib

    import numpy as np

    out = dict(_drawn_inputs(seed))
    spreads = {}
    factors = {'norm_mix_post': 3.177,
     'norm_ffn_pre': 3.463,
     'norm_ffn_post': 10.506,
     'conv_ln_g': 9.103,
     'conv_ln_b': 20.968,
     'nsa_b_gate': 22.583,
     'conv_b_out': 16.485}
    for name, (base, spread) in spreads.items():
        noise = np.random.default_rng([zlib.crc32(name.encode()), seed]).standard_normal(out[name].shape)
        drawn = base * np.exp(spread * noise) if base else spread * noise
        out[name] = jnp.asarray(drawn.astype(out[name].dtype))
    for name, factor in factors.items():
        out[name] = (out[name] * factor).astype(out[name].dtype)
    return out
```

```python
from contextlib import ExitStack

import concourse.bass as bass
from concourse import mybir

F32 = mybir.dt.float32
F32R = mybir.dt.float32r
BF16 = mybir.dt.bfloat16
I32 = mybir.dt.int32
ALU = mybir.AluOpType
ACT = mybir.ActivationFunctionType
AX = mybir.AxisListType
ds = bass.ds

P = 128
D = 1024
NC = D // P
SEQ = 512
DB, DT = 8, 4
NS = DB * DT
T = SEQ + NS
HT = T // 2
NH, HD, KG = 16, 64, 4
GQ = NH // KG
PAST, PAGE = 256, 128
NPAGE = PAST // PAGE
NPOOL = 20
CW = 31
FF = 4 * D
PLE = 256
CH = 128
NSLABCOL = 256
SLAB = NC * NSLABCOL
EPS = 1e-6
SCALE = HD ** -0.5
NEG = -1e30
FLOOR = -1e28
XP = CW - 1 + SEQ
XS = (CW - 1 + DT) * DB
XC = XP + XS
QT = SEQ // P
NTT = QT + 1
NCMP_P = 32
XTC = 2 * DB * 16 + 8

C_ID, C_ROT, C_COS, C_SIN = 0, 128, 256, 256 + T
C_TC = C_SIN + T
C_TS = C_TC + NTT * 32
C_HM = C_TS + NTT * 32
C_NM = C_HM + 48
C_CMS = C_NM + 4 * 32
C_CAU = C_CMS + 32
C_CMP = C_CAU + 128
C_SEL = C_CMP + QT * 32
C_ONE = C_SEL + 4 * 128
C_ALL = C_ONE + 128

V_MPRE, V_MPOST, V_FPRE, V_FPOST = 0, 16, 32, 48
V_BIN, V_BDW, V_LNG, V_LNB, V_BOUT = 64, 80, 88, 96, 104
V_ALL = 112


class Link:

    def __init__(self, eng, chain):
        self.eng, self.chain, self.count, self.var, self.per = eng, chain, {}, None, {}

    def loop(self, var, **per):
        self.var, self.per, self.start = var, per, dict(self.count)

    def end(self, trips):
        for s, n in self.count.items():
            p = n - self.start.get(s, 0)
            assert p == self.per.get(s.name, 0), (s.name, p)
            self.count[s] = self.start.get(s, 0) + p * trips
        self.var = None

    def __call__(self, ins, s=None, wait=True):
        s = self.chain if s is None else s
        self.count[s] = self.count.get(s, 0) + 1
        ins.then_inc(s, 1)
        if wait:
            n = self.count[s]
            self.eng.wait_ge(s, n if self.var is None else self.var * self.per[s.name] + n)


def trunk(nc, a, o):
    ctx = ExitStack()
    with ctx:
        top = [(nc.sbuf_base + 63) // 64 * 64]

        def at(name, shape, dt, offset):
            return nc.alloc_sbuf_tensor_at(name, shape, dt, offset=offset)

        def size(shape, dt=F32):
            n = 2 if dt == BF16 else 4
            for s in shape[1:]:
                n *= s
            return (n + 31) // 32 * 32

        def sb(name, shape, dt=F32):
            t = at(name, shape, dt, top[0])
            top[0] += size(shape, dt)
            return t

        def over(start, *wanted):
            out = []
            for name, shape, dt in wanted:
                out.append(at(name, shape, dt, start))
                start += size(shape, dt)
            return out, start

        def sem(name):
            return ctx.enter_context(nc.semaphore(name))

        RAW = [sb(f"w_raw{i}", [P, SLAB]) for i in range(2)]
        WH = [sb(f"w_hi{i}", [P, SLAB], F32R) for i in range(2)]
        WL = [sb(f"w_lo{i}", [P, SLAB], F32R) for i in range(2)]
        R = sb("resid", [P, NC, T])
        x_at = top[0]
        XH = sb("x_hi", [P, NC, T], F32R)
        XL = sb("x_lo", [P, NC, T], F32R)
        h_at = top[0]
        HH = sb("hid_hi", [P, NC, T], F32R)
        HL = sb("hid_lo", [P, NC, T], F32R)
        f_at = top[0]
        F = sb("sub_out", [P, NC, T])
        g_at = top[0]
        G = sb("ple_proj", [P, NC, T])
        end_at = top[0]
        t_at = top[0]
        TMP = [sb(f"tmp{i}", [P, T]) for i in range(4)]
        RS = sb("rstd", [P, T])
        QV = sb("inv_var", [P, T])
        CST = sb("consts", [P, C_ALL])
        VEC = sb("vecs", [P, V_ALL])
        WDW = sb("w_dw", [P, NC, 32])
        p_at = top[0]
        PH = sb("ple_hi", [P, 2, T], F32R)
        PL = sb("ple_lo", [P, 2, T], F32R)
        IDB = sb("ident_bf", [P, P], BF16)
        CAUB = sb("causal_bf", [P, P], BF16)
        CMPB = sb("cmpmask_bf", [P, QT * 32], BF16)
        NMB = sb("newmask_bf", [P, 4 * 32], BF16)
        CMSB = sb("cmpmask_s_bf", [P, 32], BF16)
        SS5 = sb("rowstat", [P, 8])

        ID = CST[:, C_ID:C_ID + P]
        ONE = CST[:, C_ONE:C_ONE + P]

        (XTOK, STT, WDT, VROW), e = over(f_at, ("x_tok", [P, NTT, D], F32), ("state_tok", [120, 2, D], F32),
                                         ("wdw_rows", [CW, D], F32), ("vec_rows", [V_ALL, P], F32))
        assert e <= end_at, (e, end_at)
        (XIN,), e = over(h_at, ("conv_in", [P, NC, XC], F32))
        assert e <= f_at
        (PTOK,), e = over(g_at, ("ple_tok", [P, NTT, PLE], F32))
        (CST_OUT,), e = over(e, ("conv_state_rows", [32, 2, D], F32))
        assert e <= end_at
        (KTS, KTW), xt_at = over(x_at, ("k_selT", [HD, KG, SEQ], F32), ("k_winT", [HD, KG, SEQ], F32))
        (XTH, XTL), e = over(xt_at, ("pairT_hi", [P, 8, XTC], F32R), ("pairT_lo", [P, 8, XTC], F32R))
        (STG,), e = over(e, ("pair_stage", [P, 4, 2, P], F32))
        kv_at = max(e, h_at)
        (KV, QC, QR), e = over(kv_at, ("kv_tok", [P, 6, NTT, 256], F32), ("qT", [P, NC, T], F32),
                               ("qT_rot", [P, NC, T], F32))
        assert e <= end_at, (e, end_at)
        (QBC, QBR), e = over(p_at, ("q_bd_cmp", [P, DB, 2, 32], F32), ("q_bd_rot", [P, DB, 2, 32], F32))
        (PCP,), e = over(p_at, ("pair_prompt", [P, 2, KG, P], F32))
        (HID,), e = over(e, ("cmp_hid", [P, 256], F32))
        (CKP, CKS, CVP), e = over(e, ("ckT_p", [HD, KG, 32], F32), ("ckT_s", [P, 2, P], F32),
                                  ("cv_p", [32, 256], F32))
        assert e <= p_at + 8704, (e - p_at)
        CVS = sb("cv_s", [32, 4, 256])
        GT = sb("gates_tok", [P, NTT, 48])
        GROW = sb("gates_row", [P, 4, 3])
        KNS = sb("k_newT", [P, 2, 2, 32])
        WC2 = sb("wc2", [P, 2, HD])
        PEB = sb("pe_bias", [P, 2])
        SM = sb("soft_small", [P, 2, 16])
        PGT = sb("page_table", [1, DB * NPAGE], I32)
        limit = nc.sbuf_base + nc.sbuf_bytes_remaining
        assert top[0] <= limit, (top[0], limit)
        (WG, WGH, WGL), e = over(t_at, ("wg", [P, NC, 48], F32), ("wg_hi", [P, NC, 48], F32R), ("wg_lo", [P, NC, 48], F32R))
        (GTMP, BGR, PER), e = over(e, ("gate_tmp", [P, 48], F32), ("bg_row", [1, 48], F32), ("pe_rows", [16, 2, P], F32))
        assert e <= t_at + 4 * 2176
        (ROT1, ROT2), _ = over(xt_at, ("rope_a", [P, NTT, KG, 32], F32), ("rope_b", [P, NTT, KG, 32], F32))
        (PEH, PEL), e = over(e, ("pe_hi", [P, 16, 2], F32R), ("pe_lo", [P, 16, 2], F32R))
        assert e <= t_at + 4 * 2176
        (JNK,), e = over(t_at, ("junk", [P, D], F32))
        (KSN, VSN, KWN, VWN), e = over(xt_at, *[(n, [P, 2, 2, 256], F32) for n in ("ks_n", "vs_n", "kw_n", "vw_n")])
        (OTS, OS), e = over(e, ("o_sT", [P, 4, P], F32), ("o_s", [P, P], F32))
        assert e <= kv_at, (e, kv_at)
        (KTB, PTA), e = over(t_at, ("k_bT", [P, 2, 2, 256], F32), ("p_sT", [P, 4, P], F32))
        (PS_, PTB), e = over(e, ("p_s", [P, 2, 288], F32), ("p_newT", [32, 3, P], F32))
        (PC_, GRT), e = over(e, ("p_cmp", [P, 32], F32), ("gates_row_tmp", [P, 4, 48], F32))
        assert e <= t_at + 6 * 2176, e
        (PP, PT, QS), e = over(xt_at, ("p", [P, 2, 2, 512], F32), ("pT", [P, 2, 512], F32),
                               ("q_stage", [HD, 2, 2, SEQ], F32))
        assert e <= kv_at, (e, kv_at)
        (ON,), _ = over(p_at, ("o_tok", [P, 2, QT, P], F32))
        (PCT, PPC, OM, SMC), e = over(t_at, ("p_cT", [32, 2, 8, P], F32), ("p_c", [P, 8, 32], F32),
                                      ("o_sum", [P, 2, HD], F32), ("soft_cmp", [P, 4, 8], F32))
        assert e <= t_at + 6 * 2176
        (YTOK,), e = over(f_at, ("y_tok", [P, NTT, D], F32))

        PS = ctx.enter_context(nc.psum_tensor("ps", [P, 8, 512], F32))

        w_raw = [sem(f"w_raw_in{i}") for i in range(2)]
        w_hi = sem("w_hi")
        w_lo = sem("w_lo")
        blk_full = sem("blk_full")
        blk_free = sem("blk_free")
        x_ready = sem("x_ready")
        phase = sem("phase")
        stores = sem("stores")
        stores_pool = sem("stores_pool")
        chain = {e: sem(f"{e}_chain") for e in ("pe", "act", "dve", "pool")}
        S = {n: sem(n) for n in (
            "ld_const", "ld_x", "ld_vec", "ld_state", "ld_p",
            "row_sq", "row_rstd", "bank_full", "bank_free", "x_scaled", "masks",
            "xs_hi", "y_full", "glu_used", "conv_done",
            "sq_ready", "sq_used", "var_ready", "std_ready", "stat_ready", "stat_used", "r_ready", "xh_ready",
            "rsq_ready", "rsq_used", "rsum_ready",
            "relu_used", "hid_sq", "hid_hi", "h_ready", "gate_ready", "mean_ready", "silu_ready",
            "cs_rows", "y_rows", "ple_full", "ple_lo", "ple_hi",
            "xn_ready", "ld_gate", "ld_wc", "kv_zero", "wg_hi", "wg_lo", "gates_full", "pe_full", "pe_hi",
            "rot_full", "rot_used", "kt_full", "kt_used", "xt_zero", "xt_full", "xt_hi", "xt_used", "ld_pair",
            "peb_full", "cmp_full", "hid_ready", "cmp2_full", "cmp2_used",
            "ld_att", "grow_full", "qbd_ready", "kb_full", "ktb_a", "ktb_d", "s_qk", "s_max", "s_exp", "s_scaled",
            "s_pt", "pta", "ptb", "s_o", "os_ready", "s_ot", "ots_ready",
            "qs_c", "qs_r", "p_qc", "p_qk", "p_max", "p_exp", "p_pt", "p_pv", "p_grp", "grp_dve", "grp_act",
            "o_used", "c_exp", "c_scaled")}
        ld_stg = [sem(f"ld_pair_slot{i}") for i in range(4)]
        block = ctx.enter_context(nc.Block())

        def cols(w):
            v = w.rearrange("(h k p) n -> p h k n", p=P, h=2)
            return lambda i, h: v[:, h, :, ds(i * NSLABCOL, NSLABCOL)]

        def glu_cols(w):
            v = w.rearrange("(k p) (h n) -> p h k n", p=P, h=2)
            return lambda i, h: v[:, h, :, ds(i * P, P)]

        def whole(w, k):
            v = w.rearrange("(h k p) n -> p h k n", p=P, h=2)
            return lambda i, h: v[:, h, :, :]

        STAGES = [(glu_cols(a["conv_w_in"][0]), 8), (cols(a["conv_w_out"][0]), 4)]

        def ffn_stages(l):
            out = []
            for q in range(FF // D):
                out.append((cols(a["ffn_w_in"][l, :, q * D:(q + 1) * D]), 4))
                out.append((cols(a["ffn_w_out"][l, q * D:(q + 1) * D, :]), 4))
            out.append((whole(a["ple_w_proj"][l], 1), 1))
            out.append((cols(a["ple_w_gate"][l]), 4))
            return out

        STAGES += ffn_stages(0)
        STAGES.append((cols(a["nsa_w_in"][0]), 10))
        STAGES.append((whole(a["nsa_wk_c1"][0], 8), 1))
        STAGES.append((whole(a["nsa_wv_c1"][0], 8), 1))
        STAGES.append((cols(a["nsa_w_o"][0]), 4))
        STAGES += ffn_stages(1)
        S_CONV, S_CONVO, S_FFN0, S_NSA = 0, 8, 12, 49
        S_CMP, S_WO, S_FFN1 = 59, 61, 65
        N_SLABS = sum(n for _, n in STAGES)

        FFN_B = 4 * 16 + 8 + 8
        B_CONV, B_CONVO, B_FFN0 = 2, 18, 26
        B_Q = B_FFN0 + FFN_B
        B_KV = B_Q + 8
        B_WO = B_KV + 6 * NTT
        B_FFN1 = B_WO + 8

        def end_phase(eng, k):
            eng.drain().then_inc(phase, 1)
            eng.wait_ge(phase, 4 * k)

        def split_hi(act, s, par, half, before):
            act.wait_ge(w_raw[par], half * 32 + 32)
            act.wait_ge(blk_full, before)
            act.activation(WH[par][:, :], RAW[par][:, :], ACT.Copy).then_inc(w_hi, 1)

        def split_lo(dve, s, par):
            dve.wait_ge(w_hi, s + 1)
            dve.tensor_tensor(WL[par][:, :], RAW[par][:, :], WH[par][:, :].bitcast(F32), ALU.subtract)\
               .then_inc(w_lo, 1)

        def blk(par):
            return PS[:, 2 * par:2 * par + 2, 0:HT]

        def two(t):
            return t.rearrange("p (h n) -> p h n", h=2)

        def three_products(pe, out, k, first, last, wcols, xh, xl, par, xcols):
            m = None
            for w, x, f, l in ((WH, xh, first, False), (WH, xl, False, False), (WL, xh, False, last)):
                for o_, c_ in zip(out, xcols):
                    m = pe.matmul(o_, w[par][:, wcols:wcols + P], x[:, k, c_], start=f, stop=l)
            return m

        HALVES = (slice(0, HT), slice(HT, T))

        def pe_block(pe, par, bpar, b, s, mb, xh, xl, ready, x0, nk=NC, width=NSLABCOL,
                     mb_step=P):
            pe.wait_ge(blk_free, b - 1)
            if mb == 0:
                pe.wait_ge(w_lo, s + 1)
            for k in range(nk):
                if ready is not None:
                    pe.wait_ge(ready, x0 + k + 1)
                m = three_products(pe, [PS[:, 2 * bpar + h, 0:HT] for h in range(2)], k, k == 0, k == nk - 1,
                                   k * width + mb * mb_step, xh, xl, par, HALVES)
            m.then_inc(blk_full, 1)

        def pe_linear(pe, n, s0, b0, ready=None, x0=0, **slab):
            with pe.Fori(0, n // 2) as i:
                for h in range(2):
                    for mb in range(2):
                        pe_block(pe, (s0 + h) % 2, mb, i * 4 + (b0 + 2 * h + mb), i * 2 + (s0 + h), mb,
                                 XH, XL, ready, x0, **slab)

        def act_split_ahead(act, i, s0, b0, h, per=2):
            s = s0 + h + 1
            split_hi(act, i * 2 + s, s % 2, i + s // 2, i * (2 * per) + (b0 + per * h))

        def dve_split_ahead(dve, i, s0, h):
            split_lo(dve, i * 2 + (s0 + h + 1), (s0 + h + 1) % 2)

        def loop_pairs(eng, n, body, last=False):
            with eng.Fori(0, n // 2 - (1 if last else 0)) as i:
                body(i, False)
            if last:
                body(n // 2 - 1, True)

        STAT = PS[:, 4:6, 0:HT]

        def stat_act(act, L, src, n):
            for c in range(NC):
                if 8 * n + c >= 2:
                    act.wait_ge(S["sq_used"], 8 * n + c - 1)
                L(act.activation(TMP[c % 2][:, :], src[:, c, :], ACT.Square), S["sq_ready"])

        def pe_ones(pe, src, first, last):
            for h, c in enumerate(HALVES):
                m = pe.matmul(PS[:, 4 + h, 0:HT], ONE, src[:, c], start=first, stop=last)
            return m

        def stat_pe(pe, n, m):
            if m:
                pe.wait_ge(S["stat_used"], m)
            for c in range(NC):
                pe.wait_ge(S["sq_ready"], 8 * n + c + 1)
                pe_ones(pe, TMP[c % 2], c == 0, c == NC - 1).then_inc(S["sq_used"], 1)

        def std_act(act, L, s, n):
            act.wait_ge(s, n)
            L(act.activation(TMP[3][:, :], TMP[2][:, :], ACT.Sqrt), S["std_ready"])

        def rstd_dve(dve, L, nsq, nstd, deferred=False):
            dve.wait_ge(S["sq_used"], 8 * (nsq + 1))
            if deferred:
                L(dve.scalar_tensor_tensor(two(TMP[2][:, :]), STAT, 1.0 / D, two(QV[:, :]), ALU.mult, ALU.mult),
                  S["stat_used"])
                L(dve.tensor_tensor(TMP[2][:, :], TMP[2][:, :], QV[:, :], ALU.mult))
                L(dve.tensor_scalar(TMP[2][:, :], TMP[2][:, :], EPS, None, ALU.add), S["var_ready"])
            else:
                L(dve.tensor_scalar(two(TMP[2][:, :]), STAT, 1.0 / D, EPS, ALU.mult, ALU.add), S["stat_used"])
            dve.wait_ge(S["std_ready"], nstd + 1)
            L(dve.reciprocal(RS[:, :], TMP[3][:, :]))
            if deferred:
                L(dve.tensor_tensor(RS[:, :], RS[:, :], QV[:, :], ALU.mult))

        def vec(row):
            return VEC[:, row:row + 1]

        def residual_dve(dve, L, gpost, gnext, nr, nx):
            def low(c):
                dve.wait_ge(S["xh_ready"], 8 * nx + c + 1)
                if gnext is None:
                    L(dve.tensor_tensor(XL[:, c, :], R[:, c, :], XH[:, c, :].bitcast(F32), ALU.subtract), x_ready)
                else:
                    L(dve.scalar_tensor_tensor(XL[:, c, :], R[:, c, :], vec(gnext + c), XH[:, c, :].bitcast(F32),
                                               ALU.mult, ALU.subtract), x_ready)
            for c in range(NC):
                L(dve.scalar_tensor_tensor(TMP[2][:, :], F[:, c, :], vec(gpost + c), RS[:, :], ALU.mult, ALU.mult))
                L(dve.tensor_tensor(R[:, c, :], R[:, c, :], TMP[2][:, :], ALU.add), S["r_ready"])
                if c:
                    low(c - 1)
            low(NC - 1)

        def residual_act(act, L, gnext, nr, nx, squares, nq=0):
            for c in range(NC):
                act.wait_ge(S["r_ready"], 8 * nr + c + 1)
                if gnext is None:
                    L(act.activation(XH[:, c, :], R[:, c, :], ACT.Copy), S["xh_ready"])
                else:
                    L(act.activation(XH[:, c, :], R[:, c, :], ACT.Copy, scale=vec(gnext + c)), S["xh_ready"])
                if squares:
                    if c >= 2:
                        act.wait_ge(S["rsq_used"], 8 * nq + c - 1)
                    L(act.activation(TMP[c % 2][:, :], R[:, c, :], ACT.Square), S["rsq_ready"])

        def residual_pool(pool, L, nq):
            for c in range(NC):
                pool.wait_ge(S["rsq_ready"], 8 * nq + c + 1)
                if c == 0:
                    L(pool.tensor_copy(QV[:, :], TMP[0][:, :]), S["rsq_used"])
                else:
                    L(pool.tensor_tensor(QV[:, :], QV[:, :], TMP[c % 2][:, :], ALU.add), S["rsq_used"])

        def ffn_pe(pe, l, s0, b0, nx, nsq, m):
            with pe.Fori(0, 4) as q:
                for j in range(4):
                    for mb in range(2):
                        pe_block(pe, (s0 + j) % 2, mb, q * 16 + (b0 + 2 * j + mb), q * 8 + (s0 + j), mb,
                                 XH, XL, x_ready, 8 * nx)
                for j in range(4):
                    for mb in range(2):
                        pe_block(pe, (s0 + 4 + j) % 2, mb, q * 16 + (b0 + 8 + 2 * j + mb), q * 8 + (s0 + 4 + j), mb,
                                 HH, HL, S["h_ready"], q * 8 + 32 * l)
            pe.wait_ge(S["rsq_used"], 8 * (l + 1))
            pe.wait_ge(S["stat_used"], m)
            pe_ones(pe, QV, True, True).then_inc(S["rsum_ready"], 1)
            stat_pe(pe, nsq, m + 1)
            pe.wait_ge(S["ld_p"], 32 * (l + 1))
            for c in range(2):
                for t in range(QT):
                    m_ = pe.transpose(PS[:, 6 + c, t * P:(t + 1) * P], PTOK[:, t, c * P:(c + 1) * P], ID)
            m_.then_inc(S["ple_full"], 1)
            pe.wait_ge(S["ple_lo"], 3 * l + 1)
            for c in range(2):
                m_ = pe.transpose(PS[:, 6, c * NS:(c + 1) * NS], PTOK[0:NS, QT, c * P:(c + 1) * P], ID[0:NS, 0:NS])
            m_.then_inc(S["ple_full"], 1)
            pe.wait_ge(S["ple_lo"], 3 * (l + 1))
            s, b = s0 + 32, b0 + 64
            for mb in range(NC):
                pe_block(pe, s % 2, mb % 2, b + mb, s, mb, PH, PL, None, 0, nk=2, width=D)
            pe_linear(pe, 4, s + 1, b + 8, x_ready, 8 * (nx + 1))

        PLE_S = PS[:, 6, 0:2 * NS].rearrange("p (c n) -> p c n", c=2)

        def ffn_act(act, L, l, s0, b0, nx, nr, nsq, nstd, last):
            h0 = 32 * l
            act.wait_ge(S["rsq_used"], 8 * (l + 1))
            with act.Fori(0, 4) as q:
                L.loop(q, hid_hi=8)
                for j in range(8):
                    s = s0 + j + 1
                    split_hi(act, q * 8 + s, s % 2, q * 4 + s // 2, q * 16 + (b0 + 2 * j))
                    if j < 4:
                        for mb in range(2):
                            c = 2 * j + mb
                            if c == 0:
                                act.wait_ge(blk_free, q * 16 + b0)
                            act.wait_ge(blk_full, q * 16 + (b0 + c + 1))
                            if c >= 2:
                                act.wait_ge(S["hid_sq"], q * 8 + (h0 + c - 1))
                            act.activation(two(TMP[mb][:, :]), blk(mb), ACT.Relu).then_inc(blk_free, 1)
                            act.wait_ge(S["hid_sq"], q * 8 + (h0 + c + 1))
                            L(act.activation(HH[:, c, :], TMP[2 + mb][:, :], ACT.Copy), S["hid_hi"])
            L.end(4)
            stat_act(act, L, F, nsq)
            std_act(act, L, S["var_ready"], l + 1)
            act.wait_ge(S["ple_full"], 2 * l + 1)
            for c in range(2):
                L(act.activation(PH[:, c, 0:SEQ], PS[:, 6 + c, :], ACT.Copy), S["ple_hi"])
            act.wait_ge(S["ple_full"], 2 * l + 2)
            L(act.activation(PH[:, :, SEQ:T], PLE_S, ACT.Copy), S["ple_hi"])
            residual_act(act, L, None, nr, nx + 1, False)
            s, b = s0 + 32, b0 + 64
            split_hi(act, s + 1, (s + 1) % 2, (s + 1) // 2, b)
            act.wait_ge(blk_free, b + 8)
            def gate(i, final):
                for h in range(2):
                    if not (final and h == 1):
                        act_split_ahead(act, i, s + 1, b + 8, h)
                    for mb in range(2):
                        act.wait_ge(blk_full, i * 4 + (b + 8 + 2 * h + mb + 1))
                        if True:
                            act.wait_ge(S["r_ready"], i * 4 + (8 * (nr + 1) + 2 * h + mb - 1))
                        act.activation(two(TMP[mb][:, :]), blk(mb), ACT.Sigmoid).then_inc(blk_free, 1)
            loop_pairs(act, 4, gate, last)

        def ffn_dve(dve, L, l, s0, b0, nx, nr, gpost, nsq, nstd, last):
            h0 = 32 * l
            L(dve.memset(F[:, :, :], 0.0))
            with dve.Fori(0, 4) as q:
                L.loop(q, hid_sq=8, h_ready=8, blk_free=16)
                L.count[blk_free] = b0
                L.start[blk_free] = b0
                for j in range(8):
                    split_lo(dve, q * 8 + (s0 + j + 1), (s0 + j + 1) % 2)
                    for mb in range(2):
                        c = 2 * (j % 4) + mb
                        if j < 4:
                            L.count[blk_free] += 1
                            dve.wait_ge(blk_free, q * 16 + (b0 + c + 1))
                            L(dve.tensor_tensor(TMP[2 + mb][:, :], TMP[mb][:, :], TMP[mb][:, :], ALU.mult), S["hid_sq"])
                            dve.wait_ge(S["hid_hi"], q * 8 + (h0 + c + 1))
                            L(dve.tensor_tensor(HL[:, c, :], TMP[2 + mb][:, :], HH[:, c, :].bitcast(F32), ALU.subtract),
                              S["h_ready"])
                        else:
                            dve.wait_ge(blk_full, q * 16 + (b0 + 8 + c + 1))
                            L(dve.tensor_tensor(two(F[:, c, :]), blk(mb), two(F[:, c, :]), ALU.add), blk_free)
            L.end(4)
            dve.wait_ge(S["rsum_ready"], l + 1)
            L(dve.tensor_scalar(two(TMP[2][:, :]), STAT, 1.0 / D, EPS, ALU.mult, ALU.add), S["stat_used"])
            L(dve.reciprocal(QV[:, :], TMP[2][:, :]))
            rstd_dve(dve, L, nsq, nstd, deferred=True)
            for c in range(2):
                dve.wait_ge(S["ple_hi"], 3 * l + c + 1)
                L(dve.tensor_tensor(PL[:, c, 0:SEQ], PS[:, 6 + c, :], PH[:, c, 0:SEQ].bitcast(F32), ALU.subtract), S["ple_lo"])
            dve.wait_ge(S["ple_hi"], 3 * l + 3)
            L(dve.tensor_tensor(PL[:, :, SEQ:T], PLE_S, PH[:, :, SEQ:T].bitcast(F32), ALU.subtract), S["ple_lo"])
            residual_dve(dve, L, gpost, None, nr, nx + 1)
            s, b = s0 + 32, b0 + 64
            split_lo(dve, s + 1, (s + 1) % 2)
            dve.wait_ge(stores_pool, 16 * conv_states_n)
            for mb in range(NC):
                dve.wait_ge(blk_full, b + mb + 1)
                L.count[blk_free] = b + mb
                L(dve.tensor_copy(two(G[:, mb, :]), blk(mb % 2)), blk_free)
            def gate(i, final):
                for h in range(2):
                    if not (final and h == 1):
                        dve_split_ahead(dve, i, s + 1, h)
                    for mb in range(2):
                        c = i * 4 + (2 * h + mb)
                        dve.wait_ge(blk_free, i * 4 + (b + 8 + 2 * h + mb + 1))
                        L(dve.tensor_tensor(TMP[2 + mb][:, :], TMP[mb][:, :], G[:, ds(c, 1), :].rearrange("p o n -> p (o n)"), ALU.mult))
                        rc = R[:, ds(c, 1), :].rearrange("p o n -> p (o n)")
                        L(dve.tensor_tensor(rc, rc, TMP[2 + mb][:, :], ALU.add), S["r_ready"])
            if last:
                L.count[blk_free] = 0
                gate(0, False)
                gate(1, True)
            else:
                with dve.Fori(0, 2) as i:
                    L.loop(i, dve_chain=4, r_ready=4)
                    gate(i, False)
                L.end(2)

        conv_states_n = 2 + DT + 2

        def load_p(pool, l):
            pool.dma_start(PTOK[:, 0:QT, :], a["p_prompt"][l, 0].rearrange("(t p) d -> p t d", p=P)).then_inc(S["ld_p"], 16)
            pool.dma_start(PTOK[0:NS, QT, :], a["p_sample"][l].rearrange("b t d -> (b t) d")).then_inc(S["ld_p"], 16)

        def conv_states(pool):
            pool.dma_start(o["conv_state_s"][0, :, 0:CW - 1 - DT, :], a["state_conv"][0, :, DT:CW - 1, :]).then_inc(stores_pool, 16)
            pool.wait_ge(S["cs_rows"], 4)
            pool.dma_start(o["conv_state_p"][0, 0], CST_OUT[0:CW - 1, 0, :]).then_inc(stores_pool, 16)
            for t in range(DT):
                pool.dma_start(o["conv_state_s"][0, :, CW - 1 - DT + t, :], CST_OUT[t * DB:(t + 1) * DB, 1, :]).then_inc(stores_pool, 16)
            for n_ in ("k_win", "v_win"):
                pool.dma_start(o[n_ + "_s"][0, :, 0:PAST].rearrange("b l g d -> b (l g d)"),
                             a["state_" + n_][0].rearrange("b l g d -> b (l g d)")).then_inc(stores_pool, 16)

        T0, T1 = NS, QT
        N_KV_ST = 6 + 4 + 2 * DB

        def rows_of(tt):
            return P if tt < QT else NS

        def page_load(sp, dst, cache, b, pg, view):
            r = sp.value_load(PGT[0:1, b * NPAGE + pg:b * NPAGE + pg + 1], min_val=0, max_val=NPOOL - 1)
            return sp.dma_start(dst, view(a[cache][0, ds(r, 1)]))

        def nsa_pair_loads(sp):
            for kv, cache in enumerate(("cache_k_cmp", "cache_v_cmp")):
                for gp in range(2):
                    for b in range(DB):
                        u = (kv * 2 + gp) * DB + b
                        if u >= 4:
                            sp.wait_ge(S["xt_full"], kv * 2 + u // 2 - 1)
                        for pg in range(NPAGE):
                            for r in range(2):
                                page_load(sp, STG[pg * 64:(pg + 1) * 64, u % 4, :, r * HD:(r + 1) * HD], cache, b, pg,
                                          lambda v: v.rearrange("o (q r) g d -> (o q) r g d", r=2)[:, r, 2 * gp:2 * gp + 2, :])\
                                    .then_inc(ld_stg[u % 4], 16)

        def nsa_kv_stores(sp):
            names = ("k_cmp", "v_cmp", "k_sel", "v_sel", "k_win", "v_win")
            for s, n in enumerate(names):
                sp.dma_start(o[n + "_p"][0, 0].rearrange("(t p) g d -> p t (g d)", p=P), KV[:, s, 0:QT, :]).then_inc(stores, 16)
                if s < 4:
                    sp.dma_start(o[n + "_s"][0].rearrange("b t g d -> (b t) (g d)"), KV[0:NS, s, QT, :]).then_inc(stores, 16)
                else:
                    for b in range(DB):
                        sp.dma_start(o[n + "_s"][0, b, PAST:PAST + DT].rearrange("t g d -> t (g d)"),
                                     KV[b * DT:(b + 1) * DT, s, QT, :]).then_inc(stores, 16)

        def nsa_sample_loads(sp, t):
            for bb in range(2):
                b = 2 * t + bb
                for dst, cache in ((KSN, "cache_k_sel"), (VSN, "cache_v_sel")):
                    for pg in range(NPAGE):
                        page_load(sp, dst[:, bb, pg, :], cache, b, pg, lambda v: v.rearrange("o q g d -> (o q) (g d)"))\
                            .then_inc(S["ld_att"], 16)
                for dst, n in ((KWN, "state_k_win"), (VWN, "state_v_win")):
                    sp.dma_start(dst[:, bb, :, :], a[n][0, b].rearrange("(h p) g d -> p h (g d)", p=P)).then_inc(S["ld_att"], 16)
        N_ATT_LD = 16 * 2 * (2 * NPAGE + 2)

        SK = S_NSA + 4

        def proj_pe(pe):
            stat_pe(pe, 3, 5)
            pe_linear(pe, 4, S_NSA, B_Q, x_ready, 8 * 4)
            with pe.Fori(0, 3) as i:
                for h in range(2):
                    par = (SK + h) % 2
                    for tt in range(NTT):
                        n = NTT * h + tt
                        pe.wait_ge(blk_free, i * (2 * NTT) + (B_KV + n - 1))
                        if tt == 0:
                            pe.wait_ge(w_lo, i * 2 + (SK + h + 1))
                        out = PS[0:rows_of(tt), 2 * (n % 2), 0:256]
                        for k in range(NC):
                            tok = slice(tt * P, tt * P + rows_of(tt))
                            w = slice(k * 256, (k + 1) * 256)
                            pe.matmul(out, XH[:, k, tok], WH[par][:, w], start=k == 0, stop=False)
                            pe.matmul(out, XL[:, k, tok], WH[par][:, w], start=False, stop=False)
                            m = pe.matmul(out, XH[:, k, tok], WL[par][:, w], start=False, stop=k == NC - 1)
                        m.then_inc(blk_full, 1)
            pe.wait_ge(S["wg_lo"], 1)
            for tt in range(NTT):
                out = PS[0:rows_of(tt), 4, tt * 48:(tt + 1) * 48]
                tok = slice(tt * P, tt * P + rows_of(tt))
                for k in range(NC):
                    pe.matmul(out, XH[:, k, tok], WGH[:, k, :], start=k == 0, stop=False)
                    pe.matmul(out, XL[:, k, tok], WGH[:, k, :], start=False, stop=False)
                    pe.matmul(out, XH[:, k, tok], WGL[:, k, :], start=False, stop=False)
                m = pe.matmul(out, ONE[0:1, 0:rows_of(tt)], BGR[0:1, :], start=False, stop=True)
            m.then_inc(S["gates_full"], 1)

        def proj_act(act, L):
            stat_act(act, L, R, 3)
            std_act(act, L, S["stat_used"], 6)
            for c in range(NC):
                act.wait_ge(S["xn_ready"], c + 1)
                L(act.activation(XH[:, c, :], F[:, c, :], ACT.Copy), S["xh_ready"])
            act.wait_ge(S["ld_gate"], 16 * 3)
            L(act.activation(WGH[:, :, :], WG[:, :, :], ACT.Copy), S["wg_hi"])
            with act.Fori(0, 2) as i:
                for h in range(2):
                    act_split_ahead(act, i, S_NSA, B_Q, h)
                    for mb in range(2):
                        act.wait_ge(blk_full, i * 4 + (B_Q + 2 * h + mb + 1))
                        act.activation(QC[:, ds(i * 4 + (2 * h + mb), 1), :].rearrange("p o (h n) -> p (o h) n", h=2),
                                       blk(mb), ACT.Copy).then_inc(blk_free, 1)
            act.wait_ge(S["kv_zero"], 1)
            with act.Fori(0, 3) as i:
                for h in range(2):
                    act_split_ahead(act, i, SK, B_KV, h, per=NTT)
                    for tt in range(NTT):
                        n = NTT * h + tt
                        act.wait_ge(blk_full, i * (2 * NTT) + (B_KV + n + 1))
                        act.activation(KV[0:rows_of(tt), ds(i * 2 + h, 1), tt, :].rearrange("p o n -> p (o n)"),
                                       PS[0:rows_of(tt), 2 * (n % 2), 0:256], ACT.Copy).then_inc(blk_free, 1)
            act.wait_ge(S["gates_full"], 1)
            L(act.activation(GT[:, 0:QT, :], PS[:, 4, 0:QT * 48].rearrange("p (t n) -> p t n", t=QT), ACT.Sigmoid))
            L(act.activation(GT[0:NS, QT, :], PS[0:NS, 4, QT * 48:NTT * 48], ACT.Sigmoid))

        def proj_dve(dve, L):
            rstd_dve(dve, L, 3, 3)
            for c in range(NC + 1):
                if c < NC:
                    L(dve.scalar_tensor_tensor(F[:, c, :], R[:, c, :], vec(V_MPRE + NC + c), RS[:, :], ALU.mult, ALU.mult),
                      S["xn_ready"])
                if c:
                    dve.wait_ge(S["xh_ready"], 8 * 4 + c)
                    L(dve.tensor_tensor(XL[:, c - 1, :], F[:, c - 1, :], XH[:, c - 1, :].bitcast(F32), ALU.subtract), x_ready)
            dve.wait_ge(S["wg_hi"], 1)
            L(dve.tensor_tensor(WGL[:, :, :], WG[:, :, :], WGH[:, :, :].bitcast(F32), ALU.subtract), S["wg_lo"])
            with dve.Fori(0, 2) as i:
                for h in range(2):
                    dve_split_ahead(dve, i, S_NSA, h)
            with dve.Fori(0, 3) as i:
                for h in range(2):
                    dve_split_ahead(dve, i, SK, h)

        def proj_pool(pool, L):
            L(pool.memset(GT[:, QT, :], 0.0))
            L(pool.memset(KV[:, :, QT, :], 0.0), S["kv_zero"])
            pool.wait_ge(x_ready, 8 * 5)
            pool.dma_start(WG[:, :, :], a["nsa_w_in"][0, :, 2560:2608].rearrange("(k p) n -> p k n", p=P)).then_inc(S["ld_gate"], 16)
            pool.dma_start(BGR[:, :], a["nsa_b_gate"]).then_inc(S["ld_gate"], 16)
            for kv, n in enumerate(("k", "v")):
                pool.dma_start(WC2[:, kv, :], a[f"nsa_w{n}_c2"][0]).then_inc(S["ld_wc"], 16)
                pool.dma_start(PER[:, kv, :], a[f"nsa_pe_{n}"][0].rearrange("(i r) d -> i (r d)", r=2)).then_inc(S["ld_wc"], 16)
            pool.dma_start(PGT[:, :], a["page_table"].rearrange("(o b) n -> o (b n)", o=1)).then_inc(S["ld_gate"], 16)

        def rope_pe(pe):
            pe.wait_ge(S["ld_wc"], 64)
            for kv in range(2):
                m = pe.transpose(PS[:, 0, kv * 16:(kv + 1) * 16], PER[:, kv, :], ID[0:16, 0:16])
            m.then_inc(S["pe_full"], 1)
            for c in range(NC):
                if c >= 2:
                    pe.wait_ge(S["rot_used"], c - 1)
                for h, cc in enumerate(HALVES):
                    m = pe.matmul(PS[:, 4 + 2 * (c % 2) + h, 0:HT], CST[:, C_ROT:C_ROT + P], QC[:, c, cc], start=True, stop=True)
                m.then_inc(S["rot_full"], 1)

        PEV = PS[:, 0, 0:32].rearrange("p (v i) -> p i v", v=2)

        def rope_act(act, L):
            act.wait_ge(S["pe_full"], 1)
            L(act.activation(PEH[:, :, :], PEV, ACT.Copy), S["pe_hi"])

        def rope_dve(dve, L):
            dve.wait_ge(S["pe_hi"], 1)
            L(dve.tensor_tensor(PEL[:, :, :], PEV, PEH[:, :, :].bitcast(F32), ALU.subtract))
            for c in range(NC):
                L(dve.tensor_tensor(RS[:, :], QC[:, c, :], CST[:, C_COS:C_COS + T], ALU.mult))
                dve.wait_ge(S["rot_full"], c + 1)
                L(dve.tensor_tensor(two(QV[:, :]), PS[:, 4 + 2 * (c % 2):6 + 2 * (c % 2), 0:HT],
                                    two(CST[:, C_SIN:C_SIN + T]), ALU.mult), S["rot_used"])
                L(dve.tensor_tensor(QR[:, c, :], RS[:, :], QV[:, :], ALU.add))

        def rope_pool(pool, L):
            tab = [CST[:, c:c + NTT * 32].rearrange("p (t o d) -> p t o d", t=NTT, o=1).broadcast_to([P, NTT, KG, 32])
                   for c in (C_TC, C_TS)]
            for s in (2, 4):
                v = KV[:, s, :, :].rearrange("p t (g h d) -> p t g h d", g=KG, h=2)
                x1, x2 = v[:, :, :, 0, :], v[:, :, :, 1, :]
                L(pool.tensor_tensor(ROT1[:, :, :, :], x1, tab[1], ALU.mult))
                L(pool.tensor_tensor(ROT2[:, :, :, :], x2, tab[1], ALU.mult))
                L(pool.tensor_tensor(x1, x1, tab[0], ALU.mult))
                L(pool.tensor_tensor(x2, x2, tab[0], ALU.mult))
                L(pool.tensor_tensor(x1, x1, ROT2[:, :, :, :], ALU.subtract))
                L(pool.tensor_tensor(x2, x2, ROT1[:, :, :, :], ALU.add))

        N_KT = 9
        GROUPS = [(kv, g) for kv in range(2) for g in range(3)]

        def group_banks(g):
            return 4 if g < 2 else 2

        def cmp_pe(pe):
            for n in range(8):
                br, g = n // KG, n % KG
                if n >= 4:
                    pe.wait_ge(S["kt_used"], n - 3)
                for tt in range(QT):
                    m = pe.transpose(PS[0:HD, 4 + n % 4, tt * P:(tt + 1) * P], KV[:, 2 + 2 * br, tt, g * HD:(g + 1) * HD], ID)
                m.then_inc(S["kt_full"], 1)
            pe.wait_ge(S["kt_used"], 5)
            for br in range(2):
                for gp in range(2):
                    j = br * 2 + gp
                    m = pe.transpose(PS[:, 4, j * NS:(j + 1) * NS], KV[0:NS, 2 + 2 * br, QT, gp * P:(gp + 1) * P], ID[0:NS, 0:NS])
            m.then_inc(S["kt_full"], 1)
            tb = 0
            pe.wait_ge(S["kt_used"], N_KT)
            for n, (kv, g) in enumerate(GROUPS):
                s = S_CMP + kv
                if g == 0:
                    pe.wait_ge(w_lo, s + 1)
                    for i in range(16):
                        for w, x in ((WH, PEH), (WH, PEL), (WL, PEH)):
                            m = pe.matmul(PS[:, 2, kv * 2:kv * 2 + 2], w[s % 2][:, i * P:(i + 1) * P], x[:, i, :],
                                          start=i == 0 and x is PEH and w is WH, stop=i == 15 and w is WL)
                    m.then_inc(S["peb_full"], 1)
                for j in range(group_banks(g)):
                    if tb >= 4:
                        pe.wait_ge(S["xt_used"], tb - 3)
                    for t2 in range(2):
                        for g2 in range(2):
                            if g < 2:
                                u = (kv * 2 + g) * DB + 2 * j + t2
                                pe.wait_ge(ld_stg[u % 4], 64 * (u // 4 + 1))
                                src = STG[:, u % 4, g2, :]
                            else:
                                pe.wait_ge(S["ld_pair"], 128 * (kv + 1))
                                src = PCP[:, t2, 2 * j + g2, :]
                            m = pe.transpose(PS[:, 4 + tb % 4, (g2 * 2 + t2) * P:(g2 * 2 + t2 + 1) * P], src, ID)
                    m.then_inc(S["xt_full"], 1)
                    tb += 1
                pe.wait_ge(S["xt_used"], tb)
                if n >= 2:
                    pe.wait_ge(S["hid_ready"], n - 1)
                N = 256 if g < 2 else P
                for i in range(16):
                    sh = i // 8
                    for w, x in ((WH, XTH), (WH, XTL), (WL, XTH)):
                        m = pe.matmul(PS[:, n % 2, 0:N], w[s % 2][:, i * P:(i + 1) * P], x[:, i % 8, sh:sh + N],
                                      start=i == 0 and x is XTH and w is WH, stop=i == 15 and w is WL)
                m.then_inc(S["cmp_full"], 1)
                pe.wait_ge(S["hid_ready"], n + 1)
                if n:
                    pe.wait_ge(S["cmp2_used"], n)
                if kv == 0 and g < 2:
                    for g2 in range(2):
                        m = pe.matmul(PS[g2 * HD:(g2 + 1) * HD, 3, 0:P], WC2[:, 0, :], HID[:, g2 * P:(g2 + 1) * P], start=True, stop=True)
                elif kv == 0:
                    m = pe.matmul(PS[0:HD, 3, 0:P], WC2[:, 0, :], HID[:, 0:P], start=True, stop=True)
                elif g < 2:
                    for t in range(4):
                        for g2 in range(2):
                            m = pe.matmul(PS[0:32, 3, t * P + g2 * HD:t * P + (g2 + 1) * HD],
                                          HID[:, g2 * P + t * 32:g2 * P + (t + 1) * 32], WC2[:, 1, :], start=True, stop=True)
                else:
                    for g_ in range(KG):
                        m = pe.matmul(PS[0:32, 3, g_ * HD:(g_ + 1) * HD], HID[:, g_ * 32:(g_ + 1) * 32], WC2[:, 1, :],
                                      start=True, stop=True)
                m.then_inc(S["cmp2_full"], 1)

        def xt_views(tb, g, j):
            ps = PS[:, 4 + tb % 4, :].rearrange("p (g c i) -> p g i c", g=2, i=8)
            step, base = (P, 32 * j) if g < 2 else (32, 64 * j)
            return ps, [t[:, :, base:base + step + 32].rearrange("p i c -> p i c") for t in (XTH, XTL)], step

        def xt_evac(eng, tb, g, j, lo):
            ps, (vh, vl), step = xt_views(tb, g, j)
            for g2 in range(2):
                c = slice(g2 * step, g2 * step + 32)
                yield ps[:, g2], vh[:, :, c], vl[:, :, c]

        def cmp_act(act, L):
            split_hi(act, S_CMP + 1, (S_CMP + 1) % 2, (S_CMP + 1) // 2, B_WO)
            for n in range(8):
                act.wait_ge(S["kt_full"], n + 1)
                L(act.activation((KTS, KTW)[n // KG][:, n % KG, :], PS[0:HD, 4 + n % 4, :], ACT.Copy), S["kt_used"])
            act.wait_ge(S["kt_full"], N_KT)
            L(act.activation(KNS[:, :, :, :], PS[:, 4, 0:P].rearrange("p (a b n) -> p a b n", a=2, b=2), ACT.Copy), S["kt_used"])
            tb = 0
            act.wait_ge(S["xt_zero"], 1)
            for n, (kv, g) in enumerate(GROUPS):
                if n:
                    act.wait_ge(S["cmp_full"], n)
                for j in range(group_banks(g)):
                    act.wait_ge(S["xt_full"], tb + 1)
                    for src, hi, lo in xt_evac(act, tb, g, j, False):
                        L(act.activation(hi, src, ACT.Copy), S["xt_hi"])
                    tb += 1
                if g == 0:
                    act.wait_ge(S["peb_full"], kv + 1)
                    L(act.activation(PEB[:, kv:kv + 1], PS[:, 2, 3 * kv:3 * kv + 1], ACT.Copy))
                act.wait_ge(S["cmp_full"], n + 1)
                if n:
                    act.wait_ge(S["cmp2_full"], n)
                N = 256 if g < 2 else P
                L(act.activation(HID[:, 0:N], PS[:, n % 2, 0:N], ACT.Gelu_apprx_tanh, bias=PEB[:, kv:kv + 1]), S["hid_ready"])
            split_hi(act, S_WO, S_WO % 2, S_WO // 2, B_WO)

        def cmp_dve(dve, L):
            split_lo(dve, S_CMP + 1, (S_CMP + 1) % 2)
            tb = 0
            for n, (kv, g) in enumerate(GROUPS):
                for j in range(group_banks(g)):
                    dve.wait_ge(S["xt_hi"], 2 * tb + 2)
                    for g2, (src, hi, lo) in enumerate(xt_evac(dve, tb, g, j, True)):
                        L(dve.tensor_tensor(lo, src, hi.bitcast(F32), ALU.subtract), S["xt_used"] if g2 else None)
                    tb += 1
                dve.wait_ge(S["cmp2_full"], n + 1)
                if kv == 0:
                    out, src = (CKS[:, g, :], PS[:, 3, 0:P]) if g < 2 else (CKP[:, :, :], PS[0:HD, 3, 0:P].rearrange("p (g n) -> p g n", g=KG))
                else:
                    out, src = ((CVS[:, :, g * P:(g + 1) * P], PS[0:32, 3, :].rearrange("p (t n) -> p t n", t=4)) if g < 2
                                else (CVP[:, :], PS[0:32, 3, 0:256]))
                L(dve.tensor_copy(out, src), S["cmp2_used"])
            split_lo(dve, S_WO, S_WO % 2)

        def cmp_pool(pool, L):
            L(pool.memset(XTH[:, :, 256:XTC].bitcast(F32), 0.0))
            L(pool.memset(XTL[:, :, 256:XTC].bitcast(F32), 0.0), S["xt_zero"])
            for kv in range(2):
                if kv:
                    pool.wait_ge(S["xt_full"], 10)
                for tt in range(QT):
                    for r in range(2):
                        pool.dma_start(PCP[(tt % 2) * 64:(tt % 2) * 64 + 64, tt // 2, :, r * HD:(r + 1) * HD],
                                       KV[r:P:2, kv, tt, :].rearrange("p (g d) -> p g d", g=KG)).then_inc(S["ld_pair"], 16)

        def soft_cols(j):
            return SM[:, 0, j:j + 1]

        def samp_pe(pe):
            for t in range(4):
                m = pe.matmul(PS[:, 7, t * 48:(t + 1) * 48], CST[0:NS, C_SEL + t * P:C_SEL + (t + 1) * P], GT[0:NS, QT, :],
                              start=True, stop=True)
            m.then_inc(S["grow_full"], 1)
            pe.wait_ge(S["qbd_ready"], 1)
            for t in range(4):
                pe.wait_ge(S["ld_att"], N_ATT_LD * (t + 1))
                for bb in range(2):
                    for br, src in enumerate((KSN, KWN)):
                        if bb == 1:
                            pe.wait_ge(S["ktb_a" if br == 0 else "ktb_d"], 2 * t + 1)
                        for gp in range(2):
                            for h in range(2):
                                m = pe.transpose(PS[:, 4 + br, (gp * 2 + h) * P:(gp * 2 + h + 1) * P],
                                                 src[:, bb, h, gp * P:(gp + 1) * P], ID)
                        m.then_inc(S["kb_full"], 1)
                    pe.wait_ge(S["ktb_a"], 2 * t + bb + 1)
                    pe.wait_ge(S["ktb_d"], 2 * t + bb + 1)
                    b = 2 * t + bb
                    for gp in range(2):
                        r0 = bb * 64 + gp * 32
                        pe.matmul(PS[r0:r0 + 32, 2, 0:32], IDB[:, r0:r0 + 32], CMSB[:, :], start=True, stop=False)
                        pe.matmul(PS[r0:r0 + 32, 2, 0:32], QBC[:, b, gp, :], CKS[:, gp, t * 32:(t + 1) * 32], start=False, stop=True)
                        for br in range(2):
                            pe.matmul(PS[r0:r0 + 32, br, 256:288], IDB[:, r0:r0 + 32], NMB[:, t * 32:(t + 1) * 32],
                                      start=True, stop=False)
                            pe.matmul(PS[r0:r0 + 32, br, 256:288], QBR[:, b, gp, :], KNS[:, br, gp, :], start=False, stop=True)
                            m = pe.matmul(PS[r0:r0 + 32, br, 0:256], QBR[:, b, gp, :], KTB[:, br, gp, :], start=True, stop=True)
                    m.then_inc(S["s_qk"], 1)
                pe.wait_ge(S["s_scaled"], t + 1)
                for br in range(2):
                    for h in range(2):
                        m = pe.transpose(PS[:, 4, (br * 2 + h) * P:(br * 2 + h + 1) * P], PS_[:, br, h * P:(h + 1) * P], ID)
                m.then_inc(S["s_pt"], 1)
                for br in range(2):
                    pe.transpose(PS[0:32, 5, br * P:(br + 1) * P], PS_[:, br, 256:288], ID)
                pe.transpose(PS[0:32, 5, 2 * P:3 * P], PC_[:, :], ID).then_inc(S["s_pt"], 1)
                pe.wait_ge(S["pta"], t + 1)
                pe.wait_ge(S["ptb"], t + 1)
                for bb in range(2):
                    for gp in range(2):
                        r = slice(bb * 64 + gp * 32, bb * 64 + gp * 32 + 32)
                        out, c = PS[r, 3, 0:P], slice(gp * P, (gp + 1) * P)
                        for br, v in enumerate((VSN, VWN)):
                            for h in range(2):
                                pe.matmul(out, PTA[:, br * 2 + h, r], v[:, bb, h, c], start=br == 0 and h == 0, stop=False)
                            pe.matmul(out, PTB[0:32, br, r], KV[0:NS, 3 + 2 * br, QT, c], start=False, stop=False)
                        m = pe.matmul(out, PTB[0:32, 2, r], CVS[0:32, t, c], start=False, stop=True)
                m.then_inc(S["s_o"], 1)
                pe.wait_ge(S["os_ready"], t + 1)
                pe.transpose(PS[:, 6, 0:P], OS[:, :], ID).then_inc(S["s_ot"], 1)
                pe.wait_ge(S["ots_ready"], t + 1)

        def samp_act(act, L):
            for t in range(4):
                for bb in range(2):
                    act.wait_ge(S["kb_full"], 4 * t + 2 * bb + 1)
                    if bb:
                        act.wait_ge(S["s_qk"], 2 * t + bb)
                    L(act.activation(KTB[:, 0, :, :], PS[:, 4, :].rearrange("p (a n) -> p a n", a=2), ACT.Copy), S["ktb_a"])
                act.wait_ge(S["s_max"], t + 1)
                for j, (p_, n) in enumerate(((PS_[:, 0, :], 288), (PS_[:, 1, :], 288), (PC_[:, :], 32))):
                    L(act.activation(p_, PS[:, j, 0:n], ACT.Exp, scale=SCALE, bias=soft_cols(3 + j), accum_out=soft_cols(6 + j)),
                      S["s_exp"])
                act.wait_ge(S["s_pt"], 2 * t + 1)
                L(act.activation(PTA[:, :, :], PS[:, 4, :].rearrange("p (a n) -> p a n", a=4), ACT.Copy), S["pta"])
                act.wait_ge(S["s_o"], t + 1)
                L(act.activation(OS[:, :], PS[:, 3, 0:P], ACT.Copy), S["os_ready"])
                act.wait_ge(S["s_ot"], t + 1)
                L(act.activation(OTS[:, t, :], PS[:, 6, 0:P], ACT.Copy), S["ots_ready"])

        def samp_dve(dve, L):
            dve.wait_ge(S["grow_full"], 1)
            gt = GRT[:, :, :]
            L(dve.tensor_tensor(gt, PS[:, 7, 0:192].rearrange("p (t n) -> p t n", t=4),
                                CST[:, C_HM:C_HM + 48].rearrange("p (o n) -> p o n", o=1).broadcast_to([P, 4, 48]), ALU.mult))
            L(dve.tensor_reduce(GROW[:, :, :], gt.rearrange("p t (h b) -> p t b h", b=3), AX.X, ALU.add))
            for t in range(4):
                for bb in range(2):
                    dve.wait_ge(S["kb_full"], 4 * t + 2 * bb + 2)
                    if bb:
                        dve.wait_ge(S["s_qk"], 2 * t + bb)
                    L(dve.tensor_copy(KTB[:, 1, :, :], PS[:, 5, :].rearrange("p (a n) -> p a n", a=2)), S["ktb_d"])
                dve.wait_ge(S["s_qk"], 2 * t + 2)
                for j, n in enumerate((288, 288, 32)):
                    L(dve.tensor_reduce(soft_cols(j), PS[:, j, 0:n], AX.X, ALU.max))
                L(dve.tensor_scalar(SM[:, 0, 3:6], SM[:, 0, 0:3], -SCALE, None, ALU.mult), S["s_max"])
                dve.wait_ge(S["s_exp"], 3 * t + 3)
                L(dve.reciprocal(SM[:, 0, 9:12], SM[:, 0, 6:9]))
                L(dve.tensor_tensor(SM[:, 0, 12:14], SM[:, 0, 9:11], GROW[:, t, 1:3], ALU.mult))
                L(dve.tensor_tensor(SM[:, 0, 14:15], SM[:, 0, 11:12], GROW[:, t, 0:1], ALU.mult))
                L(dve.tensor_scalar(PS_[:, 0, :], PS_[:, 0, :], soft_cols(12), None, ALU.mult))
                L(dve.tensor_scalar(PS_[:, 1, :], PS_[:, 1, :], soft_cols(13), None, ALU.mult))
                L(dve.tensor_scalar(PC_[:, :], PC_[:, :], soft_cols(14), None, ALU.mult), S["s_scaled"])
                dve.wait_ge(S["s_pt"], 2 * t + 2)
                L(dve.tensor_copy(PTB[0:32, :, :], PS[0:32, 5, 0:3 * P].rearrange("p (a n) -> p a n", a=3)), S["ptb"])
            dve.wait_ge(S["ots_ready"], 4)
            for g2 in range(2):
                for hh in range(GQ):
                    src = OTS[g2 * HD:(g2 + 1) * HD, :, :].rearrange("p t (b a g h s) -> p a (t b) g h s", b=2, a=2, g=2, h=GQ)
                    dst = QC[(hh % 2) * HD:(hh % 2) * HD + HD, :, SEQ:T].rearrange("p (a g h) (b s) -> p a b g h s", a=2, g=2, s=DT)
                    L(dve.tensor_copy(dst[:, :, :, g2, hh // 2, :], src[:, :, :, g2, hh, :]))

        def samp_pool(pool, L):
            for dst, src in ((QBC, QC), (QBR, QR)):
                L(pool.memset(dst[:, :, :, :], 0.0))
                for g2 in range(2):
                    for hh in range(GQ):
                        s_ = src[(hh % 2) * HD:(hh % 2) * HD + HD, :, SEQ:T].rearrange("p (a g h) (b s) -> p b a g h s", a=2, g=2, s=DT)
                        L(pool.tensor_copy(dst[g2 * HD:(g2 + 1) * HD, :, :, g2 * 16 + hh * 4:g2 * 16 + hh * 4 + 4],
                                           s_[:, :, :, g2, hh // 2, :]),
                          S["qbd_ready"] if dst is QBR and g2 == 1 and hh == GQ - 1 else None)

        class Group:
            def __init__(self, kind, step, pair=0, half=0, blocks=(), last=False):
                self.kind, self.step, self.pair, self.half = kind, step, pair, half
                self.blocks, self.last, self.real = blocks, last, None

        def prompt_groups():
            out = []
            for u in range(16):
                qt = u % QT
                if u == 0:
                    out.append(Group("scores", -1, pair=0))
                    out += [Group("cmp", u, pair=0, half=h) for h in range(2)]
                if u == 6:
                    out += [Group("cmp", u, pair=1, half=h) for h in range(2)]
                if u == 9:
                    out.append(Group("out", u, pair=0))
                blocks = [(br, kt) for br in range(2) for kt in range(qt + 1)]
                for i in range(0, len(blocks), 4):
                    out.append(Group("pv", u, blocks=blocks[i:i + 4], last=i + 4 >= len(blocks)))
                if u == 4:
                    out.append(Group("scores", u, pair=1))
            out.append(Group("out", 16, pair=1))
            real = 0
            for i, g in enumerate(out):
                g.bank, g.nth = i % 2, i // 2
                if g.kind == "pv":
                    g.real = real
                    real += 1
            return out, real

        GRP, N_REAL = prompt_groups()
        N_HALF = len(GRP) // 2
        OWNER = ("grp_dve", "grp_act")
        assert len(GRP) % 2 == 0 and N_REAL % 2 == 0
        assert all(x.bank == 0 for x in GRP if x.kind == "scores")

        def at_step(u):
            return [g for g in GRP if g.step == u]

        def head_gates(hp, half, first, n):
            return (2 * hp + half) * 3 + first

        def SC(u, br):
            return 2 * (u % 2) + br

        def prompt_pe(pe):
            pe.drain().then_inc(S["p_qk"], 8)
            pe.drain().then_inc(S["p_qc"], 1)
            pe.drain().then_inc(S["p_pt"], 2)
            pe.drain().then_inc(S["p_pv"], 2)
            with pe.Fori(0, KG) as g:
                def qk_cmp(gr):
                    pe.wait_ge(S["qs_c"], g * 4 + (2 * gr.pair + 2))
                    for half in range(2):
                        for qt in range(QT):
                            c = half * P + qt * 32
                            pe.matmul(PS[:, 6, c:c + 32], IDB[:, :], CMPB[:, qt * 32:(qt + 1) * 32], start=True, stop=False)
                            m = pe.matmul(PS[:, 6, c:c + 32], QS[:, half, 0, qt * P:(qt + 1) * P],
                                          CKP[:, ds(g, 1), :].rearrange("p o n -> p (o n)"), start=False, stop=True)
                    m.then_inc(S["p_grp"], 1)
                    pe.drain().then_inc(S["p_qc"], 1)

                def qk(u):
                    hh, qt = u // QT, u % QT
                    n = (qt + 1) * P
                    if qt == 0:
                        pe.wait_ge(S["qs_r"], g * 4 + (hh + 1))
                    pe.wait_ge(S["p_exp"], g * 16 + (u + 1))
                    for br, kt in enumerate((KTS, KTW)):
                        q = QS[:, hh % 2, 1, qt * P:(qt + 1) * P]
                        pe.matmul(PS[:, SC(u, br), qt * P:n], IDB[:, :], CAUB[:, :], start=True, stop=False)
                        m = pe.matmul(PS[:, SC(u, br), qt * P:n], q, kt[:, ds(g, 1), qt * P:n].rearrange("p o n -> p (o n)"),
                                      start=False, stop=True)
                        if qt:
                            m = pe.matmul(PS[:, SC(u, br), 0:qt * P], q, kt[:, ds(g, 1), 0:qt * P].rearrange("p o n -> p (o n)"),
                                          start=True, stop=True)
                    m.then_inc(S["p_qk"], 1)

                def bank_wait(gr):
                    pe.wait_ge(S[OWNER[gr.bank]], g * N_HALF + (gr.nth + 1))

                def transposes(gr):
                    bank_wait(gr)
                    if gr.kind == "scores":
                        qk_cmp(gr)
                        return
                    if gr.kind == "cmp":
                        if gr.half == 0:
                            pe.wait_ge(S["c_scaled"], g * 2 + (gr.pair + 1))
                        for qt in range(QT):
                            m = pe.transpose(PS[0:32, 6 + gr.bank, qt * P:(qt + 1) * P], PPC[:, gr.half * QT + qt, :], ID)
                    elif gr.kind == "out":
                        pe.wait_ge(S["o_used"], g * 16 + (8 * gr.pair + 10))
                        for qt in range(QT):
                            m = pe.transpose(PS[:, 6 + gr.bank, qt * P:(qt + 1) * P], ON[:, gr.pair, qt, :], ID)
                    else:
                        pe.wait_ge(S["p_exp"], g * 16 + (gr.step + 3))
                        for i, (br, kt) in enumerate(gr.blocks):
                            m = pe.transpose(PS[:, 6 + gr.bank, i * P:(i + 1) * P], PP[:, gr.step % 2, br, kt * P:(kt + 1) * P], ID)
                        if gr.last:
                            m.then_inc(S["p_grp"], 1)
                            pe.drain().then_inc(S["p_pt"], 1)
                            return
                    m.then_inc(S["p_grp"], 1)

                def values(gr):
                    u = gr.step
                    qt = u % QT
                    pe.wait_ge(S[OWNER[gr.bank]], g * N_HALF + (gr.nth + 2))
                    if gr.blocks[0] == (0, 0):
                        pe.wait_ge(S["o_used"], g * 16 + (u + 1))
                        hp, half = u // 8, (u // 4) % 2
                        cg = [x for x in GRP if x.kind == "cmp" and x.pair == hp and x.half == half][0]
                        if qt == 0:
                            pe.wait_ge(S[OWNER[cg.bank]], g * N_HALF + (cg.nth + 2))
                    for i, (br, kt) in enumerate(gr.blocks):
                        m = pe.matmul(PS[:, 4 + u % 2, (1 + br) * HD:(2 + br) * HD], PT[:, gr.real % 2, i * P:(i + 1) * P],
                                      KV[:, 3 + 2 * br, kt, ds(g * HD, HD)], start=kt == 0, stop=kt == qt)
                        if (br, kt) == (0, qt):
                            m = pe.matmul(PS[:, 4 + u % 2, 0:HD], PCT[0:32, u // 8, (u // 4) % 2 * QT + qt, :],
                                          CVP[0:32, ds(g * HD, HD)], start=True, stop=True)
                    m.then_inc(S["p_pv"], 1)

                for gr in at_step(-1):
                    transposes(gr)
                qk(0)
                pending = None
                for u in range(16):
                    if u < 15:
                        qk(u + 1)
                    for gr in at_step(u):
                        transposes(gr)
                        if pending is not None:
                            values(pending)
                            pending = None
                        if gr.kind == "pv":
                            pending = gr
                values(pending)
                for gr in at_step(16):
                    transposes(gr)

        def evacs(eng, L, g, u, bank, scores=None):
            copy = (lambda o_, i_: eng.activation(o_, i_, ACT.Copy)) if bank == 1 else (lambda o_, i_: eng.tensor_copy(o_, i_))
            done = S[OWNER[bank]]
            for i, gr in enumerate(GRP):
                if gr.step != u or gr.bank != bank:
                    continue
                eng.wait_ge(S["p_grp"], g * len(GRP) + (i + 1))
                src = PS[:, 6 + bank, :]
                if gr.kind == "scores":
                    scores(src, done)
                elif gr.kind == "cmp":
                    eng.wait_ge(S["p_pv"], g * N_REAL + 2)
                    L(copy(PCT[0:32, gr.pair, gr.half * QT:(gr.half + 1) * QT, :],
                           src[0:32, :].rearrange("p (t n) -> p t n", t=QT)), done)
                elif gr.kind == "out":
                    L(copy(QC[:, ds(g * 2 + gr.pair, 1), 0:SEQ].rearrange("p o n -> p (o n)"), src), done)
                else:
                    n = len(gr.blocks) * P
                    eng.wait_ge(S["p_pv"], g * N_REAL + (gr.real + 1))
                    L(copy(PT[:, gr.real % 2, 0:n], src[:, 0:n]), done)

        def prompt_act(act, L):
            act.drain().then_inc(S["grp_act"], 1)
            act.drain().then_inc(S["p_exp"], 2)
            L.count[S["grp_act"]], L.count[S["p_exp"]] = 1, 2
            with act.Fori(0, KG) as g:
                L.loop(g, grp_act=N_HALF, act_chain=16, p_exp=16, c_exp=2)
                def exps(u):
                    n = (u % QT + 1) * P
                    act.wait_ge(S["p_max"], g * 16 + (u + 1))
                    act.wait_ge(S["p_pt"], g * 16 + (u + 1))
                    for br in range(2):
                        L(act.activation(PP[:, u % 2, br, 0:n], PS[:, SC(u, br), 0:n], ACT.Exp, scale=SCALE,
                                         bias=SM[:, u % 2, 2 + br:3 + br], accum_out=SM[:, u % 2, 4 + br:5 + br]),
                          S["p_exp"] if br else None)

                def exp_cmp(hp):
                    sc = [x for x in GRP if x.kind == "scores" and x.pair == hp][0]
                    act.wait_ge(S["grp_dve"], g * N_HALF + (sc.nth + 2))
                    L(act.activation(PPC[:, :, :], PPC[:, :, :], ACT.Exp, scale=SCALE), S["c_exp"])

                exp_cmp(0)
                exps(0)
                for u in range(16):
                    if u == 5:
                        exp_cmp(1)
                    evacs(act, L, g, u, 1)
                    if u < 15:
                        exps(u + 1)
                evacs(act, L, g, 16, 1)
            L.end(KG)

        def prompt_dve(dve, L):
            dve.drain().then_inc(S["grp_dve"], 1)
            dve.drain().then_inc(S["o_used"], 2)
            L.count[S["grp_dve"]], L.count[S["o_used"]] = 1, 2
            with dve.Fori(0, KG) as g:
                L.loop(g, grp_dve=N_HALF, dve_chain=110, p_max=16, c_scaled=2, o_used=16)
                def cmp_a(src, done):
                    s = src[:, 0:256].rearrange("p (t n) -> p t n", n=32)
                    L(dve.tensor_reduce(SMC[:, 0, :], s, AX.X, ALU.max))
                    L(dve.tensor_scalar(SMC[:, 0, :], SMC[:, 0, :], FLOOR, None, ALU.max))
                    L(dve.tensor_tensor(PPC[:, :, :], s, SMC[:, 0, :].rearrange("p (t o) -> p t o", o=1).broadcast_to([P, 8, 32]),
                                        ALU.subtract), done)

                def cmp_b(hp):
                    dve.wait_ge(S["c_exp"], g * 2 + (hp + 1))
                    L(dve.tensor_reduce(SMC[:, 1, :], PPC[:, :, :], AX.X, ALU.add))
                    L(dve.tensor_scalar(SMC[:, 1, :], SMC[:, 1, :], 1e-30, None, ALU.max))
                    L(dve.reciprocal(SMC[:, 2, :], SMC[:, 1, :]))
                    for half in range(2):
                        c = SMC[:, 3, half * QT:(half + 1) * QT].rearrange("p (t o) -> p t o", o=1)
                        r = SMC[:, 2, half * QT:(half + 1) * QT].rearrange("p (t o) -> p t o", o=1)
                        L(dve.tensor_tensor(c, r, GT[:, 0:QT, ds(g * 12 + head_gates(hp, half, 0, 1), 1)], ALU.mult))
                    L(dve.tensor_tensor(PPC[:, :, :], PPC[:, :, :],
                                        SMC[:, 3, :].rearrange("p (t o) -> p t o", o=1).broadcast_to([P, 8, 32]), ALU.mult),
                      S["c_scaled"])

                def maxima(u):
                    n = (u % QT + 1) * P
                    dve.wait_ge(S["p_qk"], g * 16 + (u + 9))
                    for br in range(2):
                        L(dve.tensor_reduce(SM[:, u % 2, br:br + 1], PS[:, SC(u, br), 0:n], AX.X, ALU.max))
                    L(dve.tensor_scalar(SM[:, u % 2, 2:4], SM[:, u % 2, 0:2], -SCALE, None, ALU.mult), S["p_max"])

                def norm(u):
                    dve.wait_ge(S["p_exp"], g * 16 + (u + 3))
                    L(dve.reciprocal(SM[:, u % 2, 6:8], SM[:, u % 2, 4:6]))
                    L(dve.tensor_tensor(SM[:, u % 2, 8:10], SM[:, u % 2, 6:8],
                                        GT[:, u % QT, ds(g * 12 + head_gates(u // 8, (u // 4) % 2, 1, 2), 2)], ALU.mult))

                def combine(u):
                    last = max(x.real for x in GRP if x.kind == "pv" and x.step == u)
                    dve.wait_ge(S["p_pv"], g * N_REAL + (last + 3))
                    ob, half = PS[:, 4 + u % 2, :], (u // 4) % 2
                    L(dve.tensor_scalar(OM[:, u % 2, :], ob[:, HD:2 * HD], SM[:, u % 2, 8:9], None, ALU.mult))
                    L(dve.scalar_tensor_tensor(OM[:, u % 2, :], ob[:, 2 * HD:3 * HD], SM[:, u % 2, 9:10], OM[:, u % 2, :],
                                               ALU.mult, ALU.add))
                    L(dve.tensor_tensor(ON[:, u // 8, u % QT, half * HD:(half + 1) * HD], OM[:, u % 2, :], ob[:, 0:HD], ALU.add),
                      S["o_used"])

                evacs(dve, L, g, -1, 0, cmp_a)
                maxima(0)
                cmp_b(0)
                for u in range(16):
                    if u < 15:
                        maxima(u + 1)
                    if u == 5:
                        cmp_b(1)
                    norm(u)
                    evacs(dve, L, g, u, 0, cmp_a)
                    if u:
                        combine(u - 1)
                combine(15)
                evacs(dve, L, g, 16, 0)
            L.end(KG)

        def prompt_pool(pool, L):
            with pool.Fori(0, KG) as g:
                L.loop(g, qs_c=4, qs_r=4)
                for hp in range(2):
                    for br, src, s in ((0, QC, "qs_c"), (1, QR, "qs_r")):
                        for half in range(2):
                            if br == 0:
                                if half == 0:
                                    pool.wait_ge(S["p_qc"], g * 2 + (hp + 1))
                            else:
                                pool.wait_ge(S["p_qk"], g * 16 + (8 * hp + 4 * half + 4))
                            pool.wait_ge(S["qbd_ready"], 1)
                            L(pool.tensor_copy(QS[:, half, br, :],
                                               src[half * HD:(half + 1) * HD, ds(g * 2 + hp, 1), 0:SEQ].rearrange("p o n -> p (o n)")),
                              S[s])
            L.end(KG)

        def nsa_pe(pe):
            proj_pe(pe)
            end_phase(pe, 5)
            rope_pe(pe)
            end_phase(pe, 6)
            cmp_pe(pe)
            end_phase(pe, 7)
            samp_pe(pe)
            end_phase(pe, 8)
            prompt_pe(pe)
            end_phase(pe, 9)
            pe_linear(pe, 4, S_WO, B_WO, x_ready, 8 * 5)
            end_phase(pe, 10)
            stat_pe(pe, 4, 6)
            ffn_pe(pe, 1, S_FFN1, B_FFN1, 6, 5, 7)
            end_phase(pe, 11)

        def nsa_act(act, L):
            proj_act(act, L)
            end_phase(act, 5)
            rope_act(act, L)
            end_phase(act, 6)
            cmp_act(act, L)
            end_phase(act, 7)
            samp_act(act, L)
            end_phase(act, 8)
            prompt_act(act, L)
            end_phase(act, 9)
            for c in range(NC):
                L(act.activation(XH[:, c, :], QC[:, c, :], ACT.Copy), S["xh_ready"])
            act.wait_ge(stores, 16 * N_KV_ST)
            with act.Fori(0, 2) as i:
                for h in range(2):
                    act_split_ahead(act, i, S_WO, B_WO, h)
                    for mb in range(2):
                        act.wait_ge(blk_full, i * 4 + (B_WO + 2 * h + mb + 1))
                        act.activation(F[:, ds(i * 4 + (2 * h + mb), 1), :].rearrange("p o (h n) -> p (o h) n", h=2),
                                       blk(mb), ACT.Copy).then_inc(blk_free, 1)
            end_phase(act, 10)
            stat_act(act, L, F, 4)
            std_act(act, L, S["stat_used"], 7)
            residual_act(act, L, V_FPRE + NC, 3, 6, True, 1)
            ffn_act(act, L, 1, S_FFN1, B_FFN1, 6, 4, 5, 5, True)
            end_phase(act, 11)

        def nsa_dve(dve, L):
            proj_dve(dve, L)
            end_phase(dve, 5)
            rope_dve(dve, L)
            end_phase(dve, 6)
            cmp_dve(dve, L)
            end_phase(dve, 7)
            samp_dve(dve, L)
            end_phase(dve, 8)
            prompt_dve(dve, L)
            end_phase(dve, 9)
            for c in range(NC):
                dve.wait_ge(S["xh_ready"], 8 * 5 + c + 1)
                L(dve.tensor_tensor(XL[:, c, :], QC[:, c, :], XH[:, c, :].bitcast(F32), ALU.subtract), x_ready)
            with dve.Fori(0, 2) as i:
                for h in range(2):
                    dve_split_ahead(dve, i, S_WO, h)
            end_phase(dve, 10)
            rstd_dve(dve, L, 4, 4)
            residual_dve(dve, L, V_MPOST + NC, V_FPRE + NC, 3, 6)
            ffn_dve(dve, L, 1, S_FFN1, B_FFN1, 6, 4, V_FPOST + NC, 5, 5, True)
            end_phase(dve, 11)

        def nsa_pool(pool, L):
            proj_pool(pool, L)
            end_phase(pool, 5)
            rope_pool(pool, L)
            end_phase(pool, 6)
            cmp_pool(pool, L)
            end_phase(pool, 7)
            samp_pool(pool, L)
            end_phase(pool, 8)
            prompt_pool(pool, L)
            end_phase(pool, 9)
            load_p(pool, 1)
            end_phase(pool, 10)
            residual_pool(pool, L, 1)
            end_phase(pool, 11)
        @block.sync
        def _(sp):
            sp.dma_start(CST[:, :], a["consts"]).then_inc(S["ld_const"], 16)
            for tt in range(QT):
                sp.dma_start(XTOK[:, tt, :], a["x_prompt"][0, tt * P:(tt + 1) * P, :]).then_inc(S["ld_x"], 16)
            sp.dma_start(XTOK[0:NS, QT, :], a["x_sample"].rearrange("b t d -> (b t) d")).then_inc(S["ld_x"], 16)
            for row, n, src in ((V_MPRE, 16, "norm_mix_pre"), (V_MPOST, 16, "norm_mix_post"), (V_FPRE, 16, "norm_ffn_pre"),
                                (V_FPOST, 16, "norm_ffn_post"), (V_BIN, 16, "conv_b_in"), (V_BDW, 8, "conv_b_dw"),
                                (V_LNG, 8, "conv_ln_g"), (V_LNB, 8, "conv_ln_b"), (V_BOUT, 8, "conv_b_out")):
                sp.dma_start(VROW[row:row + n, :], a[src].rearrange("l (c p) -> (l c) p", p=P)).then_inc(S["ld_vec"], 16)
            sp.dma_start(WDT[:, :], a["conv_w_dw"][0]).then_inc(S["ld_vec"], 16)
            sp.dma_start(STT[:, :, :], a["state_conv"][0].rearrange("(h b) j d -> (b j) h d", h=2)).then_inc(S["ld_state"], 16)

            def slab(src, i, s, par, wait=True):
                if wait:
                    sp.wait_ge(w_lo, s - 1)
                raw = RAW[par][:, :].rearrange("p (h x) -> p h x", h=2)
                for h in range(2):
                    v = src(i, h)
                    sp.dma_start(raw[:, h, :].rearrange("p (k n) -> p k n", k=v.shape[1]), v).then_inc(w_raw[par], 16)

            s = 0
            for n_stage, (src, n) in enumerate(STAGES):
                if s == S_WO:
                    sp.wait_ge(S["ld_gate"], 48)
                    sp.wait_ge(phase, 4 * 6)
                    nsa_kv_stores(sp)
                    nsa_pair_loads(sp)
                    for h in range(2):
                        slab(src, h, s + h, (s + h) % 2)
                    sp.wait_ge(phase, 4 * 7)
                    for t in range(4):
                        if t:
                            sp.wait_ge(S["s_o"], t)
                        nsa_sample_loads(sp, t)
                    for h in range(2, 4):
                        slab(src, h, s + h, (s + h) % 2)
                    s += n
                    continue
                if n == 1:
                    slab(src, 0, s, s % 2)
                elif s == 0:
                    for h in range(2):
                        slab(src, h, h, h, wait=False)
                    with sp.Fori(1, n // 2) as i:
                        for h in range(2):
                            slab(src, i * 2 + h, i * 2 + h, h)
                else:
                    with sp.Fori(0, n // 2) as i:
                        for h in range(2):
                            slab(src, i * 2 + h, i * 2 + (s + h), (s + h) % 2)
                s += n
            for tt in range(NTT):
                sp.wait_ge(S["y_rows"], 2 * tt + 2)
                if tt < QT:
                    sp.dma_start(o["y_prompt"][0, tt * P:(tt + 1) * P, :], YTOK[:, tt, :]).then_inc(stores, 16)
                else:
                    sp.dma_start(o["y_sample"].rearrange("b t d -> (b t) d"), YTOK[0:NS, QT, :]).then_inc(stores, 16)
            sp.wait_ge(stores, 16 * (NTT + N_KV_ST))
            sp.wait_ge(stores_pool, 16 * conv_states_n)

        @block.tensor
        def _(pe):
            pe.drain().then_inc(blk_full, 2)
            pe.wait_ge(S["ld_const"], 16)
            pe.wait_ge(S["ld_vec"], 160)
            pe.wait_ge(S["ld_state"], 16)
            pe.transpose(PS[:, 4, 0:V_ALL], VROW[:, :], ID[0:V_ALL, 0:V_ALL]).then_inc(S["bank_full"], 1)
            for c in range(NC):
                m = pe.transpose(PS[:, 5, c * 32:c * 32 + CW], WDT[:, c * P:(c + 1) * P], ID[0:CW, 0:CW])
            m.then_inc(S["bank_full"], 1)
            pe.wait_ge(S["ld_x"], 16 * NTT)
            for c in range(NC):
                if c >= 4:
                    pe.wait_ge(S["bank_free"], 2 + c - 3)
                for tt in range(QT):
                    m = pe.transpose(PS[:, c % 4, tt * P:(tt + 1) * P], XTOK[:, tt, c * P:(c + 1) * P], ID)
                m.then_inc(S["bank_full"], 1)
            for c in range(NC):
                m = pe.transpose(PS[:, 6, c * NS:(c + 1) * NS], XTOK[0:NS, QT, c * P:(c + 1) * P], ID[0:NS, 0:NS])
            m.then_inc(S["bank_full"], 1)
            for c in range(NC):
                pe.wait_ge(S["bank_free"], c + 7 if c < 4 else c + 8)
                for h in range(2):
                    m = pe.transpose(PS[:, c % 4, h * 120:(h + 1) * 120], STT[:, h, c * P:(c + 1) * P], ID[0:120, 0:120])
                m.then_inc(S["bank_full"], 1)
            pe.wait_ge(S["bank_free"], 19)
            for c in range(NC):
                pe.wait_ge(S["x_scaled"], 10)
                if c >= 4:
                    pe.wait_ge(x_ready, c - 3)
                for tt in range(QT):
                    m = pe.transpose(PS[:, c % 4, tt * P:(tt + 1) * P], XTOK[:, tt, c * P:(c + 1) * P], ID)
                m.then_inc(S["bank_full"], 1)
            for c in range(NC):
                m = pe.transpose(PS[:, 7, c * NS:(c + 1) * NS], XTOK[0:NS, QT, c * P:(c + 1) * P], ID[0:NS, 0:NS])
            m.then_inc(S["bank_full"], 1)
            end_phase(pe, 1)
            pe_linear(pe, 8, S_CONV, B_CONV, width=P, mb_step=D)
            pe.wait_ge(S["conv_done"], NC)
            for h, (c0, n) in enumerate(((SEQ, CW - 1), (XP + (CW - 1) * DB, NS))):
                for half in range(2):
                    for c in range(4):
                        m = pe.transpose(PS[0:n, 4 + 2 * h + half, c * P:(c + 1) * P], XIN[:, half * 4 + c, c0:c0 + n], ID)
                    m.then_inc(S["bank_full"], 1)
            end_phase(pe, 2)
            for c in range(NC):
                m = pe_ones(pe, F[:, c, :], c == 0, c == NC - 1)
            m.then_inc(S["stat_ready"], 1)
            stat_pe(pe, 0, 1)
            pe_linear(pe, 4, S_CONVO, B_CONVO, x_ready, 8 * 1)
            end_phase(pe, 3)
            stat_pe(pe, 1, 2)
            ffn_pe(pe, 0, S_FFN0, B_FFN0, 2, 2, 3)
            end_phase(pe, 4)
            nsa_pe(pe)
            for tt in range(NTT):
                rows = P if tt < QT else NS
                for half in range(2):
                    i = 2 * tt + half
                    if i >= 4:
                        pe.wait_ge(S["y_rows"], i - 3)
                    for c in range(4):
                        m = pe.transpose(PS[0:rows, 4 + i % 4, c * P:(c + 1) * P],
                                         R[:, half * 4 + c, tt * P:tt * P + rows], ID)
                    m.then_inc(S["y_full"], 1)

        @block.scalar
        def _(act):
            L = Link(act, chain["act"])
            act.wait_ge(S["ld_x"], 16 * NTT)
            act.wait_ge(S["masks"], 6)
            for tt in range(NTT):
                rows = P if tt < QT else NS
                L(act.activation(JNK[0:rows, :], XTOK[0:rows, tt, :], ACT.Square, accum_out=SS5[0:rows, tt:tt + 1]),
                  S["row_sq"])
            act.wait_ge(S["row_rstd"], 1)
            L(act.activation(SS5[:, 0:NTT], SS5[:, 0:NTT], ACT.Sqrt), S["row_sq"])
            act.wait_ge(S["row_rstd"], 2)
            act.wait_ge(S["bank_full"], 11)
            for tt in range(NTT):
                rows = P if tt < QT else NS
                for h in range(2):
                    L(act.activation(XTOK[0:rows, tt, h * 512:(h + 1) * 512], XTOK[0:rows, tt, h * 512:(h + 1) * 512],
                                     ACT.Copy, scale=SS5[0:rows, tt:tt + 1]), S["x_scaled"])
            for c in range(NC):
                act.wait_ge(S["bank_full"], 20 + c)
                L(act.activation(XH[:, c, 0:SEQ], PS[:, c % 4, :], ACT.Copy, scale=vec(V_MPRE + c)), S["xh_ready"])
            act.wait_ge(S["bank_full"], 28)
            L(act.activation(TMP[0][:, 0:256], PS[:, 7, 0:256], ACT.Copy), S["row_sq"])
            act.wait_ge(S["row_rstd"], 3)
            L(act.activation(XH[:, :, SEQ:T], TMP[0][:, 0:256].rearrange("p (c n) -> p c n", c=NC), ACT.Copy), S["xs_hi"])
            split_hi(act, 0, 0, 0, B_CONV)
            end_phase(act, 1)
            with act.Fori(0, 4) as i:
                for h in range(2):
                    act_split_ahead(act, i, S_CONV, B_CONV, h)
                    b = B_CONV + 2 * h
                    act.wait_ge(S["glu_used"], i * 2 + (h + 1))
                    c = i * 2 + h
                    act.wait_ge(blk_full, i * 4 + (b + 1))
                    act.activation(two(TMP[2 * h][:, :]), blk(0), ACT.Identity,
                                   bias=VEC[:, ds(c + V_BIN, 1)]).then_inc(blk_free, 1)
                    act.wait_ge(blk_full, i * 4 + (b + 2))
                    act.activation(two(TMP[2 * h + 1][:, :]), blk(1), ACT.Sigmoid,
                                   bias=VEC[:, ds(c + V_BIN + NC, 1)]).then_inc(blk_free, 1)
            act.wait_ge(S["bank_full"], 32)
            for h, n in enumerate((CW - 1, NS)):
                for half in range(2):
                    L(act.activation(CST_OUT[0:n, h, half * 512:(half + 1) * 512], PS[0:n, 4 + 2 * h + half, :], ACT.Copy),
                      S["cs_rows"])
            end_phase(act, 2)
            act.wait_ge(S["mean_ready"], 1)
            for c in range(NC):
                act.wait_ge(S["mean_ready"], 1 + c)
                if c >= 2:
                    act.wait_ge(S["sq_used"], c - 1)
                L(act.activation(TMP[c % 2][:, :], F[:, c, :], ACT.Square), S["sq_ready"])
            std_act(act, L, S["stat_used"], 2)
            for c in range(NC):
                act.wait_ge(S["silu_ready"], c + 1)
                L(act.activation(TMP[c % 2][:, :], TMP[c % 2][:, :], ACT.Silu, scale=vec(V_LNG + c), bias=vec(V_LNB + c)))
                L(act.activation(XH[:, c, :], TMP[c % 2][:, :], ACT.Copy), S["xh_ready"])
            with act.Fori(0, 2) as i:
                for h in range(2):
                    act_split_ahead(act, i, S_CONVO, B_CONVO, h)
                    for mb in range(2):
                        c = i * 4 + (2 * h + mb)
                        act.wait_ge(blk_full, i * 4 + (B_CONVO + 2 * h + mb + 1))
                        act.activation(F[:, ds(c, 1), :].rearrange("p o (h n) -> p (o h) n", h=2), blk(mb), ACT.Identity,
                                       bias=VEC[:, ds(c + V_BOUT, 1)]).then_inc(blk_free, 1)
            end_phase(act, 3)
            stat_act(act, L, F, 1)
            std_act(act, L, S["stat_used"], 3)
            residual_act(act, L, V_FPRE, 0, 2, True, 0)
            ffn_act(act, L, 0, S_FFN0, B_FFN0, 2, 1, 2, 2, False)
            end_phase(act, 4)
            nsa_act(act, L)
            for i in range(2 * NTT):
                rows = P if i // 2 < QT else NS
                act.wait_ge(S["y_full"], i + 1)
                L(act.activation(YTOK[0:rows, i // 2, (i % 2) * 512:(i % 2) * 512 + 512], PS[0:rows, 4 + i % 4, :], ACT.Copy),
                  S["y_rows"])

        @block.vector
        def _(dve):
            L = Link(dve, chain["dve"])
            L(dve.memset(SS5[:, :], 1.0), S["masks"])
            dve.wait_ge(S["ld_const"], 16)
            L(dve.tensor_copy(IDB[:, :], CST[:, C_ID:C_ID + P]), S["masks"])
            L(dve.tensor_copy(CAUB[:, :], CST[:, C_CAU:C_CAU + P]), S["masks"])
            L(dve.tensor_copy(CMPB[:, :], CST[:, C_CMP:C_CMP + QT * 32]), S["masks"])
            L(dve.tensor_copy(NMB[:, :], CST[:, C_NM:C_NM + 128]), S["masks"])
            L(dve.tensor_copy(CMSB[:, :], CST[:, C_CMS:C_CMS + 32]), S["masks"])
            dve.wait_ge(S["bank_full"], 1)
            L(dve.tensor_copy(VEC[:, :], PS[:, 4, 0:V_ALL]), S["bank_free"])
            dve.wait_ge(S["bank_full"], 2)
            L(dve.tensor_copy(WDW[:, :, 0:CW], PS[:, 5, 0:256].rearrange("p (c j) -> p c j", j=32)[:, :, 0:CW]), S["bank_free"])
            dve.wait_ge(S["row_sq"], NTT)
            L(dve.tensor_scalar(SS5[:, 0:NTT], SS5[:, 0:NTT], 1.0 / D, EPS, ALU.mult, ALU.add), S["row_rstd"])
            for c in range(NC):
                dve.wait_ge(S["bank_full"], 3 + c)
                L(dve.tensor_copy(R[:, c, 0:SEQ], PS[:, c % 4, :]), S["bank_free"])
            dve.wait_ge(S["bank_full"], 11)
            L(dve.tensor_copy(R[:, :, SEQ:T], PS[:, 6, 0:256].rearrange("p (c n) -> p c n", c=NC)), S["bank_free"])
            dve.wait_ge(S["row_sq"], NTT + 1)
            L(dve.reciprocal(SS5[:, 0:NTT], SS5[:, 0:NTT]), S["row_rstd"])
            for c in range(NC):
                dve.wait_ge(S["bank_full"], 12 + c)
                L(dve.tensor_copy(XIN[:, c, XP:XP + 240].rearrange("p (j b) -> p b j", b=DB),
                                  PS[:, c % 4, 0:240].rearrange("p (b j) -> p b j", b=DB)), S["bank_free"])
            for c in range(NC):
                dve.wait_ge(S["xh_ready"], c + 1)
                L(dve.scalar_tensor_tensor(XL[:, c, 0:SEQ], PS[:, c % 4, :], vec(V_MPRE + c), XH[:, c, 0:SEQ].bitcast(F32),
                                           ALU.mult, ALU.subtract), x_ready)
            dve.wait_ge(S["row_sq"], NTT + 2)
            tv = TMP[0][:, 0:256].rearrange("p (c n) -> p c n", c=NC)
            L(dve.tensor_tensor(tv, tv, VEC[:, V_MPRE:V_MPRE + NC].rearrange("p (c o) -> p c o", o=1).broadcast_to([P, NC, NS]),
                                ALU.mult), S["row_rstd"])
            dve.wait_ge(S["xs_hi"], 1)
            L(dve.tensor_tensor(XL[:, :, SEQ:T], tv, XH[:, :, SEQ:T].bitcast(F32), ALU.subtract))
            split_lo(dve, 0, 0)
            dve.drain().then_inc(S["glu_used"], 2)
            L.count[S["glu_used"]] = 2
            end_phase(dve, 1)
            with dve.Fori(0, 4) as i:
                L.loop(i, dve_chain=2 * 2 * CW, glu_used=2, conv_done=2)
                for h in range(2):
                    dve_split_ahead(dve, i, S_CONV, h)
                    c = i * 2 + h
                    ta, tg = TMP[2 * h], TMP[2 * h + 1]
                    dve.wait_ge(blk_free, i * 4 + (B_CONV + 2 * h + 2))
                    xin = XIN[:, ds(c, 1), :].rearrange("p o n -> p (o n)")
                    L(dve.tensor_tensor(xin[:, CW - 1:XP], ta[:, 0:SEQ], tg[:, 0:SEQ], ALU.mult))
                    L(dve.tensor_tensor(xin[:, XP + 240:XC].rearrange("p (t b) -> p b t", b=DB),
                                        ta[:, SEQ:T].rearrange("p (b t) -> p b t", b=DB),
                                        tg[:, SEQ:T].rearrange("p (b t) -> p b t", b=DB), ALU.mult), S["glu_used"])
                    y = F[:, ds(c, 1), :].rearrange("p o n -> p (o n)")
                    yp, ys = y[:, 0:SEQ], y[:, SEQ:T].rearrange("p (b t) -> p t b", b=DB)
                    for j in range(CW):
                        w = WDW[:, ds(c, 1), j:j + 1].rearrange("p o n -> p (o n)")
                        xp_ = xin[:, j:j + SEQ]
                        xs_ = xin[:, XP + j * DB:XP + j * DB + NS].rearrange("p (t b) -> p t b", b=DB)
                        if j == 0:
                            bdw = VEC[:, ds(c + V_BDW, 1)]
                            L(dve.tensor_scalar(yp, xp_, w, bdw, ALU.mult, ALU.add))
                            L(dve.tensor_scalar(ys, xs_, w, bdw, ALU.mult, ALU.add))
                        else:
                            L(dve.scalar_tensor_tensor(yp, xp_, w, yp, ALU.mult, ALU.add))
                            L(dve.scalar_tensor_tensor(ys, xs_, w, ys, ALU.mult, ALU.add),
                              S["conv_done"] if j == CW - 1 else None)
            L.end(4)
            end_phase(dve, 2)
            dve.wait_ge(S["stat_ready"], 1)
            L(dve.tensor_scalar(two(TMP[3][:, :]), STAT, 1.0 / D, None, ALU.mult), S["stat_used"])
            for c in range(NC):
                L(dve.tensor_tensor(F[:, c, :], F[:, c, :], TMP[3][:, :], ALU.subtract), S["mean_ready"])
            rstd_dve(dve, L, 0, 0)
            for c in range(NC + 1):
                if c < NC:
                    L(dve.tensor_tensor(TMP[c % 2][:, :], F[:, c, :], RS[:, :], ALU.mult), S["silu_ready"])
                if c:
                    dve.wait_ge(S["xh_ready"], NC + c)
                    L(dve.tensor_tensor(XL[:, c - 1, :], TMP[(c - 1) % 2][:, :], XH[:, c - 1, :].bitcast(F32),
                                        ALU.subtract), x_ready)
            with dve.Fori(0, 2) as i:
                for h in range(2):
                    dve_split_ahead(dve, i, S_CONVO, h)
            end_phase(dve, 3)
            rstd_dve(dve, L, 1, 1)
            residual_dve(dve, L, V_MPOST, V_FPRE, 0, 2)
            ffn_dve(dve, L, 0, S_FFN0, B_FFN0, 2, 1, V_FPOST, 2, 2, False)
            end_phase(dve, 4)
            nsa_dve(dve, L)

        @block.gpsimd
        def _(pool):
            L = Link(pool, chain["pool"])
            L(pool.memset(XIN[:, :, 0:CW - 1], 0.0))
            pool.drain().then_inc(blk_free, 2)
            end_phase(pool, 1)
            end_phase(pool, 2)
            end_phase(pool, 3)
            load_p(pool, 0)
            conv_states(pool)
            residual_pool(pool, L, 0)
            end_phase(pool, 4)
            nsa_pool(pool, L)


_INS = ["x_prompt", "x_sample", "state_conv", "cache_k_cmp", "cache_v_cmp", "cache_k_sel", "cache_v_sel",
        "state_k_win", "state_v_win", "page_table", "p_prompt", "p_sample",
        "norm_mix_pre", "norm_mix_post", "norm_ffn_pre", "norm_ffn_post",
        "conv_w_in", "conv_b_in", "conv_w_dw", "conv_b_dw", "conv_ln_g", "conv_ln_b", "conv_w_out", "conv_b_out",
        "nsa_w_in", "nsa_b_gate", "nsa_pe_k", "nsa_pe_v", "nsa_wk_c1", "nsa_wk_c2", "nsa_wv_c1", "nsa_wv_c2",
        "nsa_w_o", "ffn_w_in", "ffn_w_out", "ple_w_gate", "ple_w_proj"]
_OUTS = [("y_prompt", (1, 512, 1024)), ("y_sample", (8, 4, 1024)), ("conv_state_p", (1, 1, 30, 1024)),
         ("k_cmp_p", (1, 1, 512, 4, 64)), ("v_cmp_p", (1, 1, 512, 4, 64)), ("k_sel_p", (1, 1, 512, 4, 64)),
         ("v_sel_p", (1, 1, 512, 4, 64)), ("k_win_p", (1, 1, 512, 4, 64)), ("v_win_p", (1, 1, 512, 4, 64)),
         ("conv_state_s", (1, 8, 30, 1024)), ("k_cmp_s", (1, 8, 4, 4, 64)), ("v_cmp_s", (1, 8, 4, 4, 64)),
         ("k_sel_s", (1, 8, 4, 4, 64)), ("v_sel_s", (1, 8, 4, 4, 64)), ("k_win_s", (1, 8, 260, 4, 64)),
         ("v_win_s", (1, 8, 260, 4, 64))]


def _consts():
    import numpy as np

    c = np.zeros((P, C_ALL), np.float32)
    r = np.arange(P)
    c[:, C_ID:C_ID + P] = np.eye(P)
    for m in range(P):
        d = m % HD
        if d < 32:
            c[m + 32, C_ROT + m] = -1.0
        else:
            c[m - 32, C_ROT + m] = 1.0
    pos = np.concatenate([np.arange(SEQ), np.tile(PAST + np.arange(DT), DB)]).astype(np.float32)
    inv = np.float32(10000.0) ** (-np.arange(32, dtype=np.float32) / np.float32(32))
    ang = pos[:, None] * inv[None, :].astype(np.float32)
    cos, sin = np.cos(ang), np.sin(ang)
    c[:, C_COS:C_COS + T] = cos[:, r % 32].T
    c[:, C_SIN:C_SIN + T] = sin[:, r % 32].T
    for t in range(NTT):
        n = P if t < QT else NS
        c[:n, C_TC + t * 32:C_TC + t * 32 + 32] = cos[t * P:t * P + n]
        c[:n, C_TS + t * 32:C_TS + t * 32 + 32] = sin[t * P:t * P + n]
    bb, gp, g2, hh, tt = r // 64, r // 32 % 2, r // 16 % 2, r // 4 % 4, r % 4
    head = (gp * 2 + g2) * GQ + hh
    for b in range(3):
        c[r, C_HM + head * 3 + b] = 1.0
    for t in range(4):
        col = np.arange(32)
        ok = (col[None, :] // 4 == 2 * t + bb[:, None]) & (col[None, :] % 4 <= tt[:, None])
        c[:, C_NM + t * 32:C_NM + t * 32 + 32] = np.where(ok, 0.0, NEG)
        c[(2 * t + bb) * 4 + tt, C_SEL + t * P + r] = 1.0
    col = np.arange(32)
    c[:, C_CMS:C_CMS + 32] = np.where((col[None, :] // 16 == bb[:, None]) & (col[None, :] % 16 < 15), 0.0, NEG)
    c[:, C_CAU:C_CAU + P] = np.where(r[None, :] <= r[:, None], 0.0, NEG)
    for t in range(QT):
        c[:, C_CMP + t * 32:C_CMP + t * 32 + 32] = np.where(16 * col[None, :] + 31 <= t * P + r[:, None], 0.0, NEG)
    c[:, C_ONE:C_ONE + P] = 1.0
    return c


def kernel(**inputs):
    import numpy as np
    import concourse.bacc as bacc
    from concourse.bass_utils import run_bass_kernel_spmd

    nc = bacc.Bacc("TRN2", target_bir_lowering=False, num_devices=1)
    arrays, args, outs = {}, {}, {}
    for name in _INS:
        v = np.ascontiguousarray(inputs[name])
        arrays["in_" + name] = v
        args[name] = nc.dram_tensor("in_" + name, v.shape, mybir.dt.from_np(v.dtype), kind="ExternalInput").ap()
    arrays["in_consts"] = _consts()
    args["consts"] = nc.dram_tensor("in_consts", (P, C_ALL), F32, kind="ExternalInput").ap()
    for name, shape in _OUTS:
        outs[name] = nc.dram_tensor("out_" + name, shape, F32, kind="ExternalOutput").ap()
    trunk(nc, args, outs)
    r = run_bass_kernel_spmd(nc, [arrays], core_ids=[0])
    return tuple(r.results[0]["out_" + name] for name, _ in _OUTS)
```

```python
from contextlib import ExitStack

import concourse.bass as bass
from concourse import mybir

F32 = mybir.dt.float32
F32R = mybir.dt.float32r
BF16 = mybir.dt.bfloat16
I32 = mybir.dt.int32
ALU = mybir.AluOpType
ACT = mybir.ActivationFunctionType
AX = mybir.AxisListType
ds = bass.ds

P = 128
D = 1024
NC = D // P
SEQ = 512
DB, DT = 8, 4
NS = DB * DT
T = SEQ + NS
HT = T // 2
NH, HD, KG = 16, 64, 4
GQ = NH // KG
PAST, PAGE = 256, 128
NPAGE = PAST // PAGE
NPOOL = 20
CW = 31
PE_TAPS = 10
FF = 4 * D
PLE = 256
NSLABCOL = 256
SLAB = NC * NSLABCOL
EPS = 1e-6
SCALE = HD ** -0.5
NEG = -1e30
FLOOR = -1e28
XP = CW - 1 + SEQ
XS = (CW - 1 + DT) * DB
XC = XP + XS
QT = SEQ // P
NTT = QT + 1
NCMP_P = 32
XTC = 2 * DB * 16 + 8

C_ID, C_ROT, C_COS, C_SIN = 0, 128, 256, 256 + T
C_TC = C_SIN + T
C_TS = C_TC + NTT * 32
C_HM = C_TS + NTT * 32
C_NM = C_HM + 48
C_CMS = C_NM + 4 * 32
C_CAU = C_CMS + 32
C_CMP = C_CAU + 128
C_SEL = C_CMP + QT * 32
C_ONE = C_SEL + 4 * 128
C_ALL = C_ONE + 128

V_MPRE, V_MPOST, V_FPRE, V_FPOST = 0, 16, 32, 48
V_BIN, V_BDW, V_LNG, V_LNB, V_BOUT = 64, 80, 88, 96, 104
V_ALL = 112


class Link:

    def __init__(self, eng, chain):
        self.eng, self.chain, self.count, self.var, self.per = eng, chain, {}, None, {}

    def loop(self, var, **per):
        self.var, self.per, self.start = var, per, dict(self.count)

    def end(self, trips):
        for s, n in self.count.items():
            p = n - self.start.get(s, 0)
            assert p == self.per.get(s.name, 0), (s.name, p)
            self.count[s] = self.start.get(s, 0) + p * trips
        self.var = None

    def need(self, n):
        self.eng.wait_ge(self.chain, n if self.var is None else self.var * self.per[self.chain.name] + n)

    def last(self):
        return self.count.get(self.chain, 0)

    def __call__(self, ins, s=None, wait=True):
        s = self.chain if s is None else s
        self.count[s] = self.count.get(s, 0) + 1
        ins.then_inc(s, 1)
        if wait:
            n = self.count[s]
            self.eng.wait_ge(s, n if self.var is None else self.var * self.per[s.name] + n)


def trunk(nc, a, o):
    ctx = ExitStack()
    with ctx:
        top = [(nc.sbuf_base + 63) // 64 * 64]

        def at(name, shape, dt, offset):
            return nc.alloc_sbuf_tensor_at(name, shape, dt, offset=offset)

        def size(shape, dt=F32):
            n = 2 if dt == BF16 else 4
            for s in shape[1:]:
                n *= s
            return (n + 31) // 32 * 32

        def sb(name, shape, dt=F32):
            t = at(name, shape, dt, top[0])
            top[0] += size(shape, dt)
            return t

        def over(start, *wanted):
            out = []
            for name, shape, dt in wanted:
                out.append(at(name, shape, dt, start))
                start += size(shape, dt)
            return out, start

        def sem(name):
            return ctx.enter_context(nc.semaphore(name))

        raw_at = top[0]
        RAW = [sb(f"w_raw{i}", [P, SLAB]) for i in range(2)]
        wh_at = top[0]
        WH = [sb(f"w_hi{i}", [P, SLAB], F32R) for i in range(2)]
        wl_at = top[0]
        WL = [sb(f"w_lo{i}", [P, SLAB], F32R) for i in range(2)]
        R = sb("resid", [P, NC, T])
        x_at = top[0]
        XH = sb("x_hi", [P, NC, T], F32R)
        XL = sb("x_lo", [P, NC, T], F32R)
        h_at = top[0]
        HH = sb("hid_hi", [P, NC, T], F32R)
        HL = sb("hid_lo", [P, NC, T], F32R)
        f_at = top[0]
        F = sb("sub_out", [P, NC, T])
        g_at = top[0]
        G = sb("ple_proj", [P, NC, T])
        end_at = top[0]
        t_at = top[0]
        TMP = [sb(f"tmp{i}", [P, T]) for i in range(4)]
        RS = sb("rstd", [P, T])
        QV = sb("inv_var", [P, T])
        CST = sb("consts", [P, C_ALL])
        VEC = sb("vecs", [P, V_ALL])
        WDW = sb("w_dw", [P, NC, 32])
        p_at = top[0]
        PH = sb("ple_hi", [P, 2, T], F32R)
        PL = sb("ple_lo", [P, 2, T], F32R)
        IDB = sb("ident_bf", [P, P], BF16)
        CAUB = sb("causal_bf", [P, P], BF16)
        CMPB = sb("cmpmask_bf", [P, QT * 32], BF16)
        NMB = sb("newmask_bf", [P, 4 * 32], BF16)
        CMSB = sb("cmpmask_s_bf", [P, 32], BF16)
        SS5 = sb("rowstat", [P, 8])

        ID = CST[:, C_ID:C_ID + P]
        ONE = CST[:, C_ONE:C_ONE + P]

        (XTOK, STT, WDT, VROW), e = over(f_at, ("x_tok", [P, NTT, D], F32), ("state_tok", [120, 2, D], F32),
                                         ("wdw_rows", [CW, D], F32), ("vec_rows", [V_ALL, P], F32))
        assert e <= end_at, (e, end_at)
        (XIN,), e = over(h_at, ("conv_in", [P, NC, XC], F32))
        assert e <= f_at
        (PTOK,), e = over(g_at, ("ple_tok", [P, NTT, PLE], F32))
        (CST_OUT, DG), e = over(e, ("conv_state_rows", [32, 2, D], F32), ("tap_diag", [P, 5, P], F32))
        assert e <= end_at
        (KT,), xt_at = over(x_at, ("k_T", [HD, 2, KG, SEQ], F32))
        (XTH, XTL), e = over(xt_at, ("pairT_hi", [P, 8, XTC], F32R), ("pairT_lo", [P, 8, XTC], F32R))
        (STG,), e2 = over(raw_at, ("pair_stage", [P, DB, KG, P], F32))
        assert e2 <= raw_at + 2 * SLAB * 4
        kv_at = max(e, h_at + 2560)
        (KV, QC, QR), e = over(kv_at, ("kv_tok", [P, 6, NTT, 256], F32), ("qT", [P, NC, T], F32),
                               ("qT_rot", [P, NC, T], F32))
        assert e <= end_at, (e, end_at)
        (QBC, QBR), e = over(p_at, ("q_bd_cmp", [P, DB, 2, 32], F32), ("q_bd_rot", [P, DB, 2, 32], F32))
        (PCP,), e = over(p_at, ("pair_prompt", [P, 2, KG, P], F32))
        (HID,), e = over(e, ("cmp_hid", [P, 256], F32))
        (CKP, CKS, CVP), e = over(e, ("ckT_p", [HD, KG, 32], F32), ("ckT_s", [P, 2, P], F32),
                                  ("cv_p", [32, 256], F32))
        assert e <= p_at + 8704, (e - p_at)
        CVS = sb("cv_s", [32, 4, 256])
        GT = sb("gates_tok", [P, NTT, 48])
        GROW = sb("gates_row", [P, 4, 3])
        KNS = sb("k_newT", [P, 2, 2, 32])
        WC2 = sb("wc2", [P, 2, HD])
        PEB = sb("pe_bias", [P, 2])
        SM = sb("soft_small", [P, 2, 16])
        PGT = sb("page_table", [1, DB * NPAGE], I32)
        limit = nc.sbuf_base + nc.sbuf_bytes_remaining
        assert top[0] <= limit, (top[0], limit)
        (WG, WGH, WGL), e = over(t_at, ("wg", [P, NC, 48], F32), ("wg_hi", [P, NC, 48], F32R), ("wg_lo", [P, NC, 48], F32R))
        (BGR, PER), e = over(e, ("bg_row", [1, 48], F32), ("pe_rows", [16, 2, P], F32))
        assert e <= t_at + 4 * 2176
        (ROT1, ROT2), _ = over(xt_at, ("rope_a", [P, NTT, KG, 32], F32), ("rope_b", [P, NTT, KG, 32], F32))
        (PEH, PEL), e = over(e, ("pe_hi", [P, 16, 2], F32R), ("pe_lo", [P, 16, 2], F32R))
        assert e <= t_at + 4 * 2176
        (JNK,), e = over(t_at, ("junk", [P, D], F32))
        CACHED = []
        for i, start in enumerate((raw_at, xt_at)):
            kv_, e = over(start, *[(f"{n}{i}", [P, 2, 2, 256], F32) for n in ("ks_n", "vs_n", "kw_n", "vw_n")])
            CACHED.append(kv_)
        (OTS, OS), e = over(e, ("o_sT", [P, 4, P], F32), ("o_s", [P, P], F32))
        assert e <= kv_at, (e, kv_at)
        (KTB, PTA), e = over(t_at, ("k_bT", [P, 2, 2, 256], F32), ("p_sT", [P, 4, P], F32))
        (PS_, PTB), e = over(e, ("p_s", [P, 2, 288], F32), ("p_newT", [32, 3, P], F32))
        (PC_, GRT), e = over(e, ("p_cmp", [P, 32], F32), ("gates_row_tmp", [P, 4, 48], F32))
        assert e <= t_at + 6 * 2176, e
        (PP, PT, QS, QF), e = over(xt_at, ("p", [P, 2, 2, 512], F32), ("pT", [P, 2, 512], F32),
                               ("q_stage", [HD, 2, SEQ], F32), ("q_chunk", [P, SEQ], F32))
        assert e <= kv_at, (e, kv_at)
        (KA, QA), e2 = over(wh_at, ("k_hi_twice", [P, 2, SEQ], F32R), ("q_hi_lo", [P, 2, SEQ], F32R))
        (KB,), e3 = over(wl_at, ("k_lo_twice", [P, 2, SEQ], F32R))
        assert e2 <= wh_at + SLAB * 4 and e3 <= wl_at + SLAB * 4
        (ON,), _ = over(p_at, ("o_tok", [P, 2, QT, P], F32))
        (PCT, PPC, OM, SMC, SMP), e = over(t_at, ("p_cT", [32, 2, 8, P], F32), ("p_c", [P, 8, 32], F32),
                                      ("o_sum", [P, 2, HD], F32), ("soft_cmp", [P, 4, 8], F32), ("soft_small_p", [P, 4, 8], F32))
        assert e <= t_at + 6 * 2176
        (YTOK,), e = over(f_at, ("y_tok", [P, NTT, D], F32))

        PS = ctx.enter_context(nc.psum_tensor("ps", [P, 8, 512], F32))

        w_raw = [sem(f"w_raw_in{i}") for i in range(2)]
        w_hi = sem("w_hi")
        w_lo = sem("w_lo")
        blk_full = sem("blk_full")
        blk_free = sem("blk_free")
        x_ready = sem("x_ready")
        phase = sem("phase")
        stores = sem("stores")
        stores_pool = sem("stores_pool")
        chain = {e: sem(f"{e}_chain") for e in ("pe", "act", "dve", "pool")}
        S = {n: sem(n) for n in (
            "ld_const", "ld_x", "ld_vec", "ld_state", "ld_p",
            "row_sq", "row_rstd", "bank_full", "bank_free", "x_scaled", "masks",
            "xs_hi", "y_full", "glu_used", "conv_done",
            "sq_ready", "sq_used", "var_ready", "std_ready", "stat_ready", "stat_used", "r_ready", "xh_ready",
            "rsq_ready", "rsq_used", "rsum_ready",
            "hid_sq", "hid_hi", "h_ready", "mean_ready", "silu_ready",
            "diag_ready", "diag_used", "tap_full", "tap_used", "cs_rows", "y_rows", "ple_full", "ple_lo", "ple_hi",
            "xn_ready", "ld_gate", "ld_wc", "kv_zero", "wg_hi", "wg_lo", "gates_full", "pe_full", "pe_hi",
            "rot_full", "rot_used", "kt_full", "kt_used", "xt_zero", "xt_full", "xt_hi", "xt_used", "ld_pair",
            "peb_full", "cmp_full", "hid_ready", "cmp2_full", "cmp2_used",
            "grow_full", "qbd_ready", "kb_full", "ktb_a", "ktb_d", "s_qk", "s_max", "s_exp", "s_scaled",
            "s_pt", "pta", "ptb", "s_o", "os_ready", "s_ot", "ots_ready",
            "qs_c", "q_chunk", "q_high", "q_pair", "k_twice", "k_low", "p_qk", "p_max", "p_exp", "p_pv", "p_grp", "grp_dve", "grp_act",
            "o_used", "c_exp", "c_scaled")}
        ld_stg = [sem(f"ld_pairs{b}") for b in range(DB)]
        ld_att = [sem(f"ld_cached{i}") for i in range(2)]
        block = ctx.enter_context(nc.Block())

        def cols(w):
            v = w.rearrange("(h k p) n -> p h k n", p=P, h=2)
            return lambda i, h: v[:, h, :, ds(i * NSLABCOL, NSLABCOL)]

        def glu_cols(w):
            v = w.rearrange("(k p) (h n) -> p h k n", p=P, h=2)
            return lambda i, h: v[:, h, :, ds(i * P, P)]

        def whole(w, k):
            v = w.rearrange("(h k p) n -> p h k n", p=P, h=2)
            return lambda i, h: v[:, h, :, :]

        STAGES = [(glu_cols(a["conv_w_in"][0]), 8), (cols(a["conv_w_out"][0]), 4)]

        def ffn_stages(l):
            out = []
            for q in range(FF // D):
                out.append((cols(a["ffn_w_in"][l, :, q * D:(q + 1) * D]), 4))
                out.append((cols(a["ffn_w_out"][l, q * D:(q + 1) * D, :]), 4))
            out.append((whole(a["ple_w_proj"][l], 1), 1))
            out.append((cols(a["ple_w_gate"][l]), 4))
            return out

        STAGES += ffn_stages(0)
        STAGES.append((cols(a["nsa_w_in"][0]), 10))
        STAGES.append((whole(a["nsa_wk_c1"][0], 8), 1))
        STAGES.append((whole(a["nsa_wv_c1"][0], 8), 1))
        STAGES.append((cols(a["nsa_w_o"][0]), 4))
        STAGES += ffn_stages(1)
        S_CONV, S_CONVO, S_FFN0, S_NSA = 0, 8, 12, 49
        S_CMP, S_WO, S_FFN1 = 59, 61, 65
        N_SLABS = sum(n for _, n in STAGES)

        FFN_B = 4 * 16 + 8 + 8
        B_CONV, B_CONVO, B_FFN0 = 2, 18, 26
        B_Q = B_FFN0 + FFN_B
        B_KV = B_Q + 8
        B_WO = B_KV + 6 * NTT
        B_FFN1 = B_WO + 8

        def end_phase(eng, k):
            eng.drain().then_inc(phase, 1)
            eng.wait_ge(phase, 4 * k)

        def split_hi(act, s, par, half, before):
            act.wait_ge(w_raw[par], half * 32 + 32)
            act.wait_ge(blk_full, before)
            act.activation(WH[par][:, :], RAW[par][:, :], ACT.Copy).then_inc(w_hi, 1)

        def split_lo(dve, s, par):
            dve.wait_ge(w_hi, s + 1)
            dve.tensor_tensor(WL[par][:, :], RAW[par][:, :], WH[par][:, :].bitcast(F32), ALU.subtract)\
               .then_inc(w_lo, 1)

        def blk(par):
            return PS[:, 2 * par:2 * par + 2, 0:HT]

        def two(t):
            return t.rearrange("p (h n) -> p h n", h=2)

        def three_products(pe, out, k, first, last, wcols, xh, xl, par, xcols):
            m = None
            for w, x, f, l in ((WH, xh, first, False), (WH, xl, False, False), (WL, xh, False, last)):
                for o_, c_ in zip(out, xcols):
                    m = pe.matmul(o_, w[par][:, wcols:wcols + P], x[:, k, c_], start=f, stop=l)
            return m

        HALVES = (slice(0, HT), slice(HT, T))

        def pe_block(pe, par, bpar, b, s, mb, xh, xl, ready, x0, nk=NC, width=NSLABCOL,
                     mb_step=P):
            pe.wait_ge(blk_free, b - 1)
            if mb == 0:
                pe.wait_ge(w_lo, s + 1)
            for k in range(nk):
                if ready is not None:
                    pe.wait_ge(ready, x0 + k + 1)
                m = three_products(pe, [PS[:, 2 * bpar + h, 0:HT] for h in range(2)], k, k == 0, k == nk - 1,
                                   k * width + mb * mb_step, xh, xl, par, HALVES)
            m.then_inc(blk_full, 1)

        def pe_linear(pe, n, s0, b0, ready=None, x0=0, **slab):
            with pe.Fori(0, n // 2) as i:
                for h in range(2):
                    for mb in range(2):
                        pe_block(pe, (s0 + h) % 2, mb, i * 4 + (b0 + 2 * h + mb), i * 2 + (s0 + h), mb,
                                 XH, XL, ready, x0, **slab)

        N_DG = 5
        assert PE_TAPS % N_DG == 0

        def taps_pe(pe, i):
            for h in range(2):
                pe.wait_ge(S["glu_used"], i * 2 + (h + 3))
                pe.wait_ge(S["tap_used"], i * 2 + (h + 1))
                xin = XIN[:, ds(i * 2 + h, 1), :].rearrange("p o n -> p (o n)")
                for j in range(PE_TAPS):
                    pe.wait_ge(S["diag_ready"], i * (2 * PE_TAPS) + (h * PE_TAPS + j + 1))
                    dg = DG[:, j % N_DG, :]
                    f, l = j == 0, j == PE_TAPS - 1
                    pe.matmul(PS[:, 4 + 2 * h, :], dg, xin[:, j:j + SEQ], start=f, stop=l)
                    pe.matmul(PS[:, 5 + 2 * h, 0:NS], dg,
                              xin[:, XP + j * DB:XP + j * DB + NS].rearrange("p (t b) -> p b t", b=DB), start=f, stop=l)\
                        .then_inc(S["diag_used"], 1)
                pe.drain().then_inc(S["tap_full"], 1)

        def diags_act(act, i):
            for h in range(2):
                for j in range(PE_TAPS):
                    act.wait_ge(S["diag_used"], i * (2 * PE_TAPS) + (h * PE_TAPS + j + 1))
                    act.activation(DG[:, j % N_DG, :], ID, ACT.Copy,
                                   scale=WDW[:, ds(i * 2 + h, 1), j:j + 1].rearrange("p o n -> p (o n)")).then_inc(S["diag_ready"], 1)

        def act_split_ahead(act, i, s0, b0, h, per=2):
            s = s0 + h + 1
            split_hi(act, i * 2 + s, s % 2, i + s // 2, i * (2 * per) + (b0 + per * h))

        def dve_split_ahead(dve, i, s0, h):
            split_lo(dve, i * 2 + (s0 + h + 1), (s0 + h + 1) % 2)

        def loop_pairs(eng, n, body, last=False):
            with eng.Fori(0, n // 2 - (1 if last else 0)) as i:
                body(i, False)
            if last:
                body(n // 2 - 1, True)

        STAT = PS[:, 4:6, 0:HT]

        def stat_act(act, L, src, n):
            for c in range(NC):
                if 8 * n + c >= 2:
                    act.wait_ge(S["sq_used"], 8 * n + c - 1)
                L(act.activation(TMP[c % 2][:, :], src[:, c, :], ACT.Square), S["sq_ready"], wait=False)

        def pe_ones(pe, src, first, last):
            for h, c in enumerate(HALVES):
                m = pe.matmul(PS[:, 4 + h, 0:HT], ONE, src[:, c], start=first, stop=last)
            return m

        def stat_pe(pe, n, m):
            if m:
                pe.wait_ge(S["stat_used"], m)
            for c in range(NC):
                pe.wait_ge(S["sq_ready"], 8 * n + c + 1)
                pe_ones(pe, TMP[c % 2], c == 0, c == NC - 1).then_inc(S["sq_used"], 1)

        def std_act(act, L, s, n):
            act.wait_ge(s, n)
            L(act.activation(TMP[3][:, :], TMP[2][:, :], ACT.Sqrt), S["std_ready"])

        def rstd_dve(dve, L, nsq, nstd, deferred=False):
            dve.wait_ge(S["sq_used"], 8 * (nsq + 1))
            if deferred:
                L(dve.scalar_tensor_tensor(two(TMP[2][:, :]), STAT, 1.0 / D, two(QV[:, :]), ALU.mult, ALU.mult),
                  S["stat_used"])
                L(dve.tensor_tensor(TMP[2][:, :], TMP[2][:, :], QV[:, :], ALU.mult))
                L(dve.tensor_scalar(TMP[2][:, :], TMP[2][:, :], EPS, None, ALU.add), S["var_ready"])
            else:
                L(dve.tensor_scalar(two(TMP[2][:, :]), STAT, 1.0 / D, EPS, ALU.mult, ALU.add), S["stat_used"])
            dve.wait_ge(S["std_ready"], nstd + 1)
            L(dve.reciprocal(RS[:, :], TMP[3][:, :]))
            if deferred:
                L(dve.tensor_tensor(RS[:, :], RS[:, :], QV[:, :], ALU.mult))

        def vec(row):
            return VEC[:, row:row + 1]

        def residual_dve(dve, L, gpost, gnext, nr, nx):
            def low(c):
                dve.wait_ge(S["r_ready"], 8 * nr + c + 1)
                dve.wait_ge(S["xh_ready"], 8 * nx + c + 1)
                if gnext is None:
                    L(dve.tensor_tensor(XL[:, c, :], R[:, c, :], XH[:, c, :].bitcast(F32), ALU.subtract), x_ready, wait=False)
                else:
                    L(dve.scalar_tensor_tensor(XL[:, c, :], R[:, c, :], vec(gnext + c), XH[:, c, :].bitcast(F32),
                                               ALU.mult, ALU.subtract), x_ready, wait=False)
            scaled = {}
            for c in range(NC + 2):
                if c < NC:
                    if c >= 2:
                        dve.wait_ge(S["r_ready"], 8 * nr + c - 1)
                    L(dve.scalar_tensor_tensor(TMP[2 + c % 2][:, :], F[:, c, :], vec(gpost + c), RS[:, :], ALU.mult, ALU.mult),
                      wait=False)
                    scaled[c] = L.last()
                if 1 <= c <= NC:
                    L.need(scaled[c - 1])
                    L(dve.tensor_tensor(R[:, c - 1, :], R[:, c - 1, :], TMP[2 + (c - 1) % 2][:, :], ALU.add), S["r_ready"],
                      wait=False)
                if c >= 2:
                    low(c - 2)

        def residual_act(act, L, gnext, nr, nx, squares, nq=0):
            for c in range(NC):
                act.wait_ge(S["r_ready"], 8 * nr + c + 1)
                if gnext is None:
                    L(act.activation(XH[:, c, :], R[:, c, :], ACT.Copy), S["xh_ready"], wait=False)
                else:
                    L(act.activation(XH[:, c, :], R[:, c, :], ACT.Copy, scale=vec(gnext + c)), S["xh_ready"], wait=False)
                if squares:
                    if c >= 2:
                        act.wait_ge(S["rsq_used"], 8 * nq + c - 1)
                    L(act.activation(TMP[c % 2][:, :], R[:, c, :], ACT.Square), S["rsq_ready"], wait=False)

        def residual_pool(pool, L, nq):
            for c in range(NC):
                pool.wait_ge(S["rsq_ready"], 8 * nq + c + 1)
                if c == 0:
                    L(pool.tensor_copy(QV[:, :], TMP[0][:, :]), S["rsq_used"])
                else:
                    L(pool.tensor_tensor(QV[:, :], QV[:, :], TMP[c % 2][:, :], ALU.add), S["rsq_used"])

        def ffn_pe(pe, l, s0, b0, nx, nsq, m):
            with pe.Fori(0, 4) as q:
                for j in range(4):
                    for mb in range(2):
                        pe_block(pe, (s0 + j) % 2, mb, q * 16 + (b0 + 2 * j + mb), q * 8 + (s0 + j), mb,
                                 XH, XL, x_ready, 8 * nx)
                for j in range(4):
                    for mb in range(2):
                        pe_block(pe, (s0 + 4 + j) % 2, mb, q * 16 + (b0 + 8 + 2 * j + mb), q * 8 + (s0 + 4 + j), mb,
                                 HH, HL, S["h_ready"], q * 8 + 32 * l)
            pe.wait_ge(S["rsq_used"], 8 * (l + 1))
            pe.wait_ge(S["stat_used"], m)
            pe_ones(pe, QV, True, True).then_inc(S["rsum_ready"], 1)
            stat_pe(pe, nsq, m + 1)
            pe.wait_ge(S["ld_p"], 32 * (l + 1))
            for c in range(2):
                for t in range(QT):
                    m_ = pe.transpose(PS[:, 6 + c, t * P:(t + 1) * P], PTOK[:, t, c * P:(c + 1) * P], ID)
            m_.then_inc(S["ple_full"], 1)
            pe.wait_ge(S["ple_lo"], 3 * l + 1)
            for c in range(2):
                m_ = pe.transpose(PS[:, 6, c * NS:(c + 1) * NS], PTOK[0:NS, QT, c * P:(c + 1) * P], ID[0:NS, 0:NS])
            m_.then_inc(S["ple_full"], 1)
            pe.wait_ge(S["ple_lo"], 3 * (l + 1))
            s, b = s0 + 32, b0 + 64
            for mb in range(NC):
                pe_block(pe, s % 2, mb % 2, b + mb, s, mb, PH, PL, None, 0, nk=2, width=D)
            pe_linear(pe, 4, s + 1, b + 8, x_ready, 8 * (nx + 1))

        PLE_S = PS[:, 6, 0:2 * NS].rearrange("p (c n) -> p c n", c=2)

        def ffn_act(act, L, l, s0, b0, nx, nr, nsq, nstd, last):
            h0 = 32 * l
            act.wait_ge(S["rsq_used"], 8 * (l + 1))
            with act.Fori(0, 4) as q:
                L.loop(q, hid_hi=8)
                for j in range(8):
                    s = s0 + j + 1
                    split_hi(act, q * 8 + s, s % 2, q * 4 + s // 2, q * 16 + (b0 + 2 * j))
                    if j < 4:
                        for mb in range(2):
                            c = 2 * j + mb
                            if c == 0:
                                act.wait_ge(blk_free, q * 16 + b0)
                            act.wait_ge(blk_full, q * 16 + (b0 + c + 1))
                            if c >= 2:
                                act.wait_ge(S["hid_sq"], q * 8 + (h0 + c - 1))
                            act.activation(two(TMP[mb][:, :]), blk(mb), ACT.Relu).then_inc(blk_free, 1)
                            act.wait_ge(S["hid_sq"], q * 8 + (h0 + c + 1))
                            L(act.activation(HH[:, c, :], TMP[2 + mb][:, :], ACT.Copy), S["hid_hi"], wait=False)
            L.end(4)
            stat_act(act, L, F, nsq)
            std_act(act, L, S["var_ready"], l + 1)
            act.wait_ge(S["ple_full"], 2 * l + 1)
            for c in range(2):
                L(act.activation(PH[:, c, 0:SEQ], PS[:, 6 + c, :], ACT.Copy), S["ple_hi"])
            act.wait_ge(S["ple_full"], 2 * l + 2)
            L(act.activation(PH[:, :, SEQ:T], PLE_S, ACT.Copy), S["ple_hi"])
            residual_act(act, L, None, nr, nx + 1, False)
            s, b = s0 + 32, b0 + 64
            split_hi(act, s + 1, (s + 1) % 2, (s + 1) // 2, b)
            act.wait_ge(blk_free, b + 8)
            def gate(i, final):
                for h in range(2):
                    if not (final and h == 1):
                        act_split_ahead(act, i, s + 1, b + 8, h)
                    for mb in range(2):
                        act.wait_ge(blk_full, i * 4 + (b + 8 + 2 * h + mb + 1))
                        act.wait_ge(S["r_ready"], i * 4 + (8 * (nr + 1) + 2 * h + mb - 1))
                        act.activation(two(TMP[mb][:, :]), blk(mb), ACT.Sigmoid).then_inc(blk_free, 1)
            loop_pairs(act, 4, gate, last)

        def ffn_dve(dve, L, l, s0, b0, nx, nr, gpost, nsq, nstd, last):
            h0 = 32 * l
            L(dve.memset(F[:, :, :], 0.0))
            with dve.Fori(0, 4) as q:
                L.loop(q, hid_sq=8, h_ready=8, blk_free=16)
                L.count[blk_free] = b0
                L.start[blk_free] = b0
                for j in range(8):
                    split_lo(dve, q * 8 + (s0 + j + 1), (s0 + j + 1) % 2)
                    for mb in range(2):
                        c = 2 * (j % 4) + mb
                        if j < 4:
                            L.count[blk_free] += 1
                            dve.wait_ge(blk_free, q * 16 + (b0 + c + 1))
                            L(dve.tensor_tensor(TMP[2 + mb][:, :], TMP[mb][:, :], TMP[mb][:, :], ALU.mult), S["hid_sq"])
                            dve.wait_ge(S["hid_hi"], q * 8 + (h0 + c + 1))
                            L(dve.tensor_tensor(HL[:, c, :], TMP[2 + mb][:, :], HH[:, c, :].bitcast(F32), ALU.subtract),
                              S["h_ready"])
                        else:
                            dve.wait_ge(blk_full, q * 16 + (b0 + 8 + c + 1))
                            L(dve.tensor_tensor(two(F[:, c, :]), blk(mb), two(F[:, c, :]), ALU.add), blk_free)
            L.end(4)
            dve.wait_ge(S["rsum_ready"], l + 1)
            L(dve.tensor_scalar(two(TMP[2][:, :]), STAT, 1.0 / D, EPS, ALU.mult, ALU.add), S["stat_used"])
            L(dve.reciprocal(QV[:, :], TMP[2][:, :]))
            rstd_dve(dve, L, nsq, nstd, deferred=True)
            for c in range(2):
                dve.wait_ge(S["ple_hi"], 3 * l + c + 1)
                L(dve.tensor_tensor(PL[:, c, 0:SEQ], PS[:, 6 + c, :], PH[:, c, 0:SEQ].bitcast(F32), ALU.subtract), S["ple_lo"])
            dve.wait_ge(S["ple_hi"], 3 * l + 3)
            L(dve.tensor_tensor(PL[:, :, SEQ:T], PLE_S, PH[:, :, SEQ:T].bitcast(F32), ALU.subtract), S["ple_lo"])
            residual_dve(dve, L, gpost, None, nr, nx + 1)
            s, b = s0 + 32, b0 + 64
            split_lo(dve, s + 1, (s + 1) % 2)
            dve.wait_ge(stores_pool, 16 * conv_states_n)
            for mb in range(NC):
                dve.wait_ge(blk_full, b + mb + 1)
                L.count[blk_free] = b + mb
                L(dve.tensor_copy(two(G[:, mb, :]), blk(mb % 2)), blk_free)
            def gate(i, final):
                for h in range(2):
                    if not (final and h == 1):
                        dve_split_ahead(dve, i, s + 1, h)
                    for mb in range(2):
                        c = i * 4 + (2 * h + mb)
                        dve.wait_ge(blk_free, i * 4 + (b + 8 + 2 * h + mb + 1))
                        L(dve.tensor_tensor(TMP[2 + mb][:, :], TMP[mb][:, :], G[:, ds(c, 1), :].rearrange("p o n -> p (o n)"), ALU.mult))
                        rc = R[:, ds(c, 1), :].rearrange("p o n -> p (o n)")
                        L(dve.tensor_tensor(rc, rc, TMP[2 + mb][:, :], ALU.add), S["r_ready"])
            if last:
                L.count[blk_free] = 0
                gate(0, False)
                gate(1, True)
            else:
                with dve.Fori(0, 2) as i:
                    L.loop(i, dve_chain=4, r_ready=4)
                    gate(i, False)
                L.end(2)

        conv_states_n = 2 + DT + 2

        def load_p(pool, l):
            pool.dma_start(PTOK[:, 0:QT, :], a["p_prompt"][l, 0].rearrange("(t p) d -> p t d", p=P)).then_inc(S["ld_p"], 16)
            pool.dma_start(PTOK[0:NS, QT, :], a["p_sample"][l].rearrange("b t d -> (b t) d")).then_inc(S["ld_p"], 16)

        def conv_states(pool):
            pool.dma_start(o["conv_state_s"][0, :, 0:CW - 1 - DT, :], a["state_conv"][0, :, DT:CW - 1, :]).then_inc(stores_pool, 16)
            pool.wait_ge(S["cs_rows"], 4)
            pool.dma_start(o["conv_state_p"][0, 0], CST_OUT[0:CW - 1, 0, :]).then_inc(stores_pool, 16)
            for t in range(DT):
                pool.dma_start(o["conv_state_s"][0, :, CW - 1 - DT + t, :], CST_OUT[t * DB:(t + 1) * DB, 1, :]).then_inc(stores_pool, 16)
            for n_ in ("k_win", "v_win"):
                pool.dma_start(o[n_ + "_s"][0, :, 0:PAST].rearrange("b l g d -> b (l g d)"),
                             a["state_" + n_][0].rearrange("b l g d -> b (l g d)")).then_inc(stores_pool, 16)

        N_KV_ST = 6 + 4 + 2 * DB

        def rows_of(tt):
            return P if tt < QT else NS

        def page_load(sp, dst, cache, b, pg, view):
            r = sp.value_load(PGT[0:1, b * NPAGE + pg:b * NPAGE + pg + 1], min_val=0, max_val=NPOOL - 1)
            return sp.dma_start(dst, view(a[cache][0, ds(r, 1)]))

        def nsa_pair_loads(sp, kv):
            for b in range(DB):
                if kv:
                    sp.wait_ge(S["xt_full"], 5 + b // 2)
                for pg in range(NPAGE):
                    for r in range(2):
                        page_load(sp, STG[pg * 64:(pg + 1) * 64, b, :, r * HD:(r + 1) * HD], ("cache_k_cmp", "cache_v_cmp")[kv],
                                  b, pg, lambda v: v.rearrange("o (q r) g d -> (o q) r g d", r=2)[:, r, :, :])\
                            .then_inc(ld_stg[b], 16)

        def nsa_kv_stores(sp):
            names = ("k_cmp", "v_cmp", "k_sel", "v_sel", "k_win", "v_win")
            for s, n in enumerate(names):
                sp.dma_start(o[n + "_p"][0, 0].rearrange("(t p) g d -> p t (g d)", p=P), KV[:, s, 0:QT, :]).then_inc(stores, 16)
                if s < 4:
                    sp.dma_start(o[n + "_s"][0].rearrange("b t g d -> (b t) (g d)"), KV[0:NS, s, QT, :]).then_inc(stores, 16)
                else:
                    for b in range(DB):
                        sp.dma_start(o[n + "_s"][0, b, PAST:PAST + DT].rearrange("t g d -> t (g d)"),
                                     KV[b * DT:(b + 1) * DT, s, QT, :]).then_inc(stores, 16)

        def nsa_sample_loads(sp, t):
            KSN, VSN, KWN, VWN = CACHED[t % 2]
            for bb in range(2):
                b = 2 * t + bb
                for dst, cache in ((KSN, "cache_k_sel"), (VSN, "cache_v_sel")):
                    for pg in range(NPAGE):
                        page_load(sp, dst[:, bb, pg, :], cache, b, pg, lambda v: v.rearrange("o q g d -> (o q) (g d)"))\
                            .then_inc(ld_att[t % 2], 16)
                for dst, n in ((KWN, "state_k_win"), (VWN, "state_v_win")):
                    sp.dma_start(dst[:, bb, :, :], a[n][0, b].rearrange("(h p) g d -> p h (g d)", p=P)).then_inc(ld_att[t % 2], 16)
        N_ATT_LD = 16 * 2 * (2 * NPAGE + 2)

        SK = S_NSA + 4

        def proj_pe(pe):
            stat_pe(pe, 3, 5)
            pe_linear(pe, 4, S_NSA, B_Q, x_ready, 8 * 4)
            with pe.Fori(0, 3) as i:
                for h in range(2):
                    par = (SK + h) % 2
                    for tt in range(NTT):
                        n = NTT * h + tt
                        pe.wait_ge(blk_free, i * (2 * NTT) + (B_KV + n - 1))
                        if tt == 0:
                            pe.wait_ge(w_lo, i * 2 + (SK + h + 1))
                        out = PS[0:rows_of(tt), 2 * (n % 2), 0:256]
                        for k in range(NC):
                            tok = slice(tt * P, tt * P + rows_of(tt))
                            w = slice(k * 256, (k + 1) * 256)
                            pe.matmul(out, XH[:, k, tok], WH[par][:, w], start=k == 0, stop=False)
                            pe.matmul(out, XL[:, k, tok], WH[par][:, w], start=False, stop=False)
                            m = pe.matmul(out, XH[:, k, tok], WL[par][:, w], start=False, stop=k == NC - 1)
                        m.then_inc(blk_full, 1)
            pe.wait_ge(S["wg_lo"], 1)
            for tt in range(NTT):
                out = PS[0:rows_of(tt), 4, tt * 48:(tt + 1) * 48]
                tok = slice(tt * P, tt * P + rows_of(tt))
                for k in range(NC):
                    pe.matmul(out, XH[:, k, tok], WGH[:, k, :], start=k == 0, stop=False)
                    pe.matmul(out, XL[:, k, tok], WGH[:, k, :], start=False, stop=False)
                    pe.matmul(out, XH[:, k, tok], WGL[:, k, :], start=False, stop=False)
                m = pe.matmul(out, ONE[0:1, 0:rows_of(tt)], BGR[0:1, :], start=False, stop=True)
            m.then_inc(S["gates_full"], 1)

        def proj_act(act, L):
            stat_act(act, L, R, 3)
            std_act(act, L, S["stat_used"], 6)
            for c in range(NC):
                act.wait_ge(S["xn_ready"], c + 1)
                L(act.activation(XH[:, c, :], F[:, c, :], ACT.Copy), S["xh_ready"])
            act.wait_ge(S["ld_gate"], 16 * 3)
            L(act.activation(WGH[:, :, :], WG[:, :, :], ACT.Copy), S["wg_hi"])
            with act.Fori(0, 2) as i:
                for h in range(2):
                    act_split_ahead(act, i, S_NSA, B_Q, h)
                    for mb in range(2):
                        act.wait_ge(blk_full, i * 4 + (B_Q + 2 * h + mb + 1))
                        act.activation(QC[:, ds(i * 4 + (2 * h + mb), 1), :].rearrange("p o (h n) -> p (o h) n", h=2),
                                       blk(mb), ACT.Copy, scale=SCALE).then_inc(blk_free, 1)
            act.wait_ge(S["kv_zero"], 1)
            with act.Fori(0, 3) as i:
                for h in range(2):
                    act_split_ahead(act, i, SK, B_KV, h, per=NTT)
                    for tt in range(NTT):
                        n = NTT * h + tt
                        act.wait_ge(blk_full, i * (2 * NTT) + (B_KV + n + 1))
                        act.activation(KV[0:rows_of(tt), ds(i * 2 + h, 1), tt, :].rearrange("p o n -> p (o n)"),
                                       PS[0:rows_of(tt), 2 * (n % 2), 0:256], ACT.Copy).then_inc(blk_free, 1)
            split_hi(act, S_CMP + 1, (S_CMP + 1) % 2, (S_CMP + 1) // 2, B_WO)
            act.wait_ge(S["gates_full"], 1)
            L(act.activation(GT[:, 0:QT, :], PS[:, 4, 0:QT * 48].rearrange("p (t n) -> p t n", t=QT), ACT.Sigmoid))
            L(act.activation(GT[0:NS, QT, :], PS[0:NS, 4, QT * 48:NTT * 48], ACT.Sigmoid))

        def proj_dve(dve, L):
            rstd_dve(dve, L, 3, 3)
            for c in range(NC + 1):
                if c < NC:
                    L(dve.scalar_tensor_tensor(F[:, c, :], R[:, c, :], vec(V_MPRE + NC + c), RS[:, :], ALU.mult, ALU.mult),
                      S["xn_ready"])
                if c:
                    dve.wait_ge(S["xh_ready"], 8 * 4 + c)
                    L(dve.tensor_tensor(XL[:, c - 1, :], F[:, c - 1, :], XH[:, c - 1, :].bitcast(F32), ALU.subtract), x_ready)
            dve.wait_ge(S["wg_hi"], 1)
            L(dve.tensor_tensor(WGL[:, :, :], WG[:, :, :], WGH[:, :, :].bitcast(F32), ALU.subtract), S["wg_lo"])
            with dve.Fori(0, 2) as i:
                for h in range(2):
                    dve_split_ahead(dve, i, S_NSA, h)
            with dve.Fori(0, 3) as i:
                for h in range(2):
                    dve_split_ahead(dve, i, SK, h)
            split_lo(dve, S_CMP + 1, (S_CMP + 1) % 2)

        def proj_pool(pool, L):
            L(pool.memset(GT[:, QT, :], 0.0))
            L(pool.memset(KV[:, :, QT, :], 0.0), S["kv_zero"])
            pool.wait_ge(x_ready, 8 * 5)
            pool.dma_start(WG[:, :, :], a["nsa_w_in"][0, :, 2560:2608].rearrange("(k p) n -> p k n", p=P)).then_inc(S["ld_gate"], 16)
            pool.dma_start(BGR[:, :], a["nsa_b_gate"]).then_inc(S["ld_gate"], 16)
            for kv, n in enumerate(("k", "v")):
                pool.dma_start(WC2[:, kv, :], a[f"nsa_w{n}_c2"][0]).then_inc(S["ld_wc"], 16)
                pool.dma_start(PER[:, kv, :], a[f"nsa_pe_{n}"][0].rearrange("(i r) d -> i (r d)", r=2)).then_inc(S["ld_wc"], 16)
            pool.dma_start(PGT[:, :], a["page_table"].rearrange("(o b) n -> o (b n)", o=1)).then_inc(S["ld_gate"], 16)

        def rope_pe(pe):
            pe.wait_ge(S["ld_wc"], 64)
            for kv in range(2):
                m = pe.transpose(PS[:, 0, kv * 16:(kv + 1) * 16], PER[:, kv, :], ID[0:16, 0:16])
            m.then_inc(S["pe_full"], 1)
            for c in range(NC):
                if c >= 2:
                    pe.wait_ge(S["rot_used"], c - 1)
                for h, cc in enumerate(HALVES):
                    m = pe.matmul(PS[:, 4 + 2 * (c % 2) + h, 0:HT], CST[:, C_ROT:C_ROT + P], QC[:, c, cc], start=True, stop=True)
                m.then_inc(S["rot_full"], 1)

        PEV = PS[:, 0, 0:32].rearrange("p (v i) -> p i v", v=2)

        def rope_act(act, L):
            act.wait_ge(S["pe_full"], 1)
            L(act.activation(PEH[:, :, :], PEV, ACT.Copy), S["pe_hi"])

        def rope_dve(dve, L):
            dve.wait_ge(S["pe_hi"], 1)
            L(dve.tensor_tensor(PEL[:, :, :], PEV, PEH[:, :, :].bitcast(F32), ALU.subtract))
            for c in range(NC):
                L(dve.tensor_tensor(RS[:, :], QC[:, c, :], CST[:, C_COS:C_COS + T], ALU.mult), wait=False)
                dve.wait_ge(S["rot_full"], c + 1)
                L(dve.tensor_tensor(two(QV[:, :]), PS[:, 4 + 2 * (c % 2):6 + 2 * (c % 2), 0:HT],
                                    two(CST[:, C_SIN:C_SIN + T]), ALU.mult), S["rot_used"])
                L(dve.tensor_tensor(QR[:, c, :], RS[:, :], QV[:, :], ALU.add))

        def rope_pool(pool, L):
            tab = [CST[:, c:c + NTT * 32].rearrange("p (t o d) -> p t o d", t=NTT, o=1).broadcast_to([P, NTT, KG, 32])
                   for c in (C_TC, C_TS)]
            for s in (2, 4):
                v = KV[:, s, :, :].rearrange("p t (g h d) -> p t g h d", g=KG, h=2)
                x1, x2 = v[:, :, :, 0, :], v[:, :, :, 1, :]
                L(pool.tensor_tensor(ROT1[:, :, :, :], x1, tab[1], ALU.mult))
                L(pool.tensor_tensor(ROT2[:, :, :, :], x2, tab[1], ALU.mult))
                L(pool.tensor_tensor(x1, x1, tab[0], ALU.mult))
                L(pool.tensor_tensor(x2, x2, tab[0], ALU.mult))
                L(pool.tensor_tensor(x1, x1, ROT2[:, :, :, :], ALU.subtract))
                L(pool.tensor_tensor(x2, x2, ROT1[:, :, :, :], ALU.add))

        N_KT = 9
        GROUPS = [(kv, g) for kv in range(2) for g in range(3)]

        def group_banks(g):
            return 4 if g < 2 else 2

        def cmp_pe(pe):
            for n in range(8):
                br, g = n // KG, n % KG
                if n >= 4:
                    pe.wait_ge(S["kt_used"], n - 3)
                for tt in range(QT):
                    m = pe.transpose(PS[0:HD, 4 + n % 4, tt * P:(tt + 1) * P], KV[:, 2 + 2 * br, tt, g * HD:(g + 1) * HD], ID)
                m.then_inc(S["kt_full"], 1)
            pe.wait_ge(S["kt_used"], 5)
            for br in range(2):
                for gp in range(2):
                    j = br * 2 + gp
                    m = pe.transpose(PS[:, 4, j * NS:(j + 1) * NS], KV[0:NS, 2 + 2 * br, QT, gp * P:(gp + 1) * P], ID[0:NS, 0:NS])
            m.then_inc(S["kt_full"], 1)
            def transposes(n):
                kv, g = GROUPS[n]
                tb = sum(group_banks(x[1]) for x in GROUPS[:n])
                for j in range(group_banks(g)):
                    if tb >= 4:
                        pe.wait_ge(S["xt_used"], tb - 3)
                    for t2 in range(2):
                        for g2 in range(2):
                            if g < 2:
                                pe.wait_ge(ld_stg[2 * j + t2], 64 * (kv + 1))
                                src = STG[:, 2 * j + t2, 2 * g + g2, :]
                            else:
                                pe.wait_ge(S["ld_pair"], 128 * (kv + 1))
                                src = PCP[:, t2, 2 * j + g2, :]
                            m = pe.transpose(PS[:, 4 + tb % 4, (g2 * 2 + t2) * P:(g2 * 2 + t2 + 1) * P], src, ID)
                    m.then_inc(S["xt_full"], 1)
                    tb += 1
                return tb

            pe.wait_ge(S["kt_used"], N_KT)
            done = transposes(0)
            for n, (kv, g) in enumerate(GROUPS):
                s = S_CMP + kv
                if g == 0:
                    pe.wait_ge(w_lo, s + 1)
                    for i in range(16):
                        for w, x in ((WH, PEH), (WH, PEL), (WL, PEH)):
                            m = pe.matmul(PS[:, 2, kv * 2:kv * 2 + 2], w[s % 2][:, i * P:(i + 1) * P], x[:, i, :],
                                          start=i == 0 and x is PEH and w is WH, stop=i == 15 and w is WL)
                    m.then_inc(S["peb_full"], 1)
                pe.wait_ge(S["xt_used"], done)
                if n >= 2:
                    pe.wait_ge(S["hid_ready"], n - 1)
                N = 256 if g < 2 else P
                for i in range(16):
                    sh = i // 8
                    for w, x in ((WH, XTH), (WH, XTL), (WL, XTH)):
                        m = pe.matmul(PS[:, n % 2, 0:N], w[s % 2][:, i * P:(i + 1) * P], x[:, i % 8, sh:sh + N],
                                      start=i == 0 and x is XTH and w is WH, stop=i == 15 and w is WL)
                m.then_inc(S["cmp_full"], 1)
                if n + 1 < len(GROUPS):
                    done = transposes(n + 1)
                pe.wait_ge(S["hid_ready"], n + 1)
                if n:
                    pe.wait_ge(S["cmp2_used"], n)
                if kv == 0 and g < 2:
                    for g2 in range(2):
                        m = pe.matmul(PS[g2 * HD:(g2 + 1) * HD, 3, 0:P], WC2[:, 0, :], HID[:, g2 * P:(g2 + 1) * P], start=True, stop=True)
                elif kv == 0:
                    m = pe.matmul(PS[0:HD, 3, 0:P], WC2[:, 0, :], HID[:, 0:P], start=True, stop=True)
                elif g < 2:
                    for t in range(4):
                        for g2 in range(2):
                            m = pe.matmul(PS[0:32, 3, t * P + g2 * HD:t * P + (g2 + 1) * HD],
                                          HID[:, g2 * P + t * 32:g2 * P + (t + 1) * 32], WC2[:, 1, :], start=True, stop=True)
                else:
                    for g_ in range(KG):
                        m = pe.matmul(PS[0:32, 3, g_ * HD:(g_ + 1) * HD], HID[:, g_ * 32:(g_ + 1) * 32], WC2[:, 1, :],
                                      start=True, stop=True)
                m.then_inc(S["cmp2_full"], 1)

        def xt_views(tb, g, j):
            ps = PS[:, 4 + tb % 4, :].rearrange("p (g c i) -> p g i c", g=2, i=8)
            step, base = (P, 32 * j) if g < 2 else (32, 64 * j)
            return ps, [t[:, :, base:base + step + 32].rearrange("p i c -> p i c") for t in (XTH, XTL)], step

        def xt_evac(eng, tb, g, j, lo):
            ps, (vh, vl), step = xt_views(tb, g, j)
            for g2 in range(2):
                c = slice(g2 * step, g2 * step + 32)
                yield ps[:, g2], vh[:, :, c], vl[:, :, c]

        def cmp_act(act, L):
            for n in range(8):
                act.wait_ge(S["kt_full"], n + 1)
                L(act.activation(KT[:, n // KG, n % KG, :], PS[0:HD, 4 + n % 4, :], ACT.Copy), S["kt_used"], wait=False)
            act.wait_ge(S["kt_full"], N_KT)
            L(act.activation(KNS[:, :, :, :], PS[:, 4, 0:P].rearrange("p (a b n) -> p a b n", a=2, b=2), ACT.Copy), S["kt_used"])
            tb = 0
            act.wait_ge(S["xt_zero"], 1)
            for n, (kv, g) in enumerate(GROUPS):
                if n:
                    act.wait_ge(S["cmp_full"], n)
                for j in range(group_banks(g)):
                    act.wait_ge(S["xt_full"], tb + 1)
                    for src, hi, lo in xt_evac(act, tb, g, j, False):
                        L(act.activation(hi, src, ACT.Copy), S["xt_hi"], wait=False)
                    tb += 1
                if g == 0:
                    act.wait_ge(S["peb_full"], kv + 1)
                    L(act.activation(PEB[:, kv:kv + 1], PS[:, 2, 3 * kv:3 * kv + 1], ACT.Copy))
                act.wait_ge(S["cmp_full"], n + 1)
                if n:
                    act.wait_ge(S["cmp2_full"], n)
                N = 256 if g < 2 else P
                L(act.activation(HID[:, 0:N], PS[:, n % 2, 0:N], ACT.Gelu_apprx_tanh, bias=PEB[:, kv:kv + 1]), S["hid_ready"])

        def cmp_dve(dve, L):
            tb = 0
            for n, (kv, g) in enumerate(GROUPS):
                for j in range(group_banks(g)):
                    dve.wait_ge(S["xt_hi"], 2 * tb + 2)
                    for g2, (src, hi, lo) in enumerate(xt_evac(dve, tb, g, j, True)):
                        L(dve.tensor_tensor(lo, src, hi.bitcast(F32), ALU.subtract), S["xt_used"] if g2 else None, wait=False)
                    tb += 1
                dve.wait_ge(S["cmp2_full"], n + 1)
                if kv == 0:
                    out, src = (CKS[:, g, :], PS[:, 3, 0:P]) if g < 2 else (CKP[:, :, :], PS[0:HD, 3, 0:P].rearrange("p (g n) -> p g n", g=KG))
                else:
                    out, src = ((CVS[:, :, g * P:(g + 1) * P], PS[0:32, 3, :].rearrange("p (t n) -> p t n", t=4)) if g < 2
                                else (CVP[:, :], PS[0:32, 3, 0:256]))
                L(dve.tensor_copy(out, src), S["cmp2_used"], wait=False)

        def cmp_pool(pool, L):
            L(pool.memset(XTH[:, :, 256:XTC].bitcast(F32), 0.0))
            L(pool.memset(XTL[:, :, 256:XTC].bitcast(F32), 0.0), S["xt_zero"])
            for kv in range(2):
                if kv:
                    pool.wait_ge(S["xt_full"], 10)
                for tt in range(QT):
                    for r in range(2):
                        pool.dma_start(PCP[(tt % 2) * 64:(tt % 2) * 64 + 64, tt // 2, :, r * HD:(r + 1) * HD],
                                       KV[r:P:2, kv, tt, :].rearrange("p (g d) -> p g d", g=KG)).then_inc(S["ld_pair"], 16)

        def soft_cols(j):
            return SM[:, 0, j:j + 1]

        def samp_pe(pe):
            for t in range(4):
                m = pe.matmul(PS[:, 7, t * 48:(t + 1) * 48], CST[0:NS, C_SEL + t * P:C_SEL + (t + 1) * P], GT[0:NS, QT, :],
                              start=True, stop=True)
            m.then_inc(S["grow_full"], 1)
            pe.wait_ge(S["qbd_ready"], 1)
            for t in range(4):
                pe.wait_ge(ld_att[t % 2], N_ATT_LD * (t // 2 + 1))
                KSN, VSN, KWN, VWN = CACHED[t % 2]
                for bb in range(2):
                    for br, src in enumerate((KSN, KWN)):
                        if bb == 1:
                            pe.wait_ge(S["ktb_a" if br == 0 else "ktb_d"], 2 * t + 1)
                        for gp in range(2):
                            for h in range(2):
                                m = pe.transpose(PS[:, 4 + br, (gp * 2 + h) * P:(gp * 2 + h + 1) * P],
                                                 src[:, bb, h, gp * P:(gp + 1) * P], ID)
                        m.then_inc(S["kb_full"], 1)
                    pe.wait_ge(S["ktb_a"], 2 * t + bb + 1)
                    pe.wait_ge(S["ktb_d"], 2 * t + bb + 1)
                    b = 2 * t + bb
                    for gp in range(2):
                        r0 = bb * 64 + gp * 32
                        pe.matmul(PS[r0:r0 + 32, 2, 0:32], IDB[:, r0:r0 + 32], CMSB[:, :], start=True, stop=False)
                        pe.matmul(PS[r0:r0 + 32, 2, 0:32], QBC[:, b, gp, :], CKS[:, gp, t * 32:(t + 1) * 32], start=False, stop=True)
                        for br in range(2):
                            pe.matmul(PS[r0:r0 + 32, br, 256:288], IDB[:, r0:r0 + 32], NMB[:, t * 32:(t + 1) * 32],
                                      start=True, stop=False)
                            pe.matmul(PS[r0:r0 + 32, br, 256:288], QBR[:, b, gp, :], KNS[:, br, gp, :], start=False, stop=True)
                            m = pe.matmul(PS[r0:r0 + 32, br, 0:256], QBR[:, b, gp, :], KTB[:, br, gp, :], start=True, stop=True)
                    m.then_inc(S["s_qk"], 1)
                pe.wait_ge(S["s_scaled"], t + 1)
                for br in range(2):
                    for h in range(2):
                        m = pe.transpose(PS[:, 4, (br * 2 + h) * P:(br * 2 + h + 1) * P], PS_[:, br, h * P:(h + 1) * P], ID)
                m.then_inc(S["s_pt"], 1)
                for br in range(2):
                    pe.transpose(PS[0:32, 5, br * P:(br + 1) * P], PS_[:, br, 256:288], ID)
                pe.transpose(PS[0:32, 5, 2 * P:3 * P], PC_[:, :], ID).then_inc(S["s_pt"], 1)
                pe.wait_ge(S["pta"], t + 1)
                pe.wait_ge(S["ptb"], t + 1)
                for bb in range(2):
                    for gp in range(2):
                        r = slice(bb * 64 + gp * 32, bb * 64 + gp * 32 + 32)
                        out, c = PS[r, 3, 0:P], slice(gp * P, (gp + 1) * P)
                        for br, v in enumerate((VSN, VWN)):
                            for h in range(2):
                                pe.matmul(out, PTA[:, br * 2 + h, r], v[:, bb, h, c], start=br == 0 and h == 0, stop=False)
                            pe.matmul(out, PTB[0:32, br, r], KV[0:NS, 3 + 2 * br, QT, c], start=False, stop=False)
                        m = pe.matmul(out, PTB[0:32, 2, r], CVS[0:32, t, c], start=False, stop=True)
                m.then_inc(S["s_o"], 1)
                pe.wait_ge(S["os_ready"], t + 1)
                pe.transpose(PS[:, 6, 0:P], OS[:, :], ID).then_inc(S["s_ot"], 1)
                pe.wait_ge(S["ots_ready"], t + 1)

        def samp_act(act, L):
            for t in range(4):
                for bb in range(2):
                    act.wait_ge(S["kb_full"], 4 * t + 2 * bb + 1)
                    if bb:
                        act.wait_ge(S["s_qk"], 2 * t + bb)
                    L(act.activation(KTB[:, 0, :, :], PS[:, 4, :].rearrange("p (a n) -> p a n", a=2), ACT.Copy), S["ktb_a"], wait=False)
                act.wait_ge(S["s_max"], 3 * t + 3)
                for j, (p_, n) in enumerate(((PS_[:, 0, :], 288), (PS_[:, 1, :], 288), (PC_[:, :], 32))):
                    L(act.activation(p_, PS[:, j, 0:n], ACT.Exp, bias=soft_cols(j), accum_out=soft_cols(6 + j)),
                      S["s_exp"], wait=False)
                act.wait_ge(S["s_pt"], 2 * t + 1)
                L(act.activation(PTA[:, :, :], PS[:, 4, :].rearrange("p (a n) -> p a n", a=4), ACT.Copy), S["pta"], wait=False)
                act.wait_ge(S["s_o"], t + 1)
                L(act.activation(OS[:, :], PS[:, 3, 0:P], ACT.Copy), S["os_ready"], wait=False)
                act.wait_ge(S["s_ot"], t + 1)
                L(act.activation(OTS[:, t, :], PS[:, 6, 0:P], ACT.Copy), S["ots_ready"], wait=False)

        def samp_dve(dve, L):
            dve.wait_ge(S["grow_full"], 1)
            gt = GRT[:, :, :]
            L(dve.tensor_tensor(gt, PS[:, 7, 0:192].rearrange("p (t n) -> p t n", t=4),
                                CST[:, C_HM:C_HM + 48].rearrange("p (o n) -> p o n", o=1).broadcast_to([P, 4, 48]), ALU.mult))
            L(dve.tensor_reduce(GROW[:, :, :], gt.rearrange("p t (h b) -> p t b h", b=3), AX.X, ALU.add))
            for t in range(4):
                for bb in range(2):
                    dve.wait_ge(S["kb_full"], 4 * t + 2 * bb + 2)
                    if bb:
                        dve.wait_ge(S["s_qk"], 2 * t + bb)
                    L(dve.tensor_copy(KTB[:, 1, :, :], PS[:, 5, :].rearrange("p (a n) -> p a n", a=2)), S["ktb_d"], wait=False)
                dve.wait_ge(S["s_qk"], 2 * t + 2)
                for j, n in enumerate((288, 288, 32)):
                    L(dve.tensor_reduce(soft_cols(j), PS[:, j, 0:n], AX.X, ALU.max, negate=True), S["s_max"], wait=False)
                dve.wait_ge(S["s_exp"], 3 * t + 3)
                L(dve.reciprocal(SM[:, 0, 9:12], SM[:, 0, 6:9]))
                L(dve.tensor_tensor(SM[:, 0, 12:14], SM[:, 0, 9:11], GROW[:, t, 1:3], ALU.mult))
                L(dve.tensor_tensor(SM[:, 0, 14:15], SM[:, 0, 11:12], GROW[:, t, 0:1], ALU.mult))
                L(dve.tensor_scalar(PS_[:, 0, :], PS_[:, 0, :], soft_cols(12), None, ALU.mult), wait=False)
                L(dve.tensor_scalar(PS_[:, 1, :], PS_[:, 1, :], soft_cols(13), None, ALU.mult), wait=False)
                L(dve.tensor_scalar(PC_[:, :], PC_[:, :], soft_cols(14), None, ALU.mult), S["s_scaled"])
                dve.wait_ge(S["s_pt"], 2 * t + 2)
                L(dve.tensor_copy(PTB[0:32, :, :], PS[0:32, 5, 0:3 * P].rearrange("p (a n) -> p a n", a=3)), S["ptb"], wait=False)
            dve.wait_ge(S["ots_ready"], 4)
            for g2 in range(2):
                for hh in range(GQ):
                    src = OTS[g2 * HD:(g2 + 1) * HD, :, :].rearrange("p t (b a g h s) -> p a (t b) g h s", b=2, a=2, g=2, h=GQ)
                    dst = QC[(hh % 2) * HD:(hh % 2) * HD + HD, :, SEQ:T].rearrange("p (a g h) (b s) -> p a b g h s", a=2, g=2, s=DT)
                    L(dve.tensor_copy(dst[:, :, :, g2, hh // 2, :], src[:, :, :, g2, hh, :]), wait=False)

        def samp_pool(pool, L):
            for dst, src in ((QBC, QC), (QBR, QR)):
                L(pool.memset(dst[:, :, :, :], 0.0))
                for g2 in range(2):
                    for hh in range(GQ):
                        s_ = src[(hh % 2) * HD:(hh % 2) * HD + HD, :, SEQ:T].rearrange("p (a g h) (b s) -> p b a g h s", a=2, g=2, s=DT)
                        L(pool.tensor_copy(dst[g2 * HD:(g2 + 1) * HD, :, :, g2 * 16 + hh * 4:g2 * 16 + hh * 4 + 4],
                                           s_[:, :, :, g2, hh // 2, :]),
                          S["qbd_ready"] if dst is QBR and g2 == 1 and hh == GQ - 1 else None)

        AHEAD = 3
        N_HS = 2 * QT * GQ

        class Group:
            def __init__(self, kind, at, pair=0, half=0):
                self.kind, self.at, self.pair, self.half = kind, at, pair, half

        def prompt_groups():
            out = [Group("scores", -1, 0), Group("cmp", 0, 0, 0), Group("cmp", 0, 0, 1)]
            for h in range(N_HS):
                if h == 12:
                    out += [Group("cmp", h, 1, half) for half in range(2)]
                if h == 19:
                    out.append(Group("out", h, 0))
                out.append(Group("pv", h))
                if h == 8:
                    out.append(Group("scores", h, 1))
            out.append(Group("out", N_HS, 1))
            for i, g in enumerate(out):
                g.index, g.bank, g.nth = i, i % 2, i // 2
            return out

        GRP = prompt_groups()
        N_GRP = len(GRP)
        OWNER = ("grp_dve", "grp_act")
        assert N_GRP % 2 == 0
        assert all(x.bank == 0 for x in GRP if x.kind == "scores")

        def group_of(kind, **want):
            return [x for x in GRP if x.kind == kind and all(want[k] == {"at": x.at, "pair": x.pair, "half": x.half}[k]
                                                             for k in want)][0]

        def split_hs(h):
            return h // (2 * QT), h // 2 % QT, h % 2

        def read_out(eng, g, gr):
            eng.wait_ge(S[OWNER[gr.bank]], g * (N_GRP // 2) + (gr.nth + 2))

        def prompt_pe(pe):
            pe.drain().then_inc(S["p_qk"], 16)
            pe.drain().then_inc(S["p_grp"], N_GRP)
            pe.drain().then_inc(S["p_pv"], 2)
            with pe.Fori(0, KG) as g:
                def scores_cmp(gr):
                    pe.wait_ge(S["qs_c"], g * 4 + (2 * gr.pair + 2))
                    for half in range(2):
                        for qt in range(QT):
                            c = half * P + qt * 32
                            pe.matmul(PS[:, 6, c:c + 32], IDB[:, :], CMPB[:, qt * 32:(qt + 1) * 32], start=True, stop=False)
                            m = pe.matmul(PS[:, 6, c:c + 32], QS[:, half, qt * P:(qt + 1) * P],
                                          CKP[:, ds(g, 1), :].rearrange("p o n -> p (o n)"), start=False, stop=True)
                    return m

                def qk(h):
                    hh, qt, br = split_hs(h)
                    n = (qt + 1) * P
                    if qt == 0 and br == 0:
                        pe.wait_ge(S["q_pair"], g * GQ + (hh + 1))
                    if h < 2:
                        pe.wait_ge(S["k_low"], g * 4 + (2 * br + 2))
                    pe.wait_ge(S["p_exp"], g * N_HS + (h + 1))
                    bank, qs, rows = PS[:, h % 4, :], slice(qt * P, (qt + 1) * P), slice(hh % 2 * HD, hh % 2 * HD + HD)
                    pe.matmul(bank[:, 0:n], QA[:, hh % 2, qs], KA[:, br, 0:n], start=True, stop=False)
                    pe.matmul(bank[:, qt * P:n], IDB[:, :], CAUB[:, :], start=False, stop=False)
                    m = pe.matmul(bank[:, 0:n], QA[rows, hh % 2, qs], KB[rows, br, 0:n], start=False, stop=True)
                    m.then_inc(S["p_qk"], 1)

                def group(gr):
                    pe.wait_ge(S[OWNER[gr.bank]], g * (N_GRP // 2) + (gr.nth + 1))
                    out = PS[:, 6 + gr.bank, :]
                    if gr.kind == "scores":
                        m = scores_cmp(gr)
                    elif gr.kind == "cmp":
                        if gr.half == 0:
                            pe.wait_ge(S["c_scaled"], g * 2 + (gr.pair + 1))
                        for qt in range(QT):
                            m = pe.transpose(out[0:32, qt * P:(qt + 1) * P], PPC[:, gr.half * QT + qt, :], ID)
                    elif gr.kind == "out":
                        pe.wait_ge(S["o_used"], g * 16 + (8 * gr.pair + 10))
                        for qt in range(QT):
                            m = pe.transpose(out[:, qt * P:(qt + 1) * P], ON[:, gr.pair, qt, :], ID)
                    else:
                        pe.wait_ge(S["p_exp"], g * N_HS + (gr.at + 5))
                        for kt in range(split_hs(gr.at)[1] + 1):
                            m = pe.transpose(out[:, kt * P:(kt + 1) * P], PP[:, gr.at // 2 % 2, gr.at % 2, kt * P:(kt + 1) * P], ID)
                    m.then_inc(S["p_grp"], 1)

                def values(gr):
                    h = gr.at
                    hh, qt, br = split_hs(h)
                    o_ = PS[:, 4 + h // 2 % 2, :]
                    read_out(pe, g, gr)
                    if br == 0:
                        pe.wait_ge(S["o_used"], g * 16 + (h // 2 + 1))
                        if qt == 0:
                            read_out(pe, g, group_of("cmp", pair=hh // 2, half=hh % 2))
                    for kt in range(qt + 1):
                        m = pe.matmul(o_[:, (1 + br) * HD:(2 + br) * HD], PT[:, h % 2, kt * P:(kt + 1) * P],
                                      KV[:, 3 + 2 * br, kt, ds(g * HD, HD)], start=kt == 0, stop=kt == qt)
                    if br == 0:
                        m = pe.matmul(o_[:, 0:HD], PCT[0:32, hh // 2, hh % 2 * QT + qt, :],
                                      CVP[0:32, ds(g * HD, HD)], start=True, stop=True)
                    m.then_inc(S["p_pv"], 1)

                for gr in GRP:
                    if gr.at < 0:
                        group(gr)
                for h in range(AHEAD):
                    qk(h)
                pending = None
                for h in range(N_HS + 1):
                    if h + AHEAD < N_HS:
                        qk(h + AHEAD)
                    for gr in GRP:
                        if gr.at == h:
                            if h == N_HS:
                                values(pending)
                            group(gr)
                            if gr.kind == "pv":
                                if pending is not None:
                                    values(pending)
                                pending = gr

        def evacs(eng, L, g, at, bank, scores=None):
            copy = (lambda o_, i_: eng.activation(o_, i_, ACT.Copy)) if bank == 1 else (lambda o_, i_: eng.tensor_copy(o_, i_))
            done = S[OWNER[bank]]
            for gr in GRP:
                if gr.at != at or gr.bank != bank:
                    continue
                eng.wait_ge(S["p_grp"], g * N_GRP + (N_GRP + gr.index + 1))
                src = PS[:, 6 + bank, :]
                if gr.kind == "scores":
                    scores(src, done)
                elif gr.kind == "cmp":
                    eng.wait_ge(S["p_pv"], g * N_HS + 2)
                    L(copy(PCT[0:32, gr.pair, gr.half * QT:(gr.half + 1) * QT, :],
                           src[0:32, :].rearrange("p (t n) -> p t n", t=QT)), done, wait=False)
                elif gr.kind == "out":
                    L(copy(QC[:, ds(g * 2 + gr.pair, 1), 0:SEQ].rearrange("p o n -> p (o n)"), src), done, wait=False)
                else:
                    n = (split_hs(gr.at)[1] + 1) * P
                    eng.wait_ge(S["p_pv"], g * N_HS + (gr.at + 1))
                    L(copy(PT[:, gr.at % 2, 0:n], src[:, 0:n]), done, wait=False)

        def prompt_act(act, L):
            split_hi(act, S_WO, S_WO % 2, S_WO // 2, B_WO)
            act.drain().then_inc(S["grp_act"], 1)
            act.drain().then_inc(S["p_exp"], 4)
            L.count[S["grp_act"]], L.count[S["p_exp"]] = 1, 4
            with act.Fori(0, KG) as g:
                L.loop(g, grp_act=N_GRP // 2, p_exp=N_HS, c_exp=2, k_twice=4, q_high=GQ)
                def exps(h):
                    hh, qt, br = split_hs(h)
                    n, u = (qt + 1) * P, h // 2
                    act.wait_ge(S["p_max"], g * N_HS + (h + 1))
                    was = group_of("pv", at=(h - 4) % N_HS)
                    act.wait_ge(S["p_grp"], g * N_GRP + (was.index + 1 + (N_GRP if h >= 4 else 0)))
                    L(act.activation(PP[:, u % 2, br, 0:n], PS[:, h % 4, 0:n], ACT.Exp, bias=SMP[:, u % 4, br:br + 1],
                                     accum_out=SMP[:, u % 4, 2 + br:3 + br]), S["p_exp"], wait=False)

                def exp_cmp(hp):
                    read_out(act, g, group_of("scores", pair=hp))
                    L(act.activation(PPC[:, :, :], PPC[:, :, :], ACT.Exp), S["c_exp"], wait=False)

                keys = KT[:, :, :, :].rearrange("p a g n -> p (a g n)")

                def keys_high(br):
                    act.wait_ge(S["p_qk"], g * N_HS + 16)
                    for r in range(2):
                        L(act.activation(KA[r * HD:(r + 1) * HD, br, :], keys[:, ds(g * SEQ + br * KG * SEQ, SEQ)], ACT.Copy),
                          S["k_twice"], wait=False)

                def q_high(hh):
                    rows = slice(hh % 2 * HD, hh % 2 * HD + HD)
                    act.wait_ge(S["q_chunk"], g * 2 + (hh // 2 + 1))
                    act.wait_ge(S["p_qk"], g * N_HS + 8 * (hh + 1))
                    L(act.activation(QA[rows, hh % 2, :], QF[rows, :], ACT.Copy), S["q_high"], wait=False)

                keys_high(0)
                q_high(0)
                exp_cmp(0)
                keys_high(1)
                for h in range(AHEAD - 1):
                    exps(h)
                for h in range(N_HS + 1):
                    if h in (1, 9, 17):
                        q_high((h + 7) // 8)
                    if h == 10:
                        exp_cmp(1)
                    evacs(act, L, g, h, 1)
                    if h + AHEAD - 1 < N_HS:
                        exps(h + AHEAD - 1)
            L.end(KG)

        def prompt_dve(dve, L):
            split_lo(dve, S_WO, S_WO % 2)
            dve.drain().then_inc(S["grp_dve"], 1)
            dve.drain().then_inc(S["o_used"], 2)
            L.count[S["grp_dve"]], L.count[S["o_used"]] = 1, 2
            with dve.Fori(0, KG) as g:
                L.loop(g, grp_dve=N_GRP // 2, dve_chain=4 * 16 + 2 * 7, p_max=N_HS, c_scaled=2, o_used=16, k_low=4)
                def cmp_a(src, done):
                    s = src[:, 0:256].rearrange("p (t n) -> p t n", n=32)
                    L(dve.tensor_reduce(SMC[:, 0, :], s, AX.X, ALU.max, negate=True))
                    L(dve.tensor_scalar(SMC[:, 0, :], SMC[:, 0, :], -FLOOR, None, ALU.min))
                    L(dve.tensor_tensor(PPC[:, :, :], s, SMC[:, 0, :].rearrange("p (t o) -> p t o", o=1).broadcast_to([P, 8, 32]),
                                        ALU.add), done)

                def cmp_b(hp):
                    dve.wait_ge(S["c_exp"], g * 2 + (hp + 1))
                    L(dve.tensor_reduce(SMC[:, 1, :], PPC[:, :, :], AX.X, ALU.add))
                    L(dve.tensor_scalar(SMC[:, 1, :], SMC[:, 1, :], 1e-30, None, ALU.max))
                    L(dve.reciprocal(SMC[:, 2, :], SMC[:, 1, :]))
                    for half in range(2):
                        c = SMC[:, 3, half * QT:(half + 1) * QT].rearrange("p (t o) -> p t o", o=1)
                        r = SMC[:, 2, half * QT:(half + 1) * QT].rearrange("p (t o) -> p t o", o=1)
                        L(dve.tensor_tensor(c, r, GT[:, 0:QT, ds(g * 12 + (2 * hp + half) * 3, 1)], ALU.mult))
                    L(dve.tensor_tensor(PPC[:, :, :], PPC[:, :, :],
                                        SMC[:, 3, :].rearrange("p (t o) -> p t o", o=1).broadcast_to([P, 8, 32]), ALU.mult),
                      S["c_scaled"])

                def maximum(h):
                    hh, qt, br = split_hs(h)
                    dve.wait_ge(S["p_qk"], g * N_HS + (h + 17))
                    L(dve.tensor_reduce(SMP[:, h // 2 % 4, br:br + 1], PS[:, h % 4, 0:(qt + 1) * P], AX.X, ALU.max, negate=True),
                      S["p_max"], wait=False)

                def norm(u):
                    dve.wait_ge(S["p_exp"], g * N_HS + (2 * u + 6))
                    L(dve.reciprocal(SMP[:, u % 4, 4:6], SMP[:, u % 4, 2:4]))
                    L(dve.tensor_tensor(SMP[:, u % 4, 6:8], SMP[:, u % 4, 4:6],
                                        GT[:, u % QT, ds(g * 12 + (u // QT) * 3 + 1, 2)], ALU.mult))

                def combine(u):
                    dve.wait_ge(S["p_pv"], g * N_HS + (2 * u + 4))
                    ob, half = PS[:, 4 + u % 2, :], u // QT % 2
                    L(dve.tensor_scalar(OM[:, u % 2, :], ob[:, HD:2 * HD], SMP[:, u % 4, 6:7], None, ALU.mult))
                    L(dve.scalar_tensor_tensor(OM[:, u % 2, :], ob[:, 2 * HD:3 * HD], SMP[:, u % 4, 7:8], OM[:, u % 2, :],
                                               ALU.mult, ALU.add))
                    L(dve.tensor_tensor(ON[:, u // 8, u % QT, half * HD:(half + 1) * HD], OM[:, u % 2, :], ob[:, 0:HD], ALU.add),
                      S["o_used"], wait=False)

                evacs(dve, L, g, -1, 0, cmp_a)
                keys = KT[:, :, :, :].rearrange("p a g n -> p (a g n)")
                for br in range(2):
                    for r in range(2):
                        dve.wait_ge(S["k_twice"], g * 4 + (2 * br + 2))
                        L(dve.tensor_tensor(KB[r * HD:(r + 1) * HD, br, :], keys[:, ds(g * SEQ + br * KG * SEQ, SEQ)],
                                            KA[0:HD, br, :].bitcast(F32), ALU.subtract), S["k_low"], wait=False)
                for h in range(AHEAD):
                    maximum(h)
                    if h == 0:
                        cmp_b(0)
                for h in range(N_HS + 1):
                    if h + AHEAD < N_HS:
                        maximum(h + AHEAD)
                    if h == 11:
                        cmp_b(1)
                    if h % 2 and h < N_HS:
                        norm(h // 2)
                    if h == N_HS:
                        combine(h // 2 - 1)
                    evacs(dve, L, g, h, 0, cmp_a)
                    if h % 2 and 3 <= h < N_HS:
                        combine(h // 2 - 1)
            L.end(KG)

        def prompt_pool(pool, L):
            with pool.Fori(0, KG) as g:
                L.loop(g, qs_c=4, q_chunk=2, q_pair=GQ)
                for hh in range(GQ):
                    half = hh % 2
                    rows, other = slice(half * HD, half * HD + HD), slice((1 - half) * HD, (2 - half) * HD)
                    if half == 0:
                        for hf in range(2):
                            if hf == 0:
                                was = group_of("scores", pair=1 - hh // 2)
                                pool.wait_ge(S["p_grp"], g * N_GRP + (was.index + 1 + (N_GRP if hh else 0)))
                            pool.wait_ge(S["qbd_ready"], 1)
                            L(pool.tensor_copy(QS[:, hf, :], QC[hf * HD:(hf + 1) * HD, ds(g * 2 + hh // 2, 1), 0:SEQ]
                                               .rearrange("p o n -> p (o n)")), S["qs_c"])
                    if half == 0:
                        L(pool.tensor_copy(QF[:, :], QR[:, ds(g * 2 + hh // 2, 1), 0:SEQ].rearrange("p o n -> p (o n)")), S["q_chunk"])
                    pool.wait_ge(S["q_high"], g * GQ + (hh + 1))
                    L(pool.tensor_tensor(QA[other, half, :], QF[rows, :], QA[rows, half, :].bitcast(F32), ALU.subtract), S["q_pair"])
            L.end(KG)

        def nsa_pe(pe):
            proj_pe(pe)
            end_phase(pe, 5)
            rope_pe(pe)
            end_phase(pe, 6)
            cmp_pe(pe)
            end_phase(pe, 7)
            samp_pe(pe)
            end_phase(pe, 8)
            prompt_pe(pe)
            end_phase(pe, 9)
            pe_linear(pe, 4, S_WO, B_WO, x_ready, 8 * 5)
            end_phase(pe, 10)
            stat_pe(pe, 4, 6)
            ffn_pe(pe, 1, S_FFN1, B_FFN1, 6, 5, 7)
            end_phase(pe, 11)

        def nsa_act(act, L):
            proj_act(act, L)
            end_phase(act, 5)
            rope_act(act, L)
            end_phase(act, 6)
            cmp_act(act, L)
            end_phase(act, 7)
            samp_act(act, L)
            end_phase(act, 8)
            prompt_act(act, L)
            end_phase(act, 9)
            for c in range(NC):
                L(act.activation(XH[:, c, :], QC[:, c, :], ACT.Copy), S["xh_ready"])
            act.wait_ge(stores, 16 * N_KV_ST)
            with act.Fori(0, 2) as i:
                for h in range(2):
                    act_split_ahead(act, i, S_WO, B_WO, h)
                    for mb in range(2):
                        act.wait_ge(blk_full, i * 4 + (B_WO + 2 * h + mb + 1))
                        act.activation(F[:, ds(i * 4 + (2 * h + mb), 1), :].rearrange("p o (h n) -> p (o h) n", h=2),
                                       blk(mb), ACT.Copy).then_inc(blk_free, 1)
            end_phase(act, 10)
            stat_act(act, L, F, 4)
            std_act(act, L, S["stat_used"], 7)
            residual_act(act, L, V_FPRE + NC, 3, 6, True, 1)
            ffn_act(act, L, 1, S_FFN1, B_FFN1, 6, 4, 5, 5, True)
            end_phase(act, 11)

        def nsa_dve(dve, L):
            proj_dve(dve, L)
            end_phase(dve, 5)
            rope_dve(dve, L)
            end_phase(dve, 6)
            cmp_dve(dve, L)
            end_phase(dve, 7)
            samp_dve(dve, L)
            end_phase(dve, 8)
            prompt_dve(dve, L)
            end_phase(dve, 9)
            for c in range(NC):
                dve.wait_ge(S["xh_ready"], 8 * 5 + c + 1)
                L(dve.tensor_tensor(XL[:, c, :], QC[:, c, :], XH[:, c, :].bitcast(F32), ALU.subtract), x_ready)
            with dve.Fori(0, 2) as i:
                for h in range(2):
                    dve_split_ahead(dve, i, S_WO, h)
            end_phase(dve, 10)
            rstd_dve(dve, L, 4, 4)
            residual_dve(dve, L, V_MPOST + NC, V_FPRE + NC, 3, 6)
            ffn_dve(dve, L, 1, S_FFN1, B_FFN1, 6, 4, V_FPOST + NC, 5, 5, True)
            end_phase(dve, 11)

        def nsa_pool(pool, L):
            proj_pool(pool, L)
            end_phase(pool, 5)
            rope_pool(pool, L)
            end_phase(pool, 6)
            cmp_pool(pool, L)
            end_phase(pool, 7)
            samp_pool(pool, L)
            end_phase(pool, 8)
            prompt_pool(pool, L)
            end_phase(pool, 9)
            load_p(pool, 1)
            end_phase(pool, 10)
            residual_pool(pool, L, 1)
            end_phase(pool, 11)
        @block.sync
        def _(sp):
            sp.dma_start(CST[:, :], a["consts"]).then_inc(S["ld_const"], 16)
            for tt in range(QT):
                sp.dma_start(XTOK[:, tt, :], a["x_prompt"][0, tt * P:(tt + 1) * P, :]).then_inc(S["ld_x"], 16)
            sp.dma_start(XTOK[0:NS, QT, :], a["x_sample"].rearrange("b t d -> (b t) d")).then_inc(S["ld_x"], 16)
            for row, n, src in ((V_MPRE, 16, "norm_mix_pre"), (V_MPOST, 16, "norm_mix_post"), (V_FPRE, 16, "norm_ffn_pre"),
                                (V_FPOST, 16, "norm_ffn_post"), (V_BIN, 16, "conv_b_in"), (V_BDW, 8, "conv_b_dw"),
                                (V_LNG, 8, "conv_ln_g"), (V_LNB, 8, "conv_ln_b"), (V_BOUT, 8, "conv_b_out")):
                sp.dma_start(VROW[row:row + n, :], a[src].rearrange("l (c p) -> (l c) p", p=P)).then_inc(S["ld_vec"], 16)
            sp.dma_start(WDT[:, :], a["conv_w_dw"][0]).then_inc(S["ld_vec"], 16)
            sp.dma_start(STT[:, :, :], a["state_conv"][0].rearrange("(h b) j d -> (b j) h d", h=2)).then_inc(S["ld_state"], 16)

            def slab(src, i, s, par, wait=True):
                if wait:
                    sp.wait_ge(w_lo, s - 1)
                raw = RAW[par][:, :].rearrange("p (h x) -> p h x", h=2)
                for h in range(2):
                    v = src(i, h)
                    sp.dma_start(raw[:, h, :].rearrange("p (k n) -> p k n", k=v.shape[1]), v).then_inc(w_raw[par], 16)

            s = 0
            for n_stage, (src, n) in enumerate(STAGES):
                if s == S_WO:
                    sp.wait_ge(S["ld_gate"], 48)
                    sp.wait_ge(w_lo, S_CMP + 2)
                    nsa_pair_loads(sp, 0)
                    sp.wait_ge(phase, 4 * 6)
                    nsa_kv_stores(sp)
                    nsa_pair_loads(sp, 1)
                    sp.wait_ge(S["xt_full"], 18)
                    nsa_sample_loads(sp, 0)
                    sp.wait_ge(phase, 4 * 7)
                    nsa_sample_loads(sp, 1)
                    for t in range(2, 4):
                        sp.wait_ge(S["s_o"], t - 1)
                        nsa_sample_loads(sp, t)
                    sp.wait_ge(S["s_o"], 3)
                    for h in range(2):
                        slab(src, h, s + h, (s + h) % 2)
                    for h in range(2, 4):
                        slab(src, h, s + h, (s + h) % 2)
                    s += n
                    continue
                if n == 1:
                    slab(src, 0, s, s % 2)
                elif s == 0:
                    for h in range(2):
                        slab(src, h, h, h, wait=False)
                    with sp.Fori(1, n // 2) as i:
                        for h in range(2):
                            slab(src, i * 2 + h, i * 2 + h, h)
                else:
                    with sp.Fori(0, n // 2) as i:
                        for h in range(2):
                            slab(src, i * 2 + h, i * 2 + (s + h), (s + h) % 2)
                s += n
            for tt in range(NTT):
                sp.wait_ge(S["y_rows"], 2 * tt + 2)
                if tt < QT:
                    sp.dma_start(o["y_prompt"][0, tt * P:(tt + 1) * P, :], YTOK[:, tt, :]).then_inc(stores, 16)
                else:
                    sp.dma_start(o["y_sample"].rearrange("b t d -> (b t) d"), YTOK[0:NS, QT, :]).then_inc(stores, 16)
            sp.wait_ge(stores, 16 * (NTT + N_KV_ST))
            sp.wait_ge(stores_pool, 16 * conv_states_n)

        @block.tensor
        def _(pe):
            pe.drain().then_inc(blk_full, 2)
            pe.wait_ge(S["ld_const"], 16)
            pe.wait_ge(S["ld_vec"], 160)
            pe.wait_ge(S["ld_state"], 16)
            pe.transpose(PS[:, 4, 0:V_ALL], VROW[:, :], ID[0:V_ALL, 0:V_ALL]).then_inc(S["bank_full"], 1)
            for c in range(NC):
                m = pe.transpose(PS[:, 5, c * 32:c * 32 + CW], WDT[:, c * P:(c + 1) * P], ID[0:CW, 0:CW])
            m.then_inc(S["bank_full"], 1)
            pe.wait_ge(S["ld_x"], 16 * NTT)
            for c in range(NC):
                if c >= 4:
                    pe.wait_ge(S["bank_free"], 2 + c - 3)
                for tt in range(QT):
                    m = pe.transpose(PS[:, c % 4, tt * P:(tt + 1) * P], XTOK[:, tt, c * P:(c + 1) * P], ID)
                m.then_inc(S["bank_full"], 1)
            for c in range(NC):
                m = pe.transpose(PS[:, 6, c * NS:(c + 1) * NS], XTOK[0:NS, QT, c * P:(c + 1) * P], ID[0:NS, 0:NS])
            m.then_inc(S["bank_full"], 1)
            for c in range(NC):
                pe.wait_ge(S["bank_free"], c + 7 if c < 4 else c + 8)
                for h in range(2):
                    m = pe.transpose(PS[:, c % 4, h * 120:(h + 1) * 120], STT[:, h, c * P:(c + 1) * P], ID[0:120, 0:120])
                m.then_inc(S["bank_full"], 1)
            pe.wait_ge(S["bank_free"], 19)
            for c in range(NC):
                pe.wait_ge(S["x_scaled"], 10)
                if c >= 4:
                    pe.wait_ge(x_ready, c - 3)
                for tt in range(QT):
                    m = pe.transpose(PS[:, c % 4, tt * P:(tt + 1) * P], XTOK[:, tt, c * P:(c + 1) * P], ID)
                m.then_inc(S["bank_full"], 1)
            for c in range(NC):
                m = pe.transpose(PS[:, 7, c * NS:(c + 1) * NS], XTOK[0:NS, QT, c * P:(c + 1) * P], ID[0:NS, 0:NS])
            m.then_inc(S["bank_full"], 1)
            end_phase(pe, 1)
            def pair(i):
                for h in range(2):
                    for mb in range(2):
                        pe_block(pe, h, mb, i * 4 + (B_CONV + 2 * h + mb), i * 2 + (S_CONV + h), mb,
                                 XH, XL, None, 0, width=P, mb_step=D)
            pe.drain().then_inc(S["diag_used"], N_DG)
            pair(0)
            with pe.Fori(1, 4) as i:
                taps_pe(pe, i - 1)
                pair(i)
            taps_pe(pe, 3)
            pe.wait_ge(S["conv_done"], NC)
            for h, (c0, n) in enumerate(((SEQ, CW - 1), (XP + (CW - 1) * DB, NS))):
                for half in range(2):
                    for c in range(4):
                        m = pe.transpose(PS[0:n, 4 + 2 * h + half, c * P:(c + 1) * P], XIN[:, half * 4 + c, c0:c0 + n], ID)
                    m.then_inc(S["bank_full"], 1)
            end_phase(pe, 2)
            for c in range(NC):
                m = pe_ones(pe, F[:, c, :], c == 0, c == NC - 1)
            m.then_inc(S["stat_ready"], 1)
            stat_pe(pe, 0, 1)
            pe_linear(pe, 4, S_CONVO, B_CONVO, x_ready, 8 * 1)
            end_phase(pe, 3)
            stat_pe(pe, 1, 2)
            ffn_pe(pe, 0, S_FFN0, B_FFN0, 2, 2, 3)
            end_phase(pe, 4)
            nsa_pe(pe)
            for tt in range(NTT):
                rows = P if tt < QT else NS
                for half in range(2):
                    i = 2 * tt + half
                    if i >= 4:
                        pe.wait_ge(S["y_rows"], i - 3)
                    for c in range(4):
                        m = pe.transpose(PS[0:rows, 4 + i % 4, c * P:(c + 1) * P],
                                         R[:, half * 4 + c, tt * P:tt * P + rows], ID)
                    m.then_inc(S["y_full"], 1)

        @block.scalar
        def _(act):
            L = Link(act, chain["act"])
            act.wait_ge(S["ld_x"], 16 * NTT)
            act.wait_ge(S["masks"], 6)
            for tt in range(NTT):
                rows = P if tt < QT else NS
                L(act.activation(JNK[0:rows, :], XTOK[0:rows, tt, :], ACT.Square, accum_out=SS5[0:rows, tt:tt + 1]),
                  S["row_sq"])
            act.wait_ge(S["row_rstd"], 1)
            L(act.activation(SS5[:, 0:NTT], SS5[:, 0:NTT], ACT.Sqrt), S["row_sq"])
            act.wait_ge(S["row_rstd"], 2)
            act.wait_ge(S["bank_full"], 11)
            for tt in range(NTT):
                rows = P if tt < QT else NS
                for h in range(2):
                    L(act.activation(XTOK[0:rows, tt, h * 512:(h + 1) * 512], XTOK[0:rows, tt, h * 512:(h + 1) * 512],
                                     ACT.Copy, scale=SS5[0:rows, tt:tt + 1]), S["x_scaled"])
            for c in range(NC):
                act.wait_ge(S["bank_full"], 20 + c)
                L(act.activation(XH[:, c, 0:SEQ], PS[:, c % 4, :], ACT.Copy, scale=vec(V_MPRE + c)), S["xh_ready"])
            act.wait_ge(S["bank_full"], 28)
            L(act.activation(TMP[0][:, 0:256], PS[:, 7, 0:256], ACT.Copy), S["row_sq"])
            act.wait_ge(S["row_rstd"], 3)
            L(act.activation(XH[:, :, SEQ:T], TMP[0][:, 0:256].rearrange("p (c n) -> p c n", c=NC), ACT.Copy), S["xs_hi"])
            split_hi(act, 0, 0, 0, B_CONV)
            end_phase(act, 1)
            split_hi(act, 1, 1, 0, 2)
            def glu_pair(i, final):
                for h in range(2):
                    b = B_CONV + 2 * h
                    act.wait_ge(S["glu_used"], i * 2 + (h + 1))
                    c = i * 2 + h
                    act.wait_ge(blk_full, i * 4 + (b + 1))
                    act.activation(two(TMP[2 * h][:, :]), blk(0), ACT.Identity,
                                   bias=VEC[:, ds(c + V_BIN, 1)]).then_inc(blk_free, 1)
                    act.wait_ge(blk_full, i * 4 + (b + 2))
                    act.activation(two(TMP[2 * h + 1][:, :]), blk(1), ACT.Sigmoid,
                                   bias=VEC[:, ds(c + V_BIN + NC, 1)]).then_inc(blk_free, 1)
                    if not (final and h):
                        split_hi(act, i * 2 + (2 + h), h, i + 1, i * 4 + (b + 2))
            glu_pair(0, False)
            with act.Fori(1, 3) as i:
                diags_act(act, i - 1)
                glu_pair(i, False)
            diags_act(act, 2)
            glu_pair(3, True)
            diags_act(act, 3)
            act.wait_ge(S["bank_full"], 32)
            for h, n in enumerate((CW - 1, NS)):
                for half in range(2):
                    L(act.activation(CST_OUT[0:n, h, half * 512:(half + 1) * 512], PS[0:n, 4 + 2 * h + half, :], ACT.Copy),
                      S["cs_rows"])
            end_phase(act, 2)
            act.wait_ge(S["mean_ready"], 1)
            for c in range(NC):
                act.wait_ge(S["mean_ready"], 1 + c)
                if c >= 2:
                    act.wait_ge(S["sq_used"], c - 1)
                L(act.activation(TMP[c % 2][:, :], F[:, c, :], ACT.Square), S["sq_ready"], wait=False)
            std_act(act, L, S["stat_used"], 2)
            for c in range(NC):
                act.wait_ge(S["silu_ready"], c + 1)
                L(act.activation(TMP[c % 2][:, :], TMP[c % 2][:, :], ACT.Silu, scale=vec(V_LNG + c), bias=vec(V_LNB + c)))
                L(act.activation(XH[:, c, :], TMP[c % 2][:, :], ACT.Copy), S["xh_ready"], wait=False)
            with act.Fori(0, 2) as i:
                for h in range(2):
                    act_split_ahead(act, i, S_CONVO, B_CONVO, h)
                    for mb in range(2):
                        c = i * 4 + (2 * h + mb)
                        act.wait_ge(blk_full, i * 4 + (B_CONVO + 2 * h + mb + 1))
                        act.activation(F[:, ds(c, 1), :].rearrange("p o (h n) -> p (o h) n", h=2), blk(mb), ACT.Identity,
                                       bias=VEC[:, ds(c + V_BOUT, 1)]).then_inc(blk_free, 1)
            end_phase(act, 3)
            stat_act(act, L, F, 1)
            std_act(act, L, S["stat_used"], 3)
            residual_act(act, L, V_FPRE, 0, 2, True, 0)
            ffn_act(act, L, 0, S_FFN0, B_FFN0, 2, 1, 2, 2, False)
            end_phase(act, 4)
            nsa_act(act, L)
            for i in range(2 * NTT):
                rows = P if i // 2 < QT else NS
                act.wait_ge(S["y_full"], i + 1)
                L(act.activation(YTOK[0:rows, i // 2, (i % 2) * 512:(i % 2) * 512 + 512], PS[0:rows, 4 + i % 4, :], ACT.Copy),
                  S["y_rows"])

        @block.vector
        def _(dve):
            L = Link(dve, chain["dve"])
            L(dve.memset(SS5[:, :], 1.0), S["masks"])
            dve.wait_ge(S["ld_const"], 16)
            L(dve.tensor_copy(IDB[:, :], CST[:, C_ID:C_ID + P]), S["masks"])
            L(dve.tensor_copy(CAUB[:, :], CST[:, C_CAU:C_CAU + P]), S["masks"])
            L(dve.tensor_copy(CMPB[:, :], CST[:, C_CMP:C_CMP + QT * 32]), S["masks"])
            L(dve.tensor_copy(NMB[:, :], CST[:, C_NM:C_NM + 128]), S["masks"])
            L(dve.tensor_copy(CMSB[:, :], CST[:, C_CMS:C_CMS + 32]), S["masks"])
            dve.wait_ge(S["bank_full"], 1)
            L(dve.tensor_copy(VEC[:, :], PS[:, 4, 0:V_ALL]), S["bank_free"])
            dve.wait_ge(S["bank_full"], 2)
            L(dve.tensor_copy(WDW[:, :, 0:CW], PS[:, 5, 0:256].rearrange("p (c j) -> p c j", j=32)[:, :, 0:CW]), S["bank_free"])
            dve.wait_ge(S["row_sq"], NTT)
            L(dve.tensor_scalar(SS5[:, 0:NTT], SS5[:, 0:NTT], 1.0 / D, EPS, ALU.mult, ALU.add), S["row_rstd"])
            for c in range(NC):
                dve.wait_ge(S["bank_full"], 3 + c)
                L(dve.tensor_copy(R[:, c, 0:SEQ], PS[:, c % 4, :]), S["bank_free"])
            dve.wait_ge(S["bank_full"], 11)
            L(dve.tensor_copy(R[:, :, SEQ:T], PS[:, 6, 0:256].rearrange("p (c n) -> p c n", c=NC)), S["bank_free"])
            dve.wait_ge(S["row_sq"], NTT + 1)
            L(dve.reciprocal(SS5[:, 0:NTT], SS5[:, 0:NTT]), S["row_rstd"])
            for c in range(NC):
                dve.wait_ge(S["bank_full"], 12 + c)
                L(dve.tensor_copy(XIN[:, c, XP:XP + 240].rearrange("p (j b) -> p b j", b=DB),
                                  PS[:, c % 4, 0:240].rearrange("p (b j) -> p b j", b=DB)), S["bank_free"])
            for c in range(NC):
                dve.wait_ge(S["xh_ready"], c + 1)
                L(dve.scalar_tensor_tensor(XL[:, c, 0:SEQ], PS[:, c % 4, :], vec(V_MPRE + c), XH[:, c, 0:SEQ].bitcast(F32),
                                           ALU.mult, ALU.subtract), x_ready)
            dve.wait_ge(S["row_sq"], NTT + 2)
            tv = TMP[0][:, 0:256].rearrange("p (c n) -> p c n", c=NC)
            L(dve.tensor_tensor(tv, tv, VEC[:, V_MPRE:V_MPRE + NC].rearrange("p (c o) -> p c o", o=1).broadcast_to([P, NC, NS]),
                                ALU.mult), S["row_rstd"])
            dve.wait_ge(S["xs_hi"], 1)
            L(dve.tensor_tensor(XL[:, :, SEQ:T], tv, XH[:, :, SEQ:T].bitcast(F32), ALU.subtract))
            split_lo(dve, 0, 0)
            dve.drain().then_inc(S["glu_used"], 2)
            L.count[S["glu_used"]] = 2
            dve.drain().then_inc(S["tap_used"], 2)
            L.count[S["tap_used"]] = 2
            end_phase(dve, 1)
            split_lo(dve, 1, 1)
            def conv_pair(i, final):
                dve.wait_ge(blk_free, i * 4 + (B_CONV + 4))
                xin, y = [], []
                for h in range(2):
                    ta, tg = TMP[2 * h], TMP[2 * h + 1]
                    xin.append(XIN[:, ds(i * 2 + h, 1), :].rearrange("p o n -> p (o n)"))
                    y.append(F[:, ds(i * 2 + h, 1), :].rearrange("p o n -> p (o n)"))
                    L(dve.tensor_tensor(xin[h][:, CW - 1:XP], ta[:, 0:SEQ], tg[:, 0:SEQ], ALU.mult), wait=False)
                    L(dve.tensor_tensor(xin[h][:, XP + 240:XC].rearrange("p (t b) -> p b t", b=DB),
                                        ta[:, SEQ:T].rearrange("p (b t) -> p b t", b=DB),
                                        tg[:, SEQ:T].rearrange("p (b t) -> p b t", b=DB), ALU.mult), S["glu_used"])
                for h in range(1 if final else 2):
                    split_lo(dve, i * 2 + (2 + h), h)
                before = {}
                for j in range(PE_TAPS, CW):
                    for part in range(2):
                        for h in range(2):
                            c = i * 2 + h
                            w = WDW[:, ds(c, 1), j:j + 1].rearrange("p o n -> p (o n)")
                            if part == 0:
                                out, x = y[h][:, 0:SEQ], xin[h][:, j:j + SEQ]
                            else:
                                out = y[h][:, SEQ:T].rearrange("p (b t) -> p t b", b=DB)
                                x = xin[h][:, XP + j * DB:XP + j * DB + NS].rearrange("p (t b) -> p t b", b=DB)
                            if j == PE_TAPS:
                                ins = dve.tensor_scalar(out, x, w, VEC[:, ds(c + V_BDW, 1)], ALU.mult, ALU.add)
                            else:
                                L.need(before[part, h])
                                ins = dve.scalar_tensor_tensor(out, x, w, out, ALU.mult, ALU.add)
                            L(ins, wait=False)
                            before[part, h] = L.last()
                for h in range(2):
                    dve.wait_ge(S["tap_full"], i * 2 + (h + 1))
                    for part in range(2):
                        L.need(before[part, h])
                        out, b = (y[h][:, 0:SEQ], PS[:, 4 + 2 * h, :]) if part == 0 else (y[h][:, SEQ:T], PS[:, 5 + 2 * h, 0:NS])
                        L(dve.tensor_tensor(out, out, b, ALU.add), S["tap_used"] if part else None, wait=False)
                dve.drain().then_inc(S["conv_done"], 2)
            with dve.Fori(0, 3) as i:
                L.loop(i, dve_chain=2 + 4 * (CW - PE_TAPS) + 2, glu_used=2, tap_used=2)
                conv_pair(i, False)
            L.end(3)
            conv_pair(3, True)
            end_phase(dve, 2)
            dve.wait_ge(S["stat_ready"], 1)
            L(dve.tensor_scalar(two(TMP[3][:, :]), STAT, 1.0 / D, None, ALU.mult), S["stat_used"])
            for c in range(NC):
                L(dve.tensor_tensor(F[:, c, :], F[:, c, :], TMP[3][:, :], ALU.subtract), S["mean_ready"], wait=False)
            rstd_dve(dve, L, 0, 0)
            for c in range(NC + 1):
                if 2 <= c < NC:
                    dve.wait_ge(x_ready, NC + c - 1)
                if c < NC:
                    L(dve.tensor_tensor(TMP[c % 2][:, :], F[:, c, :], RS[:, :], ALU.mult), S["silu_ready"], wait=False)
                if c:
                    dve.wait_ge(S["xh_ready"], NC + c)
                    L(dve.tensor_tensor(XL[:, c - 1, :], TMP[(c - 1) % 2][:, :], XH[:, c - 1, :].bitcast(F32),
                                        ALU.subtract), x_ready, wait=False)
            with dve.Fori(0, 2) as i:
                for h in range(2):
                    dve_split_ahead(dve, i, S_CONVO, h)
            end_phase(dve, 3)
            rstd_dve(dve, L, 1, 1)
            residual_dve(dve, L, V_MPOST, V_FPRE, 0, 2)
            ffn_dve(dve, L, 0, S_FFN0, B_FFN0, 2, 1, V_FPOST, 2, 2, False)
            end_phase(dve, 4)
            nsa_dve(dve, L)

        @block.gpsimd
        def _(pool):
            L = Link(pool, chain["pool"])
            L(pool.memset(XIN[:, :, 0:CW - 1], 0.0))
            pool.drain().then_inc(blk_free, 2)
            end_phase(pool, 1)
            end_phase(pool, 2)
            end_phase(pool, 3)
            load_p(pool, 0)
            conv_states(pool)
            residual_pool(pool, L, 0)
            end_phase(pool, 4)
            nsa_pool(pool, L)


_INS = ["x_prompt", "x_sample", "state_conv", "cache_k_cmp", "cache_v_cmp", "cache_k_sel", "cache_v_sel",
        "state_k_win", "state_v_win", "page_table", "p_prompt", "p_sample",
        "norm_mix_pre", "norm_mix_post", "norm_ffn_pre", "norm_ffn_post",
        "conv_w_in", "conv_b_in", "conv_w_dw", "conv_b_dw", "conv_ln_g", "conv_ln_b", "conv_w_out", "conv_b_out",
        "nsa_w_in", "nsa_b_gate", "nsa_pe_k", "nsa_pe_v", "nsa_wk_c1", "nsa_wk_c2", "nsa_wv_c1", "nsa_wv_c2",
        "nsa_w_o", "ffn_w_in", "ffn_w_out", "ple_w_gate", "ple_w_proj"]
_OUTS = [("y_prompt", (1, 512, 1024)), ("y_sample", (8, 4, 1024)), ("conv_state_p", (1, 1, 30, 1024)),
         ("k_cmp_p", (1, 1, 512, 4, 64)), ("v_cmp_p", (1, 1, 512, 4, 64)), ("k_sel_p", (1, 1, 512, 4, 64)),
         ("v_sel_p", (1, 1, 512, 4, 64)), ("k_win_p", (1, 1, 512, 4, 64)), ("v_win_p", (1, 1, 512, 4, 64)),
         ("conv_state_s", (1, 8, 30, 1024)), ("k_cmp_s", (1, 8, 4, 4, 64)), ("v_cmp_s", (1, 8, 4, 4, 64)),
         ("k_sel_s", (1, 8, 4, 4, 64)), ("v_sel_s", (1, 8, 4, 4, 64)), ("k_win_s", (1, 8, 260, 4, 64)),
         ("v_win_s", (1, 8, 260, 4, 64))]


def _consts():
    import numpy as np

    c = np.zeros((P, C_ALL), np.float32)
    r = np.arange(P)
    c[:, C_ID:C_ID + P] = np.eye(P)
    for m in range(P):
        d = m % HD
        if d < 32:
            c[m + 32, C_ROT + m] = -1.0
        else:
            c[m - 32, C_ROT + m] = 1.0
    pos = np.concatenate([np.arange(SEQ), np.tile(PAST + np.arange(DT), DB)]).astype(np.float32)
    inv = np.float32(10000.0) ** (-np.arange(32, dtype=np.float32) / np.float32(32))
    ang = pos[:, None] * inv[None, :].astype(np.float32)
    cos, sin = np.cos(ang), np.sin(ang)
    c[:, C_COS:C_COS + T] = cos[:, r % 32].T
    c[:, C_SIN:C_SIN + T] = sin[:, r % 32].T
    for t in range(NTT):
        n = P if t < QT else NS
        c[:n, C_TC + t * 32:C_TC + t * 32 + 32] = cos[t * P:t * P + n]
        c[:n, C_TS + t * 32:C_TS + t * 32 + 32] = sin[t * P:t * P + n]
    bb, gp, g2, hh, tt = r // 64, r // 32 % 2, r // 16 % 2, r // 4 % 4, r % 4
    head = (gp * 2 + g2) * GQ + hh
    for b in range(3):
        c[r, C_HM + head * 3 + b] = 1.0
    for t in range(4):
        col = np.arange(32)
        ok = (col[None, :] // 4 == 2 * t + bb[:, None]) & (col[None, :] % 4 <= tt[:, None])
        c[:, C_NM + t * 32:C_NM + t * 32 + 32] = np.where(ok, 0.0, NEG)
        c[(2 * t + bb) * 4 + tt, C_SEL + t * P + r] = 1.0
    col = np.arange(32)
    c[:, C_CMS:C_CMS + 32] = np.where((col[None, :] // 16 == bb[:, None]) & (col[None, :] % 16 < 15), 0.0, NEG)
    c[:, C_CAU:C_CAU + P] = np.where(r[None, :] <= r[:, None], 0.0, NEG)
    for t in range(QT):
        c[:, C_CMP + t * 32:C_CMP + t * 32 + 32] = np.where(16 * col[None, :] + 31 <= t * P + r[:, None], 0.0, NEG)
    c[:, C_ONE:C_ONE + P] = 1.0
    return c


def kernel(**inputs):
    import numpy as np
    import concourse.bacc as bacc
    from concourse.bass_utils import run_bass_kernel_spmd

    nc = bacc.Bacc("TRN2", target_bir_lowering=False, num_devices=1)
    arrays, args, outs = {}, {}, {}
    for name in _INS:
        v = np.ascontiguousarray(inputs[name])
        arrays["in_" + name] = v
        args[name] = nc.dram_tensor("in_" + name, v.shape, mybir.dt.from_np(v.dtype), kind="ExternalInput").ap()
    arrays["in_consts"] = _consts()
    args["consts"] = nc.dram_tensor("in_consts", (P, C_ALL), F32, kind="ExternalInput").ap()
    for name, shape in _OUTS:
        outs[name] = nc.dram_tensor("out_" + name, shape, F32, kind="ExternalOutput").ap()
    trunk(nc, args, outs)
    r = run_bass_kernel_spmd(nc, [arrays], core_ids=[0])
    return tuple(r.results[0]["out_" + name] for name, _ in _OUTS)
```
